# Optimizing a Trainium2 kernel written in Bass

```python
import math
import jax, jax.numpy as jnp
from jax import lax
import numpy as np
import jax
import jax.numpy as jnp

D_MODEL = 1024
BATCH = 1
SEQ = 256
DEPTH = 1

D_MIX = D_MODEL
CONV_WIDTH = D_MIX // 2
CONV_GROUPS = 8
CONV_K = 3
DN_WIDTH = D_MIX - CONV_WIDTH
DN_HEADS = 4
DN_HEAD_DIM = DN_WIDTH // DN_HEADS
DN_CONV_K = 4
DN_CHUNK = 64
IN_COLS = 3 * CONV_WIDTH + 4 * DN_WIDTH + 2 * DN_HEADS
MEM_LEN = 256
X_HEADS = 4
X_HEAD_DIM = D_MODEL // X_HEADS
PEER_HEADS = 8
PEER_KEYS = 128
PEER_EXPERTS = PEER_KEYS * PEER_KEYS
PEER_TOPK = 16
PEER_QDIM = 128
PEER_HALF = PEER_QDIM // 2
PEER_BLOCK = 128
EPS = 1e-6


def rms_norm(x, gain, eps=EPS):
    xf = x.astype(jnp.float32)
    y = xf * lax.rsqrt(jnp.mean(xf * xf, axis=-1, keepdims=True) + eps)
    return (y * gain.astype(jnp.float32)).astype(x.dtype)

def l2_normalize(t, eps=EPS):
    tf = t.astype(jnp.float32)
    return tf * lax.rsqrt(jnp.sum(tf * tf, axis=-1, keepdims=True) + eps)

def causal_depthwise_conv(x, w):
    k = w.shape[0]
    return lax.conv_general_dilated(
        x, w[:, None, :].astype(x.dtype), window_strides=(1,), padding=[(k - 1, 0)],
        dimension_numbers=("NWC", "WIO", "NWC"), feature_group_count=x.shape[-1])

def chunk_gated_delta_rule(q, k, v, g, beta):
    f32 = jnp.float32
    bsz, seq, nh, dk = q.shape
    dv = v.shape[-1]
    nc = seq // DN_CHUNK

    def to_chunks(t):
        t = t.astype(f32).reshape(bsz, nc, DN_CHUNK, nh, *t.shape[3:])
        return jnp.moveaxis(t, 3, 1)

    q = to_chunks(q) * (dk ** -0.5)
    k = to_chunks(k)
    v = to_chunks(v)
    beta = to_chunks(beta)
    g = jnp.cumsum(to_chunks(g), axis=-1)

    causal = jnp.tril(jnp.ones((DN_CHUNK, DN_CHUNK), dtype=bool))
    strict = jnp.tril(jnp.ones((DN_CHUNK, DN_CHUNK), dtype=bool), -1)
    diff = g[..., :, None] - g[..., None, :]
    decay = jnp.where(causal, jnp.exp(jnp.where(causal, diff, 0.0)), 0.0)

    k_beta = k * beta[..., None]
    v_beta = v * beta[..., None]
    a = jnp.where(strict, jnp.einsum("bhnid,bhnjd->bhnij", k_beta, k) * decay, 0.0)
    eye = jnp.eye(DN_CHUNK, dtype=f32)
    t_mat = lax.linalg.triangular_solve(a + eye, jnp.broadcast_to(eye, a.shape),
                                        left_side=True, lower=True, unit_diagonal=True)
    u = jnp.einsum("bhnij,bhnjd->bhnid", t_mat, v_beta)
    w = jnp.einsum("bhnij,bhnjd->bhnid", t_mat, k_beta * jnp.exp(g)[..., None])
    intra = jnp.einsum("bhnid,bhnjd->bhnij", q, k) * decay
    q_dec = q * jnp.exp(g)[..., None]
    k_dec = k * jnp.exp(g[..., -1:] - g)[..., None]
    g_last = jnp.exp(g[..., -1])

    xs = tuple(jnp.moveaxis(t, 2, 0) for t in (q_dec, k_dec, u, w, intra, g_last))

    def step(state, inp):
        q_c, k_c, u_c, w_c, a_c, gl = inp
        v_new = u_c - jnp.einsum("bhcd,bhde->bhce", w_c, state)
        o = jnp.einsum("bhcd,bhde->bhce", q_c, state) + jnp.einsum("bhij,bhje->bhie", a_c, v_new)
        state = state * gl[..., None, None] + jnp.einsum("bhcd,bhce->bhde", k_c, v_new)
        return state, o

    s0 = jnp.zeros((bsz, nh, dk, dv), f32)
    _, o = lax.scan(step, s0, xs)
    return o.transpose(1, 0, 3, 2, 4).reshape(bsz, seq, nh, dv)

def hybrid_mixer(xn, w_in, conv_w, dn_conv_w, dn_a_log, dn_dt_bias, dn_norm, w_out):
    bsz, seq, _ = xn.shape
    proj = xn @ w_in
    o1 = CONV_WIDTH
    o2 = 2 * CONV_WIDTH
    o3 = 3 * CONV_WIDTH
    o4 = o3 + 3 * DN_WIDTH
    o5 = o4 + DN_WIDTH
    o6 = o5 + DN_HEADS
    b_gate, c_gate, h_conv, qkv, z, beta_logit, a_logit = jnp.split(
        proj, [o1, o2, o3, o4, o5, o6], axis=-1)

    y_conv = b_gate * causal_depthwise_conv(c_gate * h_conv, conv_w)

    qkv = jax.nn.silu(causal_depthwise_conv(qkv, dn_conv_w))
    q, k, v = jnp.split(qkv, 3, axis=-1)
    hs = (bsz, seq, DN_HEADS, DN_HEAD_DIM)
    q = l2_normalize(q.reshape(hs))
    k = l2_normalize(k.reshape(hs))
    v = v.reshape(hs)
    beta = jax.nn.sigmoid(beta_logit.astype(jnp.float32))
    g = -jnp.exp(dn_a_log.astype(jnp.float32)) * jax.nn.softplus(
        a_logit.astype(jnp.float32) + dn_dt_bias.astype(jnp.float32))
    o = chunk_gated_delta_rule(q, k, v, g, beta)
    o = rms_norm(o, dn_norm) * jax.nn.silu(z.reshape(hs).astype(jnp.float32))
    y_dn = o.reshape(bsz, seq, DN_WIDTH).astype(xn.dtype)

    return jnp.concatenate([y_conv, y_dn], axis=-1) @ w_out

def memory_cross_attention(xn, mem_n, w_q, w_kv, w_o):
    bsz, seq, _ = xn.shape
    q = (xn @ w_q).reshape(bsz, seq, X_HEADS, X_HEAD_DIM)
    kv = (mem_n @ w_kv).reshape(bsz, mem_n.shape[1], 2, X_HEADS, X_HEAD_DIM)
    k, v = kv[:, :, 0], kv[:, :, 1]
    s = jnp.einsum("bshd,bmhd->bhsm", q, k).astype(jnp.float32) * (X_HEAD_DIM ** -0.5)
    p = jax.nn.softmax(s, axis=-1).astype(xn.dtype)
    o = jnp.einsum("bhsm,bmhd->bshd", p, v).reshape(bsz, seq, D_MODEL)
    return o @ w_o

def peer_ffn(xn, w_query, sub_keys, expert_u, expert_v):
    bsz, seq, d = xn.shape
    q = (xn @ w_query).reshape(bsz, seq, PEER_HEADS, 2, PEER_HALF)
    scores = jnp.einsum("bshpd,hpnd->bshpn", q, sub_keys).astype(jnp.float32)
    s_top, i_top = lax.top_k(scores, PEER_TOPK)
    cand = (s_top[..., 0, :, None] + s_top[..., 1, None, :]).reshape(
        bsz, seq, PEER_HEADS, PEER_TOPK * PEER_TOPK)
    cand_idx = (i_top[..., 0, :, None] * PEER_KEYS + i_top[..., 1, None, :]).reshape(
        bsz, seq, PEER_HEADS, PEER_TOPK * PEER_TOPK)
    best, pos = lax.top_k(cand, PEER_TOPK)
    idx = jnp.take_along_axis(cand_idx, pos, axis=-1)
    gates = jax.nn.softmax(best, axis=-1).astype(xn.dtype)

    n_blk = (bsz * seq) // PEER_BLOCK
    sel = PEER_HEADS * PEER_TOPK
    xb = xn.reshape(n_blk, PEER_BLOCK, d)
    ib = idx.reshape(n_blk, PEER_BLOCK, sel)
    gb = gates.reshape(n_blk, PEER_BLOCK, sel)

    def block(args):
        xt, it, gt = args
        u = expert_u[it]
        v = expert_v[it]
        act = jax.nn.gelu(jnp.einsum("td,ted->te", xt, u), approximate=False)
        return jnp.einsum("te,ted->td", gt * act, v)

    y = lax.map(block, (xb, ib, gb))
    return y.reshape(bsz, seq, d)

def first_inputs(seed: int = 0) -> dict:
    key = jax.random.key(seed)
    ks = iter(jax.random.split(key, 32))
    f32 = jnp.float32
    L = DEPTH

    def nrm(shape, scale):
        return jax.random.normal(next(ks), shape, f32) * scale

    def gain(shape):
        return 1.0 + 0.02 * jax.random.normal(next(ks), shape, f32)

    x = nrm((BATCH, SEQ, D_MODEL), 1.0)
    mem = nrm((BATCH, MEM_LEN, D_MODEL), 1.0)
    norm_mix = gain((L, D_MODEL))
    w_in = nrm((L, D_MODEL, IN_COLS), D_MODEL ** -0.5)
    conv_w = nrm((L, CONV_K, CONV_WIDTH), CONV_K ** -0.5)
    dn_conv_w = nrm((L, DN_CONV_K, 3 * DN_WIDTH), DN_CONV_K ** -0.5)
    dn_a_log = jnp.log(jax.random.uniform(next(ks), (L, DN_HEADS), f32, 1.0, 16.0))
    dt = jnp.exp(jax.random.uniform(next(ks), (L, DN_HEADS), f32,
                                    math.log(1e-3), math.log(1e-1)))
    dn_dt_bias = dt + jnp.log(-jnp.expm1(-dt))
    dn_norm = gain((L, DN_HEAD_DIM))
    w_out = nrm((L, D_MIX, D_MODEL), D_MIX ** -0.5)
    norm_x = gain((L, D_MODEL))
    norm_mem = gain((L, D_MODEL))
    w_xq = nrm((L, D_MODEL, D_MODEL), D_MODEL ** -0.5)
    w_xkv = nrm((L, D_MODEL, 2 * D_MODEL), D_MODEL ** -0.5)
    w_xo = nrm((L, D_MODEL, D_MODEL), D_MODEL ** -0.5)
    norm_ffn = gain((L, D_MODEL))
    w_pq = nrm((L, D_MODEL, PEER_HEADS * PEER_QDIM), D_MODEL ** -0.5)
    peer_keys = nrm((L, PEER_HEADS, 2, PEER_KEYS, PEER_HALF), PEER_HALF ** -0.5)
    expert_u = nrm((L, PEER_EXPERTS, D_MODEL), D_MODEL ** -0.5)
    expert_v = nrm((L, PEER_EXPERTS, D_MODEL), PEER_TOPK ** -0.5)
    norm_final = gain((D_MODEL,))
    return {"x": x, "mem": mem, "norm_mix": norm_mix, "w_in": w_in, "conv_w": conv_w,
            "dn_conv_w": dn_conv_w, "dn_a_log": dn_a_log, "dn_dt_bias": dn_dt_bias,
            "dn_norm": dn_norm, "w_out": w_out, "norm_x": norm_x, "norm_mem": norm_mem,
            "w_xq": w_xq, "w_xkv": w_xkv, "w_xo": w_xo, "norm_ffn": norm_ffn,
            "w_pq": w_pq, "peer_keys": peer_keys, "expert_u": expert_u,
            "expert_v": expert_v, "norm_final": norm_final}

def first_block(x, mem, norm_mix, w_in, conv_w, dn_conv_w, dn_a_log, dn_dt_bias, dn_norm,
              w_out, norm_x, norm_mem, w_xq, w_xkv, w_xo, norm_ffn, w_pq, peer_keys,
              expert_u, expert_v, norm_final):
    h = x
    for layer in range(DEPTH):
        h = h + hybrid_mixer(rms_norm(h, norm_mix[layer]), w_in[layer], conv_w[layer],
                             dn_conv_w[layer], dn_a_log[layer], dn_dt_bias[layer],
                             dn_norm[layer], w_out[layer])
        h = h + memory_cross_attention(rms_norm(h, norm_x[layer]),
                                       rms_norm(mem, norm_mem[layer]),
                                       w_xq[layer], w_xkv[layer], w_xo[layer])
        h = h + peer_ffn(rms_norm(h, norm_ffn[layer]), w_pq[layer], peer_keys[layer],
                         expert_u[layer], expert_v[layer])
    return rms_norm(h, norm_final)


DEPTH_2 = 2

GRID_W = 64
CTX_LEN = 256
N_MIXERS = 4
MIX_CONV = 0
MIX_POOL = 1
MIX_MLA = 2
MIX_CHUNK = 3
BRANCH = D_MODEL
CONV_WIDTH_2 = 31
POOL_WINDOWS = (2, 4, 8, 16)
POOL_GROUP = BRANCH // len(POOL_WINDOWS)
MLA_HEADS = D_MODEL // 128
MLA_NOPE = 128
MLA_ROPE = 64
MLA_V = 128
MLA_Q_RANK = 3 * D_MODEL // 8
MLA_KV_RANK = D_MODEL // 4
MLA_KVC = MLA_KV_RANK + MLA_ROPE
MLA_SCALE = (MLA_NOPE + MLA_ROPE) ** -0.5
ROPE_THETA = 10000.0
Q_BLOCK = 128
CHUNK = 128
CHUNK_GROUPS = 8
CHUNK_GC = BRANCH // CHUNK_GROUPS


def _n_layers_of(kind):
    return len(range(kind, DEPTH_2, N_MIXERS))

def _rms(x, g):
    xf = x.astype(jnp.float32)
    y = xf * lax.rsqrt(jnp.mean(xf * xf, axis=-1, keepdims=True) + EPS)
    return (y * g.astype(jnp.float32)).astype(x.dtype)

def _layernorm(x, g, b):
    xf = x.astype(jnp.float32)
    mu = jnp.mean(xf, axis=-1, keepdims=True)
    var = jnp.mean(jnp.square(xf - mu), axis=-1, keepdims=True)
    y = (xf - mu) * lax.rsqrt(var + EPS)
    return (y * g.astype(jnp.float32) + b.astype(jnp.float32)).astype(x.dtype)

def _rope_tables(rows):
    row_id = jnp.repeat(jnp.arange(rows), GRID_W).astype(jnp.float32)
    col_id = jnp.tile(jnp.arange(GRID_W), rows).astype(jnp.float32)
    axis_dim = MLA_ROPE // 2
    freqs = ROPE_THETA ** (-jnp.arange(0, axis_dim, 2, dtype=jnp.float32) / axis_dim)
    ar = row_id[:, None] * freqs
    ac = col_id[:, None] * freqs
    return (jnp.cos(ar), jnp.sin(ar), jnp.cos(ac), jnp.sin(ac))

def _rope1d(x, cos, sin):
    x1, x2 = jnp.split(x, 2, axis=-1)
    return jnp.concatenate([x1 * cos - x2 * sin, x1 * sin + x2 * cos], axis=-1)

def _rope2d(x, tabs):
    cr, sr, cc, sc = [t.astype(x.dtype) for t in tabs]
    if x.ndim == 4:
        cr, sr, cc, sc = cr[:, None], sr[:, None], cc[:, None], sc[:, None]
    xr, xc = jnp.split(x, 2, axis=-1)
    return jnp.concatenate([_rope1d(xr, cr, sr), _rope1d(xc, cc, sc)], axis=-1)

def _conv_mixer(h, w_in, dw, db, ln_g, ln_b, w_out):
    a, b, g = jnp.split(h @ w_in, 3, axis=-1)
    y = a * jax.nn.sigmoid(b)
    y = lax.conv_general_dilated(
        y, dw[:, None, :].astype(y.dtype), window_strides=(1,),
        padding=[(CONV_WIDTH_2 // 2, CONV_WIDTH_2 // 2)],
        dimension_numbers=('NWC', 'WIO', 'NWC'),
        feature_group_count=BRANCH) + db
    y = jax.nn.silu(_layernorm(y, ln_g, ln_b)) * jax.nn.silu(g)
    return y @ w_out

def _window_mean(v, w):
    L = v.shape[1]
    cs = jnp.pad(jnp.cumsum(v.astype(jnp.float32), axis=1), ((0, 0), (1, 0), (0, 0)))
    t = jnp.arange(L)
    start = jnp.clip(t - w // 2, 0, L)
    end = jnp.clip(t + (w - w // 2), 0, L)
    total = jnp.take(cs, end, axis=1) - jnp.take(cs, start, axis=1)
    cnt = (end - start).astype(jnp.float32)
    return (total / cnt[None, :, None]).astype(v.dtype)

def _pool_mixer(h, w_in, w_grp, scale, w_out):
    v, g = jnp.split(h @ w_in, 2, axis=-1)
    B, L, _ = v.shape
    vg = v.reshape(B, L, len(POOL_WINDOWS), POOL_GROUP)
    pooled = jnp.stack([_window_mean(vg[:, :, k], w) for k, w in enumerate(POOL_WINDOWS)], axis=2) - vg
    y = jnp.einsum('blgc,gcd->blgd', pooled, w_grp).reshape(B, L, BRANCH) * scale
    return (y * jax.nn.silu(g)) @ w_out

def _mla_keys(pkv, kv_norm, w_ukv, k_nope_g, k_rope_g, tabs):
    ckv, kr = jnp.split(pkv, [MLA_KV_RANK], axis=-1)
    B, L, _ = ckv.shape
    kv = (_rms(ckv, kv_norm) @ w_ukv).reshape(B, L, MLA_HEADS, MLA_NOPE + MLA_V)
    kn, v = jnp.split(kv, [MLA_NOPE], axis=-1)
    kn = _rms(kn, k_nope_g)
    kr = _rms(kr, k_rope_g)
    if tabs is not None:
        kr = _rope2d(kr, tabs)
    return kn, kr, v

def _mla_queries(cq, q_norm, w_uq, q_nope_g, q_rope_g, tabs):
    B, L, _ = cq.shape
    q = (_rms(cq, q_norm) @ w_uq).reshape(B, L, MLA_HEADS, MLA_NOPE + MLA_ROPE)
    qn, qr = jnp.split(q, [MLA_NOPE], axis=-1)
    qn = _rms(qn, q_nope_g)
    qr = _rms(qr, q_rope_g)
    if tabs is not None:
        qr = _rope2d(qr, tabs)
    return qn, qr

def _attend(qn, qr, kn, kr, v):
    s = (jnp.einsum('bqhd,bkhd->bhqk', qn, kn)
         + jnp.einsum('bqhr,bkr->bhqk', qr, kr)).astype(jnp.float32) * MLA_SCALE
    p = jax.nn.softmax(s, axis=-1).astype(v.dtype)
    return jnp.einsum('bhqk,bkhd->bqhd', p, v)

def _attend_blocks(qn, qr, kn, kr, v):
    B, L, H, _ = qn.shape
    nb = L // Q_BLOCK

    def blk(t):
        return jnp.moveaxis(t.reshape((B, nb, Q_BLOCK) + t.shape[2:]), 1, 0)

    out = lax.map(lambda q: _attend(q[0], q[1], kn, kr, v), (blk(qn), blk(qr)))
    return jnp.moveaxis(out, 0, 1).reshape(B, L, H * MLA_V)

def _mla_mixer(h, hc, with_ctx_out, tabs, w_in, q_norm, kv_norm, w_uq, w_ukv, nope_g, rope_g, w_out):
    pkv, cq, g = jnp.split(h @ w_in, [MLA_KVC, MLA_KVC + MLA_Q_RANK], axis=-1)
    kn, kr, v = _mla_keys(pkv, kv_norm, w_ukv, nope_g[1], rope_g[1], tabs)
    qn, qr = _mla_queries(cq, q_norm, w_uq, nope_g[0], rope_g[0], tabs)
    pc = hc @ (w_in if with_ctx_out else w_in[:, :MLA_KVC])
    knc, krc, vc = _mla_keys(pc[..., :MLA_KVC], kv_norm, w_ukv, nope_g[1], rope_g[1], None)
    o = _attend_blocks(qn, qr,
                       jnp.concatenate([kn, knc], axis=1),
                       jnp.concatenate([kr, krc], axis=1),
                       jnp.concatenate([v, vc], axis=1))
    out = (o * jax.nn.silu(g)) @ w_out
    out_c = None
    if with_ctx_out:
        cqc, gc = jnp.split(pc[..., MLA_KVC:], [MLA_Q_RANK], axis=-1)
        qnc, qrc = _mla_queries(cqc, q_norm, w_uq, nope_g[0], rope_g[0], None)
        Bc, Lc = hc.shape[0], hc.shape[1]
        oc = _attend(qnc, qrc, knc, krc, vc).reshape(Bc, Lc, MLA_HEADS * MLA_V)
        out_c = (oc * jax.nn.silu(gc)) @ w_out
    return out, out_c

def _chunk_mixer(h, w_in, ln_g, ln_b, w_s, b_s, w_out):
    u, v, g = jnp.split(h @ w_in, 3, axis=-1)
    B, L, _ = v.shape
    v = _layernorm(v, ln_g, ln_b).reshape(B, L // CHUNK, CHUNK, CHUNK_GROUPS, CHUNK_GC)
    s = jnp.einsum('gpq,bnqgc->bnpgc', w_s, v) + b_s[:, :, None]
    y = u * s.reshape(B, L, BRANCH) * jax.nn.silu(g)
    return y @ w_out

def second_inputs(seed: int = 0) -> dict:
    key = jax.random.key(seed)
    ks = iter(jax.random.split(key, 40))

    def nrm(shape, s):
        return jax.random.normal(next(ks), shape, jnp.float32) * s

    nA, nB, nC, nD = (_n_layers_of(k) for k in range(N_MIXERS))
    D, E = D_MODEL, BRANCH
    HQK = MLA_HEADS * (MLA_NOPE + MLA_ROPE)
    HKV = MLA_HEADS * (MLA_NOPE + MLA_V)
    HV = MLA_HEADS * MLA_V
    return {
        'x': nrm((BATCH, SEQ, D), 1.0),
        'c': nrm((BATCH, D), 1.0),
        'ctx': nrm((BATCH, CTX_LEN, D), 1.0),
        'c_ctx': nrm((D,), 1.0),
        'norm_g': 1.0 + nrm((DEPTH_2, D), 0.05),
        'w_mod': nrm((DEPTH_2, D, 3 * D), 0.5 * D ** -0.5),
        'b_mod': nrm((DEPTH_2, 3 * D), 0.01),
        'cv_w_in': nrm((nA, D, 3 * E), D ** -0.5),
        'cv_dw': nrm((nA, CONV_WIDTH_2, E), CONV_WIDTH_2 ** -0.5),
        'cv_db': nrm((nA, E), 0.01),
        'cv_ln_g': 1.0 + nrm((nA, E), 0.05),
        'cv_ln_b': nrm((nA, E), 0.01),
        'cv_w_out': nrm((nA, E, D), E ** -0.5),
        'pl_w_in': nrm((nB, D, 2 * E), D ** -0.5),
        'pl_w_grp': nrm((nB, len(POOL_WINDOWS), POOL_GROUP, POOL_GROUP), POOL_GROUP ** -0.5),
        'pl_scale': 1.0 + nrm((nB, E), 0.05),
        'pl_w_out': nrm((nB, E, D), E ** -0.5),
        'ml_w_in': nrm((nC, D, MLA_KVC + MLA_Q_RANK + HV), D ** -0.5),
        'ml_q_norm': 1.0 + nrm((nC, MLA_Q_RANK), 0.05),
        'ml_kv_norm': 1.0 + nrm((nC, MLA_KV_RANK), 0.05),
        'ml_w_uq': nrm((nC, MLA_Q_RANK, HQK), MLA_Q_RANK ** -0.5),
        'ml_w_ukv': nrm((nC, MLA_KV_RANK, HKV), MLA_KV_RANK ** -0.5),
        'ml_nope_norm': 1.0 + nrm((nC, 2, MLA_NOPE), 0.05),
        'ml_rope_norm': 1.0 + nrm((nC, 2, MLA_ROPE), 0.05),
        'ml_w_out': nrm((nC, HV, D), HV ** -0.5),
        'ch_w_in': nrm((nD, D, 3 * E), D ** -0.5),
        'ch_ln_g': 1.0 + nrm((nD, E), 0.05),
        'ch_ln_b': nrm((nD, E), 0.01),
        'ch_w_s': nrm((nD, CHUNK_GROUPS, CHUNK, CHUNK), CHUNK ** -0.5),
        'ch_b_s': 1.0 + nrm((nD, CHUNK, CHUNK_GROUPS), 0.05),
        'ch_w_out': nrm((nD, E, D), E ** -0.5),
    }

def second_block(x, c, ctx, c_ctx, norm_g, w_mod, b_mod,
              cv_w_in, cv_dw, cv_db, cv_ln_g, cv_ln_b, cv_w_out,
              pl_w_in, pl_w_grp, pl_scale, pl_w_out,
              ml_w_in, ml_q_norm, ml_kv_norm, ml_w_uq, ml_w_ukv, ml_nope_norm, ml_rope_norm, ml_w_out,
              ch_w_in, ch_ln_g, ch_ln_b, ch_w_s, ch_b_s, ch_w_out):
    L = x.shape[1]
    ROWS = L // GRID_W
    tabs = _rope_tables(ROWS)
    s_lat = jax.nn.silu(c)
    s_ctx = jax.nn.silu(c_ctx)
    cx = ctx
    for i in range(DEPTH_2):
        kind, j = i % N_MIXERS, i // N_MIXERS
        ctx_out = any(k % N_MIXERS == MIX_MLA for k in range(i + 1, DEPTH_2))
        ctx_in = ctx_out or kind == MIX_MLA
        sh, sc, gt = jnp.split((s_lat @ w_mod[i] + b_mod[i])[:, None, :], 3, axis=-1)
        h = _rms(x, norm_g[i]) * (1.0 + sc) + sh
        if ctx_in:
            shc, scc, gtc = jnp.split(s_ctx @ w_mod[i] + b_mod[i], 3, axis=-1)
            hc = _rms(cx, norm_g[i]) * (1.0 + scc) + shc
        if kind == MIX_CONV:
            args = (cv_w_in[j], cv_dw[j], cv_db[j], cv_ln_g[j], cv_ln_b[j], cv_w_out[j])
            o = _conv_mixer(h, *args)
            oc = _conv_mixer(hc, *args) if ctx_out else None
        elif kind == MIX_POOL:
            args = (pl_w_in[j], pl_w_grp[j], pl_scale[j], pl_w_out[j])
            o = _pool_mixer(h, *args)
            oc = _pool_mixer(hc, *args) if ctx_out else None
        elif kind == MIX_MLA:
            o, oc = _mla_mixer(h, hc, ctx_out, tabs, ml_w_in[j], ml_q_norm[j], ml_kv_norm[j],
                               ml_w_uq[j], ml_w_ukv[j], ml_nope_norm[j], ml_rope_norm[j], ml_w_out[j])
        else:
            args = (ch_w_in[j], ch_ln_g[j], ch_ln_b[j], ch_w_s[j], ch_b_s[j], ch_w_out[j])
            o = _chunk_mixer(h, *args)
            oc = _chunk_mixer(hc, *args) if ctx_out else None
        x = x + gt * o
        if ctx_out:
            cx = cx + gtc * oc
    return x


def setup_inputs(seed=0):
    out = dict(first_inputs(seed))
    for name, value in second_inputs(seed + 1).items():
        if name != "x":
            out[name + "_2"] = value
    return out


def reference(
    x, mem, norm_mix, w_in, conv_w, dn_conv_w, dn_a_log, dn_dt_bias, dn_norm, w_out, norm_x,
    norm_mem, w_xq, w_xkv, w_xo, norm_ffn, w_pq, peer_keys, expert_u, expert_v, norm_final, c_2,
    ctx_2, c_ctx_2, norm_g_2, w_mod_2, b_mod_2, cv_w_in_2, cv_dw_2, cv_db_2, cv_ln_g_2,
    cv_ln_b_2, cv_w_out_2, pl_w_in_2, pl_w_grp_2, pl_scale_2, pl_w_out_2, ml_w_in_2,
    ml_q_norm_2, ml_kv_norm_2, ml_w_uq_2, ml_w_ukv_2, ml_nope_norm_2, ml_rope_norm_2,
    ml_w_out_2, ch_w_in_2, ch_ln_g_2, ch_ln_b_2, ch_w_s_2, ch_b_s_2, ch_w_out_2,
):
    x = first_block(
        x, mem, norm_mix, w_in, conv_w, dn_conv_w, dn_a_log, dn_dt_bias, dn_norm, w_out, norm_x,
        norm_mem, w_xq, w_xkv, w_xo, norm_ffn, w_pq, peer_keys, expert_u, expert_v, norm_final,
    )
    return second_block(
        x, c_2, ctx_2, c_ctx_2, norm_g_2, w_mod_2, b_mod_2, cv_w_in_2, cv_dw_2, cv_db_2,
        cv_ln_g_2, cv_ln_b_2, cv_w_out_2, pl_w_in_2, pl_w_grp_2, pl_scale_2, pl_w_out_2,
        ml_w_in_2, ml_q_norm_2, ml_kv_norm_2, ml_w_uq_2, ml_w_ukv_2, ml_nope_norm_2,
        ml_rope_norm_2, ml_w_out_2, ch_w_in_2, ch_ln_g_2, ch_ln_b_2, ch_w_s_2, ch_b_s_2,
        ch_w_out_2,
    )


_drawn_inputs = setup_inputs


def setup_inputs(seed=0):
    import zlib

    import numpy as np

    out = dict(_drawn_inputs(seed))
    spreads = {}
    factors = {'dn_norm': 5.277,
     'norm_x': 8.0,
     'norm_mem': 8.0,
     'norm_ffn': 15.006,
     'norm_final': 2.884,
     'norm_g_2': 3.661,
     'b_mod_2': 6.945,
     'cv_db_2': 8.0,
     'cv_ln_g_2': 7.356,
     'cv_ln_b_2': 33.805,
     'pl_scale_2': 6.447}
    for name, (base, spread) in spreads.items():
        noise = np.random.default_rng([zlib.crc32(name.encode()), seed]).standard_normal(out[name].shape)
        drawn = base * np.exp(spread * noise) if base else spread * noise
        out[name] = jnp.asarray(drawn.astype(out[name].dtype))
    for name, factor in factors.items():
        out[name] = (out[name] * factor).astype(out[name].dtype)
    return out
```

```python
from contextlib import ExitStack

import concourse.bass as bass
from concourse import mybir

F32 = mybir.dt.float32
U32 = mybir.dt.uint32
ALU = mybir.AluOpType
ACT = mybir.ActivationFunctionType
AX_X = mybir.AxisListType.X

P = 128
D = 1024
S = 256
KB = D // P
TT = S // P
CHUNK = 64
NH = 4
PH, TOPK, KEYS = 8, 16, 128
TAPS, DN_TAPS, CV_TAPS = 3, 4, 31
EPS = 1e-6
LOWEST = -3.0e38

COLS = {}
_n = 0
for _name, _w in (("norm_mix", 8), ("norm_x", 8), ("norm_mem", 8), ("norm_ffn", 8), ("norm_final", 8),
                  ("norm_g0", 8), ("norm_g1", 8), ("conv_w", TAPS * 4), ("dn_conv_w", DN_TAPS * 12),
                  ("dn_norm", 1), ("cv_dw", CV_TAPS * 8), ("cv_db", 8), ("ln_g", 8), ("ln_b", 8),
                  ("pl_scale", 8), ("b_mod", 48), ("c", 8), ("a_log", 4), ("dt_bias", 4)):
    COLS[_name] = (_n, _w)
    _n += _w
NCOLS = _n

CONST = {}
_n = 0
for _name, _w in (("ident", P), ("ones", P), ("upto", P), ("whole", P), ("causal", P), ("strict16", P),
                  ("off32", P), ("off64", P), ("count_inv", 4 * S), ("iota16", 16), ("eps", 1), ("one", 1)):
    CONST[_name] = (_n, _w)
    _n += _w
NCONST = _n

UNITS = (["q", "k", "v", "b", "c", "h", "z"] + ["mem_k0", "mem_k1", "mem_v0", "mem_v1"]
         + ["mix_out0", "mix_out1", "xq0", "xq1", "xo0", "xo1", "pq0", "pq1"]
         + [f"cv_ab{i}" for i in range(4)] + ["cv_g0", "cv_g1", "cv_out0", "cv_out1"]
         + ["pl_v0", "pl_v1", "pl_g0", "pl_g1", "grp", "pl_out0", "pl_out1"])
PAIRS = {u: (4 if u == "grp" else 2) for u in UNITS}
FIRST_PAIR = {}
_n = 0
for _u in UNITS:
    FIRST_PAIR[_u] = _n
    _n += PAIRS[_u]
W_SLOTS = 3
PAIR_BANKS = 4

MOD_CHUNKS = 24
MOD_AFTER = {}
_n = 0
for _i, _u in enumerate(UNITS[1:18]):
    _w = 1 if _i < 10 else 2
    MOD_AFTER[_u] = (_n, min(_n + _w, MOD_CHUNKS))
    _n += _w

TILE_BANKS = 3
TILES = (["ss_x", "ss_mem", "logits", "ss_q0", "ss_q1", "ss_k0", "ss_k1", "gcum", "gB0", "gB1"]
         + [f"{n}{t}" for n in ("ktok", "vtok", "KK", "QK") for t in range(TT)]
         + [f"{n}{t}" for n in ("NT",) for t in range(TT)]
         + [f"{n}{t}" for r in ("2", "4") for g in (("P" + r, "PT" + r), ("T" + r, "TT" + r))
            for t in range(TT) for n in (g[0] + "_", g[1] + "_")]
         + [f"P8_{t}" for t in range(TT)]
         + [f"{n}{t}" for t in range(TT) for n in ("T8_", "TT8_")]
         + [f"Y32_{t}" for t in range(TT)]
         + [f"{n}{t}" for t in range(TT) for n in ("T32_", "TT32_")]
         + [f"Y64_{t}" for t in range(TT)] + [f"TT64_{t}" for t in range(TT)]
         + [f"{n}{t}" for n in ("intraT", "u", "wT") for t in range(TT)]
         + [n + str(c) for c in range(4) for n in ((["wS"] if c else []) + ["o", "dS"])]
         + ["ss_o0", "ss_o1", "ss_h1"] + [f"att_s{h}" for h in range(NH)]
         + [f"att_p{h}" for h in range(NH)] + [f"att_o{h}" for h in range(NH)]
         + ["ss_h2"] + [f"sc{t}_{i}" for t in range(TT) for i in range(4)]
         + ["ss_h3", "ss_m0", "mean", "var", "ss_m1"])
TILE_NO = {n: i for i, n in enumerate(TILES)}

RING = 8
HEADS = TT * PH
AHEAD = 2
HEAD_LOOPS = [[(0, PH)]] * (TT - 1) + [[(0, PH - AHEAD), (PH - AHEAD, PH)]]
ROUTE_POSTS = 26


def build(nc, x_t, mem_t, cols_d, const_d, small_d, keys_d, units_d, grp_d, mod_d, uv_d, out_d, dbg=None):
    with ExitStack() as ctx:
        def sb(name, shape, dt=F32):
            return ctx.enter_context(nc.sbuf_tensor(name, shape, dt))

        sems = {}

        def sem(name):
            if name not in sems:
                sems[name] = ctx.enter_context(nc.semaphore(name))
            return sems[name]

        hA = sb("hA", [P, KB, S])
        hB = sb("hB", [P, KB, S])
        xn = sb("xn", [P, KB, S])
        sq = sb("sq", [P, KB, S])
        wring = sb("wring", [P, W_SLOTS, KB, 512])
        cols = sb("cols", [P, NCOLS])
        const = sb("const", [P, NCONST])
        small_w = sb("small_w", [P, KB, 8])
        modc = sb("modc", [P, 48])
        gmod = sb("gmod", [P, 2, KB])
        silu_c = sb("silu_c", [P, KB])
        rms = sb("rms", [P, 1, S])
        rinv = sb("rinv", [P, 1, S])
        gl = sb("gl", [P, 4, NH])
        tiny = sb("tiny", [P, 16, TT, NH])
        arena = sb("arena", [P, 28 * 1024])
        ps = ctx.enter_context(nc.psum_tensor("ps", [P, 8, 512], F32))

        def col(name, i=0, n=1):
            return cols[:, COLS[name][0] + i:COLS[name][0] + i + n]

        def cst(name):
            return const[:, CONST[name][0]:CONST[name][0] + CONST[name][1]]

        ident, ones = cst("ident"), cst("ones")

        def slab(i, width=1024):
            return arena[:, i * 1024:i * 1024 + width]

        def blocks(ap, b):
            return ap.rearrange("p (b t) -> p b t", b=b)

        def heads(ap):
            return ap.rearrange("p (t h j) -> p t h j", t=TT, h=NH)

        mod_w = slab(0, 4096).rearrange("p (s k n) -> p s k n", s=2, k=KB)
        mem_kT = blocks(slab(4, 2048), KB)
        mem_v = slab(6, 2048).rearrange("p (m n) -> p m n", m=TT)
        qkv = blocks(slab(8, 3072), 12)
        zT = blocks(slab(11), 4)
        yT = blocks(slab(12, 2048), KB)
        S_st = slab(14, 512).rearrange("p (h e) -> p h e", h=NH)
        kbe, kdec, vbeta, qdec = (heads(slab(15 + i)) for i in range(4))
        E, N_, NT, T_, T_T, off32, off64, intra, Y = (heads(slab(19 + i)) for i in range(9))
        intraT, u_tok, wT, v_new, oT = E, N_, NT, T_, blocks(slab(26), 4)
        qkv_pad = slab(19, 12 * 259).rearrange("p (b t) -> p b t", b=12)
        bT, cT = blocks(slab(23), 4), blocks(slab(24), 4)
        hc_pad = slab(25, 4 * 258).rearrange("p (b t) -> p b t", b=4)
        norm2 = slab(15, 2048)
        egB = heads(slab(27))
        aq = blocks(slab(8, 2048), KB)
        prob = slab(10, 2048).rearrange("p (h t m) -> p h t m", h=NH, t=TT)
        probT = slab(12, 2048).rearrange("p (h m t) -> p h m t", h=NH, m=TT)
        ao = blocks(slab(14, 2048), KB)
        keys = slab(27).rearrange("p (h n) -> p h n", h=PH)
        pq = blocks(slab(16, 2048), KB)
        ring = [slab(2 * i, 2048) for i in range(RING)]
        score = [slab(18 + 2 * t, 2048) for t in range(TT)]
        all_scores = slab(18, 4096)
        ysb = [slab(16), slab(17)]
        diag = slab(26, 2048).rearrange("p (j t) -> p j t", j=TOPK)
        spare = sq[:].rearrange("p k t -> p (k t)")
        halves = spare[:, 0:256].rearrange("p (s n) -> p s n", s=2)
        cand = spare[:, 256:512]
        scr = spare[:, 512:768]
        hot = spare[:, 768:1280].rearrange("p (s j a) -> p s j a", s=2, j=TOPK)

        def small(i, dt=None):
            ap = spare[:, 1280 + 32 * i:1312 + 32 * i]
            return (ap.bitcast(dt) if dt else ap).rearrange("p (s k) -> p s k", s=2)

        topv, topi, topf, pab, pabf, picked = small(0), small(1, U32), small(2), small(3, U32), small(4), small(5)
        best, posn, gate_now = small(6)[:, 0], small(7, U32)[:, 0], small(8)[:, 0]
        gexp, gsum = small(9)[:, 0], small(10)[:, 0, 0:1]
        idx = sb("idx", [P, HEADS * TOPK], U32)
        gate = sb("gate", [P, HEADS * TOPK])
        idx_now = sb("idx_now", [P, 2, RING], U32)
        act16 = sb("act16", [P, TOPK])
        gel16 = sb("gel16", [P, TOPK])
        ypad = slab(0, 8 * 286).rearrange("p (b t) -> p b t", b=KB)
        sgb = blocks(slab(3, 512), 2)
        yc = blocks(slab(4, 2048), KB)
        gT = blocks(slab(6, 2048), KB)
        ycn = blocks(slab(8, 2048), KB)
        vpad = slab(10, 8 * 272).rearrange("p (b t) -> p b t", b=KB)
        win = [slab(13 + i, 544).rearrange("p (b t) -> p b t", b=2) for i in range(4)]
        pooled = blocks(slab(17, 2048), KB)

        counts = {}

        def post(ins, name):
            counts[name] = counts.get(name, 0) + 1
            ins.then_inc(sem(name), 1)
            return counts[name]

        def signal(eng, name, n=1):
            counts[name] = counts.get(name, 0) + n
            eng.sem_inc(sem(name), n)

        def did(eng, ins, name):
            n = post(ins, name)
            eng.wait_ge(sem(name), n)
            return n

        def need(eng, name, n=1):
            eng.wait_ge(sem(name), n)

        def tile_bank(name):
            return 4 + TILE_NO[name] % TILE_BANKS

        def tile_ps(name):
            return ps[:, tile_bank(name), :]

        def tile_ready(eng, name):
            eng.wait_ge(sem("tiles"), TILE_NO[name] + 1)

        def tile_used(ins, name):
            ins.then_inc(sem(f"tile_free{tile_bank(name)}"), 1)

        def tile_used_wait(eng, ins, name):
            tile_used(ins, name)
            eng.wait_ge(sem(f"tile_free{tile_bank(name)}"), TILE_NO[name] // TILE_BANKS + 1)

        def pair_ps(p):
            return ps[:, p % PAIR_BANKS, :]

        def pair_ready(eng, p):
            eng.wait_ge(sem("pairs"), p + 1)

        def pair_used(ins, p):
            ins.then_inc(sem(f"pair_free{p % PAIR_BANKS}"), 1)

        def pair_used_wait(eng, ins, p):
            pair_used(ins, p)
            eng.wait_ge(sem(f"pair_free{p % PAIR_BANKS}"), p // PAIR_BANKS + 1)

        block = ctx.enter_context(nc.Block())

        @block.sync
        def _(sp):
            for n, u in enumerate(UNITS):
                slot = n % W_SLOTS
                if n >= W_SLOTS:
                    before = UNITS[n - W_SLOTS]
                    sp.wait_ge(sem("pairs"), FIRST_PAIR[before] + PAIRS[before])
                if u == "grp":
                    sp.dma_start(wring[:, slot, 0:4, :].rearrange("p k n -> p (k n)"), grp_d).then_inc(sem(f"w_in{slot}"), 16)
                else:
                    sp.dma_start(wring[:, slot].rearrange("p k n -> p (k n)"),
                                 units_d[n if n < UNITS.index("grp") else n - 1]).then_inc(sem(f"w_in{slot}"), 16)
            need(sp, "result", KB)
            sp.dma_start(out_d, hB[:]).then_inc(sem("stored"), 16)
            sp.wait_ge(sem("stored"), 16)

        @block.gpsimd
        def _(pool):
            for i in range(2):
                pool.dma_start(mod_w[:, i].rearrange("p k n -> p (k n)"), mod_d[i]).then_inc(sem(f"mod_in{i}"), 16)
            need(pool, "silu_c")
            for i in range(MOD_CHUNKS):
                w = mod_w[:, i % 2]
                pool.wait_ge(sem(f"mod_in{i % 2}"), 16 * (i // 2 + 1))
                did(pool, pool.tensor_tensor(w, w, silu_c[:].unsqueeze(2).broadcast_to([P, KB, 256]), ALU.mult), "pool_step")
                did(pool, pool.tensor_tensor(w[:, 0:4], w[:, 0:4], w[:, 4:8], ALU.add), "pool_step")
                did(pool, pool.tensor_tensor(w[:, 0:2], w[:, 0:2], w[:, 2:4], ALU.add), "pool_step")
                did(pool, pool.tensor_tensor(w[:, 0], w[:, 0], w[:, 1], ALU.add), "mod_part")
                if i >= 1 and i + 1 < MOD_CHUNKS:
                    need(pool, "mod_sum", i)
                    pool.dma_start(mod_w[:, (i + 1) % 2].rearrange("p k n -> p (k n)"), mod_d[i + 1]).then_inc(sem(f"mod_in{(i + 1) % 2}"), 16)
            for b in range(RING):
                pool.sem_inc(sem(f"row_free{b}"), 1)
            with pool.Fori(0, HEADS) as h:
                pool.wait_ge(sem("routed"), h + 1)
                for half in range(TOPK // RING):
                    pool.tensor_copy(idx_now[:, half, :],
                                     idx[:, bass.ds(h * TOPK + half * RING, RING)]).then_inc(sem("idx_now"), 1)
                    for b in range(RING):
                        if b == 0:
                            pool.wait_ge(sem("idx_now"), 2 * h + half + 1)
                        pool.wait_ge(sem(f"row_free{b}"), 2 * h + half + 1)
                        pool.sem_inc(sem("row_turn"), 1)
                        pool.indirect_dma_start(
                            ring[b], None, uv_d,
                            bass.IndirectOffsetOnAxis(ap=idx_now[:, half, b:b + 1], axis=0)
                        ).then_inc(sem(f"row_in{b}"), 16)

        @block.tensor
        def _(pe):
            def tile_begin(name):
                n = TILE_NO[name]
                if n >= TILE_BANKS:
                    pe.wait_ge(sem(f"tile_free{tile_bank(name)}"), n // TILE_BANKS)
                return tile_ps(name)

            def sum_channels(name, src, nblk):
                out = tile_begin(name)
                for k in range(nblk):
                    mm = pe.matmul(out[:, 0:S], lhsT=ones, rhs=src[:, k, :], start=(k == 0), stop=(k == nblk - 1))
                post(mm, "tiles")

            def unit(u, rhs, ready=None, tokens_out=False):
                n = UNITS.index(u)
                w = wring[:, n % W_SLOTS]
                pe.wait_ge(sem(f"w_in{n % W_SLOTS}"), 16 * (n // W_SLOTS + 1))
                for i in range(2):
                    p = FIRST_PAIR[u] + i
                    if p >= PAIR_BANKS:
                        pe.wait_ge(sem(f"pair_free{p % PAIR_BANKS}"), p // PAIR_BANKS)
                    out = pair_ps(p)
                    if tokens_out:
                        for k in range(KB):
                            mm = pe.matmul(out, lhsT=rhs[:, k, i * P:(i + 1) * P], rhs=w[:, k, :],
                                           start=(k == 0), stop=(k == KB - 1))
                    else:
                        for j in range(2):
                            for k in range(KB):
                                if ready and i == 0 and j == 0:
                                    ready(k)
                                mm = pe.matmul(out[:, j * S:(j + 1) * S], lhsT=w[:, k, (2 * i + j) * P:(2 * i + j + 1) * P],
                                               rhs=rhs[:, k, :], start=(k == 0), stop=(k == KB - 1))
                    post(mm, "pairs")
                for i in range(*MOD_AFTER.get(u, (0, 0))):
                    mod_chunk(i)

            def mod_chunk(i):
                need(pe, "mod_part", i + 1)
                for j in range(2):
                    mm = pe.matmul(ps[:, 7, 2 * i + j:2 * i + j + 1], lhsT=mod_w[:, i % 2, 0, j * P:(j + 1) * P], rhs=cst("one"),
                                   start=True, stop=True)
                post(mm, "mod_sum")

            def four(name, lhs, rhs, transpose=False):
                out = tile_begin(name)
                for h in range(NH):
                    o = out[:, h * P:(h + 1) * P]
                    if transpose:
                        mm = pe.transpose(o, lhs(h), ident)
                    else:
                        mm = pe.matmul(o, lhsT=lhs(h), rhs=rhs(h), start=True, stop=True)
                post(mm, "tiles")

            pe.wait_ge(sem("const_in"), 16)
            need(pe, "squares", 1)
            sum_channels("ss_x", sq, KB)
            need(pe, "squares", 2)
            sum_channels("ss_mem", sq, KB)
            unit("q", xn, ready=lambda k: need(pe, "xn", k + 1))
            pe.wait_ge(sem("small_in"), 16)
            out = tile_begin("logits")
            for t in range(TT):
                for k in range(KB):
                    mm = pe.matmul(out[:, t * 8:(t + 1) * 8], lhsT=xn[:, k, t * P:(t + 1) * P], rhs=small_w[:, k, :],
                                   start=(k == 0), stop=(k == KB - 1))
            post(mm, "tiles")
            unit("k", xn)
            unit("v", xn)
            for i, n in enumerate(("ss_q0", "ss_q1", "ss_k0", "ss_k1")):
                need(pe, "qk_squares", i // 2 + 1)
                out = tile_begin(n)
                post(pe.matmul(out, lhsT=ones, rhs=norm2[:, 512 * (i % 2) + 1024 * (i // 2):][:, 0:512],
                               start=True, stop=True), "tiles")
            unit("b", xn)
            need(pe, "g")
            out = tile_begin("gcum")
            g = tiny[:, 8].rearrange("p t h -> p (t h)")
            pe.matmul(out[:, 0:8], lhsT=cst("upto"), rhs=g, start=True, stop=True)
            post(pe.matmul(out[:, 8:16], lhsT=cst("whole"), rhs=g, start=True, stop=True), "tiles")
            for t in range(TT):
                four(f"gB{t}", lambda h: tiny[:, 8, t, h:h + 1].broadcast_to([P, P]), lambda h: cst("upto"))
            unit("c", xn)
            unit("h", xn)
            def seg(i, h, t):
                return qkv[:, 4 * i + h, t * P:(t + 1) * P]
            need(pe, "k_normed")
            for t in range(TT):
                four(f"ktok{t}", lambda h: seg(1, h, t), None, transpose=True)
            for t in range(TT):
                four(f"vtok{t}", lambda h: seg(2, h, t), None, transpose=True)
            for t in range(TT):
                four(f"KK{t}", lambda h: seg(1, h, t), lambda h: seg(1, h, t))
            need(pe, "q_normed")
            for t in range(TT):
                four(f"QK{t}", lambda h: seg(0, h, t), lambda h: seg(1, h, t))
            unit("z", xn)
            for t in range(TT):
                need(pe, "N16", t + 1)
                four(f"NT{t}", lambda h: N_[:, t, h], None, transpose=True)
            for r in ("2", "4"):
                for t in range(TT):
                    need(pe, "P_ready", (t + 1) if r == "2" else TT + 2 * t + 2)
                    four(f"P{r}_{t}", lambda h: NT[:, t, h], lambda h: N_[:, t, h])
                    four(f"PT{r}_{t}", lambda h: N_[:, t, h], lambda h: NT[:, t, h])
                for t in range(TT):
                    need(pe, "P_ready", TT + (0 if r == "2" else 2 * TT) + 2 * t + 2)
                    need(pe, "T_ready", (2 * t + 2) + (0 if r == "2" else 2 * TT))
                    four(f"T{r}_{t}", lambda h: T_T[:, t, h], lambda h: N_[:, t, h])
                    four(f"TT{r}_{t}", lambda h: N_[:, t, h], lambda h: T_T[:, t, h])
            unit("mem_k0", hB, ready=lambda k: need(pe, "mem_n", k + 1))
            for t in range(TT):
                four(f"P8_{t}", lambda h: NT[:, t, h], lambda h: N_[:, t, h])
            for t in range(TT):
                need(pe, "P_ready", 5 * TT + t + 1)
                need(pe, "T_ready", 4 * TT + 2 * t + 2)
                four(f"T8_{t}", lambda h: T_T[:, t, h], lambda h: N_[:, t, h])
                four(f"TT8_{t}", lambda h: N_[:, t, h], lambda h: T_T[:, t, h])
            for t in range(TT):
                need(pe, "T_ready", 6 * TT + 2 * t + 2)
                four(f"Y32_{t}", lambda h: off32[:, t, h], lambda h: T_T[:, t, h])
            for t in range(TT):
                need(pe, "Y_ready", t + 1)
                four(f"T32_{t}", lambda h: Y[:, t, h], lambda h: T_[:, t, h])
                four(f"TT32_{t}", lambda h: T_[:, t, h], lambda h: Y[:, t, h])
            unit("mem_k1", hB)
            for t in range(TT):
                need(pe, "T_ready", 8 * TT + 2 * t + 2)
                four(f"Y64_{t}", lambda h: off64[:, t, h], lambda h: T_T[:, t, h])
            for t in range(TT):
                need(pe, "Y_ready", TT + t + 1)
                four(f"TT64_{t}", lambda h: T_[:, t, h], lambda h: Y[:, t, h])
            for t in range(TT):
                need(pe, "intra", t + 1)
                four(f"intraT{t}", lambda h: intra[:, t, h], None, transpose=True)
            for t in range(TT):
                need(pe, "T_ready", 10 * TT + t + 1)
                four(f"u{t}", lambda h: T_T[:, t, h], lambda h: vbeta[:, t, h])
            for t in range(TT):
                four(f"wT{t}", lambda h: kbe[:, t, h], lambda h: T_T[:, t, h])
            unit("mem_v0", hB, tokens_out=True)
            need(pe, "delta_operands", 6)
            for c in range(4):
                t, o = c // 2, CHUNK * (c % 2)
                rows = slice(o, o + CHUNK)
                if c:
                    need(pe, "state", c)
                    out = tile_begin(f"wS{c}")
                    for h in range(NH):
                        mm = pe.matmul(out[rows, h * P:(h + 1) * P], lhsT=wT[:, t, h, rows], rhs=S_st[:, h, :],
                                       start=True, stop=True)
                    post(mm, "tiles")
                out = tile_begin(f"o{c}")
                need(pe, "v_new", c + 1)
                for h in range(NH):
                    oh = out[:, h * CHUNK:(h + 1) * CHUNK]
                    if c:
                        pe.matmul(oh, lhsT=S_st[:, h, :], rhs=qdec[:, t, h, rows], start=True, stop=False)
                    mm = pe.matmul(oh, lhsT=v_new[rows, t, h, :], rhs=intraT[rows, t, h, rows], start=(c == 0), stop=True)
                post(mm, "tiles")
                out = tile_begin(f"dS{c}")
                for h in range(NH):
                    mm = pe.matmul(out[:, h * P:(h + 1) * P], lhsT=kdec[rows, t, h, :], rhs=v_new[rows, t, h, :],
                                   start=True, stop=True)
                post(mm, "tiles")
            unit("mem_v1", hB, tokens_out=True)
            need(pe, "o_squares")
            for i in range(2):
                out = tile_begin(f"ss_o{i}")
                post(pe.matmul(out, lhsT=ones, rhs=norm2[:, 512 * i:512 * (i + 1)], start=True, stop=True), "tiles")
            unit("mix_out0", yT, ready=lambda k: need(pe, "y_conv", k + 1) if k < 4 else need(pe, "y_dn", k - 3))
            unit("mix_out1", yT)
            need(pe, "squares", 3)
            sum_channels("ss_h1", sq, KB)
            unit("xq0", xn, ready=lambda k: need(pe, "xn", KB + k + 1))
            unit("xq1", xn)
            need(pe, "mem_kv", 8)
            for h in range(NH):
                need(pe, "aq", h + 1)
                out = tile_begin(f"att_s{h}")
                for t in range(TT):
                    for j in range(2):
                        mm = pe.matmul(out[:, t * S:(t + 1) * S], lhsT=aq[:, 2 * h + j, t * P:(t + 1) * P],
                                       rhs=mem_kT[:, 2 * h + j, :], start=(j == 0), stop=(j == 1))
                post(mm, "tiles")
            for h in range(NH):
                need(pe, "prob", TT * (h + 1))
                out = tile_begin(f"att_p{h}")
                for m in range(2):
                    for t in range(TT):
                        mm = pe.transpose(out[:, m * S + t * P:m * S + (t + 1) * P], prob[:, h, t, m * P:(m + 1) * P], ident)
                post(mm, "tiles")
            for h in range(NH):
                need(pe, "probT", h + 1)
                out = tile_begin(f"att_o{h}")
                for j in range(2):
                    for m in range(2):
                        mm = pe.matmul(out[:, j * S:(j + 1) * S], lhsT=mem_v[:, m, (2 * h + j) * P:(2 * h + j + 1) * P],
                                       rhs=probT[:, h, m, :], start=(m == 0), stop=(m == 1))
                post(mm, "tiles")
            unit("xo0", ao, ready=lambda k: need(pe, "ao", k // 2 + 1))
            unit("xo1", ao)
            need(pe, "squares", 4)
            sum_channels("ss_h2", sq, KB)
            unit("pq0", xn, ready=lambda k: need(pe, "xn", 2 * KB + k + 1))
            unit("pq1", xn)
            pe.wait_ge(sem("keys_in"), 16)
            for t in range(TT):
                for i in range(4):
                    half = slice(64 * (i % 2), 64 * (i % 2) + 64)
                    need(pe, "pq", 2 * (i // 2) + 2)
                    out = tile_begin(f"sc{t}_{i}")
                    for j in range(4):
                        h = 4 * (i // 2) + j
                        mm = pe.matmul(out[:, j * KEYS:(j + 1) * KEYS], lhsT=pq[half, h, t * P:(t + 1) * P],
                                       rhs=keys[half, h, :], start=True, stop=True)
                    post(mm, "tiles")
            need(pe, "scores", 8)
            need(pe, "mod_read")
            for t in range(TT):
                for i in range(2):
                    for j in range(4):
                        mm = pe.transpose(ps[:, 4 + 2 * t + i, j * P:(j + 1) * P], xn[:, 4 * i + j, t * P:(t + 1) * P], ident)
                    post(mm, "x_tok")
            need(pe, "pq", 4)
            need(pe, "zeros")
            for i in range(4):
                pe.matmul(ps[:, i, :], lhsT=diag[:, 0], rhs=const[:, 0:512],
                          start=True, stop=False, skip_group_check=True).then_inc(sem("acc_zero"), 1)
            for t in range(TT):
                with pe.Fori(0, PH) as h:
                    for j in range(TOPK):
                        b = j % RING
                        pe.wait_ge(sem("diag"), t * PH * TOPK + h * TOPK + j + 1)
                        for n in range(2):
                            mm = pe.matmul(ps[:, 2 * t + n, :], lhsT=diag[:, j], rhs=ring[b][:, D + 512 * n:D + 512 * (n + 1)],
                                           start=False, stop=False, skip_group_check=True)
                        mm.then_inc(sem(f"row_free{b}"), 1)
                need(pe, "y_tok", t + 1)
                for i in range(2):
                    for j in range(4):
                        mm = pe.transpose(ps[:, 4 + 2 * t + i, j * P:(j + 1) * P],
                                          ysb[t][:, (4 * i + j) * P:(4 * i + j + 1) * P], ident)
                    post(mm, "y_back")
            need(pe, "squares", 5)
            sum_channels("ss_h3", sq, KB)
            need(pe, "squares", 6)
            sum_channels("ss_m0", sq, KB)
            for i in range(4):
                unit(f"cv_ab{i}", xn, ready=(lambda k: need(pe, "xn", 3 * KB + k + 1)) if i == 0 else None)
            unit("cv_g0", xn)
            unit("cv_g1", xn)
            for k in range(KB):
                need(pe, "conv_out", k + 1)
            sum_channels("mean", yc, KB)
            need(pe, "squares", 7)
            sum_channels("var", sq, KB)
            unit("cv_out0", ycn, ready=lambda k: need(pe, "cv_y", k + 1))
            unit("cv_out1", ycn)
            need(pe, "squares", 8)
            sum_channels("ss_m1", sq, KB)
            unit("pl_v0", xn, ready=lambda k: need(pe, "xn", 4 * KB + k + 1))
            for n in ("pl_v1", "pl_g0", "pl_g1"):
                unit(n, xn)
            n = UNITS.index("grp")
            wg = wring[:, n % W_SLOTS].rearrange("p k n -> p (k n)")[:, 0:2048].rearrange("p (k n) -> p k n", k=8)
            pe.wait_ge(sem(f"w_in{n % W_SLOTS}"), 16 * (n // W_SLOTS + 1))
            for g in range(4):
                p = FIRST_PAIR["grp"] + g
                pe.wait_ge(sem(f"pair_free{p % PAIR_BANKS}"), p // PAIR_BANKS)
                need(pe, "pooled", g + 1)
                for j in range(2):
                    for k in range(2):
                        mm = pe.matmul(pair_ps(p)[:, j * S:(j + 1) * S], lhsT=wg[:, 2 * g + k, j * P:(j + 1) * P],
                                       rhs=pooled[:, 2 * g + k, :], start=(k == 0), stop=(k == 1))
                post(mm, "pairs")
            unit("pl_out0", ycn, ready=lambda k: need(pe, "pl_y", k + 1))
            unit("pl_out1", ycn)

        @block.scalar
        def _(act):
            def go(ins, name):
                return did(act, ins, name)

            act.dma_start(hA[:], x_t).then_inc(sem("x_in"), 16)
            act.dma_start(const[:], const_d).then_inc(sem("const_in"), 16)
            act.dma_start(cols[:], cols_d).then_inc(sem("cols_in"), 16)
            act.dma_start(hB[:], mem_t).then_inc(sem("mem_in"), 16)
            act.dma_start(small_w[:], small_d).then_inc(sem("small_in"), 16)

            def squares(src):
                go(act.activation(sq[:], src, ACT.Square), "squares")

            def root(name, out, n, scale):
                tile_ready(act, name)
                tile_used_wait(act, act.activation(out, tile_ps(name)[:, 0:n], ACT.Sqrt, bias=cst("eps"), scale=scale), name)

            act.wait_ge(sem("x_in"), 16)
            squares(hA[:])
            act.wait_ge(sem("const_in"), 16)
            root("ss_x", rms[:, 0], S, 1.0 / D)
            signal(act, "root")
            act.wait_ge(sem("mem_in"), 16)
            squares(hB[:])
            need(act, "rinv", 1)
            root("ss_mem", rms[:, 0], S, 1.0 / D)
            signal(act, "root")
            act.wait_ge(sem("cols_in"), 16)
            go(act.activation(silu_c[:], col("c", 0, KB), ACT.Silu), "silu_c")
            need(act, "pads")
            for i, u in enumerate(("q", "k", "v")):
                for j in range(2):
                    p = FIRST_PAIR[u] + j
                    pair_ready(act, p)
                    pair_used_wait(act, act.copy(qkv_pad[:, 4 * i + 2 * j:4 * i + 2 * j + 2, 3:3 + S],
                                                 pair_ps(p).rearrange("p (b t) -> p b t", b=2)), p)
                    signal(act, "qkv_in", 1)
            for i in range(3):
                need(act, "qkv_conv", 4 * (i + 1))
                v = qkv[:, 4 * i:4 * i + 4, :]
                go(act.activation(v, v, ACT.Silu), "qkv_act")
            for i in range(2):
                go(act.activation(blocks(norm2[:, 1024 * i:1024 * (i + 1)], 4), qkv[:, 4 * i:4 * i + 4, :], ACT.Square), "qk_squares")
            for i, n in enumerate(("ss_q0", "ss_q1", "ss_k0", "ss_k1")):
                root(n, norm2[:, 512 * i:512 * (i + 1)], 512, 1.0)
                signal(act, "qk_root", 1)
            need(act, "logits")
            beta_l, z_abs = tiny[:, 1], tiny[:, 4]
            go(act.activation(tiny[:, 2], beta_l, ACT.Exp, scale=-1.0), "exp_b")
            need(act, "z_abs")
            go(act.activation(tiny[:, 5], z_abs, ACT.Exp, scale=-1.0), "exp_z")
            go(act.activation(tiny[:, 6, 0], col("a_log", 0, NH), ACT.Exp), "exp_a")
            need(act, "z_exp1")
            go(act.activation(tiny[:, 5], tiny[:, 5], ACT.Ln), "ln_z")
            for j in range(2):
                p = FIRST_PAIR["b"] + j
                pair_ready(act, p)
                pair_used_wait(act, act.copy(bT[:, 2 * j:2 * j + 2, :], blocks(pair_ps(p), 2)), p)
                signal(act, "bT", 1)
            need(act, "gcum")
            go(act.activation(tiny[:, 10], tiny[:, 9], ACT.Exp), "exp_g")
            go(act.activation(tiny[:, 12], tiny[:, 11], ACT.Exp), "exp_gd")
            for t in range(TT):
                tile_ready(act, f"gB{t}")
                go(act.activation(egB[:, t].rearrange("p h j -> p (h j)"), tile_ps(f"gB{t}"), ACT.Exp), "egB")
            for t in range(TT):
                need(act, "diff", t + 1)
                go(act.activation(E[:, t], E[:, t], ACT.Exp, scale=-1.0), "E")
            for j in range(2):
                p = FIRST_PAIR["c"] + j
                pair_ready(act, p)
                pair_used_wait(act, act.copy(cT[:, 2 * j:2 * j + 2, :], blocks(pair_ps(p), 2)), p)
                signal(act, "cT", 1)
            for j in range(2):
                p = FIRST_PAIR["z"] + j
                pair_ready(act, p)
                pair_used_wait(act, act.activation(zT[:, 2 * j:2 * j + 2, :], blocks(pair_ps(p), 2), ACT.Silu), p)
                signal(act, "zT", 1)
            def kv_copy(u):
                for j in range(2):
                    p = FIRST_PAIR[u] + j
                    pair_ready(act, p)
                    if u[4] == "k":
                        dst, src = mem_kT[:, 4 * int(u[5]) + 2 * j:4 * int(u[5]) + 2 * j + 2, :], blocks(pair_ps(p), 2)
                    else:
                        dst, src = mem_v[:, j, 512 * int(u[5]):512 * int(u[5]) + 512], pair_ps(p)
                    pair_used_wait(act, act.copy(dst, src), p)
                    signal(act, "mem_kv", 1)
            kv_copy("mem_k0")
            kv_copy("mem_k1")
            for t in range(TT):
                tile_ready(act, f"intraT{t}")
                tile_used_wait(act, act.copy(intraT[:, t].rearrange("p h j -> p (h j)"), tile_ps(f"intraT{t}")), f"intraT{t}")
                signal(act, "delta_operands", 1)
            for t in range(TT):
                tile_ready(act, f"u{t}")
                tile_used_wait(act, act.copy(u_tok[:, t].rearrange("p h j -> p (h j)"), tile_ps(f"u{t}")), f"u{t}")
                signal(act, "delta_operands", 1)
            for t in range(TT):
                tile_ready(act, f"wT{t}")
                tile_used_wait(act, act.copy(wT[:, t].rearrange("p h j -> p (h j)"), tile_ps(f"wT{t}")), f"wT{t}")
                signal(act, "delta_operands", 1)
            kv_copy("mem_v0")
            need(act, "inverted")
            for c in range(4):
                tile_ready(act, f"o{c}")
                tile_used_wait(act, act.copy(oT[:, :, c * CHUNK:(c + 1) * CHUNK],
                                             tile_ps(f"o{c}")[:, 0:NH * CHUNK].rearrange("p (h j) -> p h j", h=NH)), f"o{c}")
            kv_copy("mem_v1")
            need(act, "scanned")
            act.dma_start(keys, keys_d).then_inc(sem("keys_in"), 16)
            go(act.activation(blocks(norm2[:, 0:1024], 4), oT, ACT.Square), "o_squares")
            for i in range(2):
                root(f"ss_o{i}", norm2[:, 512 * i:512 * (i + 1)], 512, 1.0 / P)
                signal(act, "o_root", 1)

            def norm_act(src, name, ready, n, rinvs):
                ready()
                squares(src)
                need(act, "rinv", rinvs)
                root(name, rms[:, 0], S, 1.0 / D)
                signal(act, "root")

            norm_act(hB[:], "ss_h1", lambda: need(act, "h1", 4), 2, 2)
            for u in ("xq0", "xq1"):
                for j in range(2):
                    p = FIRST_PAIR[u] + j
                    b = 4 * int(u[2]) + 2 * j
                    pair_ready(act, p)
                    pair_used_wait(act, act.copy(aq[:, b:b + 2, :], blocks(pair_ps(p), 2)), p)
                    signal(act, "aq", 1)
            for h in range(NH):
                need(act, "att_max", h + 1)
                for t in range(TT):
                    ins = act.activation(prob[:, h, t], tile_ps(f"att_s{h}")[:, t * S:(t + 1) * S], ACT.Exp,
                                         bias=tiny[:, 14, t, h:h + 1], scale=float(S) ** -0.5,
                                         accum_out=tiny[:, 15, t, h:h + 1])
                    if t == TT - 1:
                        tile_used_wait(act, ins, f"att_s{h}")
                    else:
                        go(ins, "att_exp0")
                signal(act, "att_exp", 1)
            for h in range(NH):
                tile_ready(act, f"att_p{h}")
                tile_used_wait(act, act.copy(probT[:, h].rearrange("p m t -> p (m t)"), tile_ps(f"att_p{h}")), f"att_p{h}")
                signal(act, "probT", 1)
            for h in range(NH):
                tile_ready(act, f"att_o{h}")
                tile_used_wait(act, act.copy(ao[:, 2 * h:2 * h + 2, :], blocks(tile_ps(f"att_o{h}"), 2)), f"att_o{h}")
                signal(act, "ao", 1)
            norm_act(hA[:], "ss_h2", lambda: need(act, "h2", 4), 3, 3)
            for u in ("pq0", "pq1"):
                for j in range(2):
                    p = FIRST_PAIR[u] + j
                    b = 4 * int(u[2]) + 2 * j
                    pair_ready(act, p)
                    pair_used_wait(act, act.copy(pq[:, b:b + 2, :], blocks(pair_ps(p), 2)), p)
                    signal(act, "pq", 1)
            for t in range(TT):
                s4 = score[t].rearrange("p (h s n) -> p h s n", h=PH, s=2)
                for i in range(4):
                    tile_ready(act, f"sc{t}_{i}")
                    tile_used_wait(act, act.copy(s4[:, 4 * (i // 2):4 * (i // 2) + 4, i % 2, :],
                                                 tile_ps(f"sc{t}_{i}").rearrange("p (h n) -> p h n", h=4)), f"sc{t}_{i}")
                    signal(act, "scores", 1)
            def gate_exp(r):
                act.wait_ge(sem("gate_arg"), r + 1)
                act.activation(gexp, gexp, ACT.Exp, accum_out=gsum).then_inc(sem("gate_exp"), 1)

            for r in range(AHEAD):
                gate_exp(r)
            for t in range(TT):
                for first, last in HEAD_LOOPS[t]:
                    with act.Fori(first, last) as h:
                        for j in range(TOPK):
                            act.wait_ge(sem("dots"), (t * PH + h) * TOPK + j + 1)
                            act.activation(gel16[:, j:j + 1], act16[:, j:j + 1], ACT.Gelu).then_inc(sem("gelu"), 1)
                            if j == 10 and t * PH + first + AHEAD < HEADS:
                                gate_exp(t * PH + h + AHEAD)
                act.wait_ge(sem(f"row_free{RING - 1}"), (t + 1) * 2 * PH + 1)
                for n in range(2):
                    go(act.copy(ysb[t][:, 512 * n:512 * (n + 1)], ps[:, 2 * t + n, :]), "y_half")
                signal(act, "y_tok", 1)
            norm_act(hA[:], "ss_h3", lambda: need(act, "h2y", 4), 4, 4)
            norm_act(hB[:], "ss_m0", lambda: need(act, "h3", KB), 5, 5)
            for i in range(4):
                p = FIRST_PAIR[f"cv_ab{i}"] + 1
                pair_ready(act, p)
                if i:
                    need(act, "glu", i)
                pair_used_wait(act, act.activation(sgb, blocks(pair_ps(p), 2), ACT.Sigmoid), p)
                signal(act, "sig_b", 1)
            for i in range(2):
                for j in range(2):
                    p = FIRST_PAIR[f"cv_g{i}"] + j
                    b = 4 * i + 2 * j
                    pair_ready(act, p)
                    pair_used_wait(act, act.activation(gT[:, b:b + 2, :], blocks(pair_ps(p), 2), ACT.Silu), p)
                    signal(act, "gT", 1)
            tile_ready(act, "mean")
            need(act, "rinv", 6)
            tile_used_wait(act, act.activation(rms[:, 0], tile_ps("mean")[:, 0:S], ACT.Copy, scale=1.0 / D), "mean")
            signal(act, "mean_sb", 1)
            need(act, "centred")
            squares(yc)
            root("var", rms[:, 0], S, 1.0 / D)
            signal(act, "root")
            for k in range(KB):
                need(act, "standard", k + 1)
                go(act.activation(ycn[:, k], ycn[:, k], ACT.Silu, bias=col("ln_b", k), scale=col("ln_g", k)), "ln_silu")
            norm_act(hA[:], "ss_m1", lambda: need(act, "h4", KB), 7, 7)
            for i in range(4):
                p = FIRST_PAIR["pl_v0"] + i
                pair_ready(act, p)
                pair_used_wait(act, act.copy(vpad[:, 2 * i:2 * i + 2, 8:8 + S], blocks(pair_ps(p), 2)), p)
                signal(act, "vpad", 1)
            for i in range(4):
                p = FIRST_PAIR["pl_g0"] + i
                pair_ready(act, p)
                pair_used_wait(act, act.activation(gT[:, 2 * i:2 * i + 2, :], blocks(pair_ps(p), 2), ACT.Silu), p)
                signal(act, "gT", 1)

        @block.vector
        def _(dve):
            V = nc.vector

            def go(ins, name="dve_step"):
                return did(dve, ins, name)

            def norm(n, src, dst, gain, name):
                need(dve, "root", n)
                go(V.reciprocal(rinv[:, 0], rms[:, 0]), "rinv")
                for k in range(KB):
                    last = post(V.scalar_tensor_tensor(out=dst[:, k], in0=src[:, k], scalar=col(gain, k), in1=rinv[:, 0],
                                                       op0=ALU.mult, op1=ALU.mult), name)
                need(dve, name, last)

            def norm_mod(n, src, layer):
                need(dve, "root", n)
                go(V.reciprocal(rinv[:, 0], rms[:, 0]), "rinv")
                for k in range(KB):
                    go(V.tensor_tensor(xn[:, k], src[:, k], rinv[:, 0], ALU.mult))
                    last = post(V.tensor_scalar(xn[:, k], xn[:, k], gmod[:, layer, k:k + 1],
                                                modc[:, 24 * layer + k:24 * layer + k + 1], ALU.mult, ALU.add), "xn")
                need(dve, "xn", last)

            dve.memset(qkv_pad[:, :, 0:3], 0.0)
            go(V.memset(hc_pad[:, :, 0:2], 0.0), "pads")
            dve.wait_ge(sem("cols_in"), 16)
            norm(1, hA, xn, "norm_mix", "xn")
            norm(2, hB, hB, "norm_mem", "mem_n")

            dve.wait_ge(sem("const_in"), 16)
            tile_ready(dve, "logits")
            lg = tile_ps("logits")[:, 0:16].rearrange("p (t c) -> p t c", t=TT)
            dt = col("dt_bias", 0, NH).unsqueeze(1).broadcast_to([P, TT, NH])
            go(V.tensor_copy(tiny[:, 1], lg[:, :, 0:4]), "logits")
            tile_used_wait(dve, V.tensor_tensor(tiny[:, 3], lg[:, :, 4:8], dt, ALU.add), "logits")
            go(V.scalar_tensor_tensor(out=tiny[:, 4], in0=tiny[:, 3], scalar=-1.0, in1=tiny[:, 3],
                                      op0=ALU.mult, op1=ALU.max), "z_abs")
            go(V.tensor_scalar(tiny[:, 3], tiny[:, 3], 0.0, None, ALU.max))

            for b in range(12):
                need(dve, "qkv_in", b // 2 + 1)
                for i in range(DN_TAPS):
                    w = col("dn_conv_w", 12 * i + b)
                    x = qkv_pad[:, b, i:i + S]
                    if i == 0:
                        go(V.tensor_scalar(qkv[:, b], x, w, None, ALU.mult))
                    else:
                        ins = V.scalar_tensor_tensor(out=qkv[:, b], in0=x, scalar=w, in1=qkv[:, b], op0=ALU.mult, op1=ALU.add)
                        go(ins, "qkv_conv" if i == DN_TAPS - 1 else "dve_step")

            need(dve, "exp_b")
            go(V.tensor_scalar(tiny[:, 2], tiny[:, 2], 1.0, None, ALU.add))
            go(V.reciprocal(tiny[:, 2], tiny[:, 2]), "beta")
            need(dve, "exp_z")
            go(V.tensor_scalar(tiny[:, 5], tiny[:, 5], 1.0, None, ALU.add), "z_exp1")
            need(dve, "ln_z")
            go(V.tensor_tensor(tiny[:, 7], tiny[:, 3], tiny[:, 5], ALU.add))
            need(dve, "exp_a")
            go(V.scalar_tensor_tensor(out=tiny[:, 8], in0=tiny[:, 7], scalar=-1.0,
                                      in1=tiny[:, 6, 0].unsqueeze(1).broadcast_to([P, TT, NH]),
                                      op0=ALU.mult, op1=ALU.mult), "g")
            beta, eg, egd = tiny[:, 2], tiny[:, 10], tiny[:, 12]

            def flat(ap):
                return ap.rearrange("p t h -> p (t h)")

            for i in range(2):
                need(dve, "qk_root", 2 * (i + 1))
                r = norm2[:, 1024 * i:1024 * (i + 1)]
                go(V.reciprocal(r, r))
                x = qkv[:, 4 * i:4 * i + 4, :]
                if i == 0:
                    go(V.scalar_tensor_tensor(out=x, in0=x, scalar=float(P) ** -0.5, in1=blocks(r, 4),
                                              op0=ALU.mult, op1=ALU.mult), "q_normed")
                else:
                    go(V.tensor_tensor(x, x, blocks(r, 4), ALU.mult), "k_normed")

            tile_ready(dve, "gcum")
            go(V.tensor_copy(flat(tiny[:, 9]), tile_ps("gcum")[:, 0:8]))
            tile_used_wait(dve, V.tensor_tensor(flat(tiny[:, 11]), tile_ps("gcum")[:, 8:16], flat(tiny[:, 9]), ALU.subtract), "gcum")
            signal(dve, "gcum", 1)
            for t in range(TT):
                need(dve, "egB", t + 1)
                src = tile_ps(f"gB{t}").rearrange("p (h j) -> p h j", h=NH)
                tile_used_wait(dve, V.tensor_tensor(E[:, t], src, tiny[:, 9, t].unsqueeze(2).broadcast_to([P, NH, P]), ALU.subtract), f"gB{t}")
                go(V.tensor_scalar(E[:, t], E[:, t], 0.0, None, ALU.max), "diff")
            need(dve, "exp_g")
            go(V.tensor_tensor(tiny[:, 13], beta, eg, ALU.mult))
            need(dve, "exp_gd")

            def per_token(t, src, dst, c):
                return V.tensor_tensor(dst[:, t], src, c[:, t].unsqueeze(2).broadcast_to([P, NH, P]), ALU.mult)

            def tile_heads(name):
                return tile_ps(name).rearrange("p (h j) -> p h j", h=NH)

            need(dve, "egB", TT)
            for t in range(TT):
                go(V.tensor_tensor(qdec[:, t], qkv[:, 0:4, t * P:(t + 1) * P], egB[:, t], ALU.mult))
            for c in range(4):
                go(V.tensor_copy(gl[:, c], egB[:, c // 2, :, CHUNK * (c % 2) + CHUNK - 1]))
            for t in range(TT):
                tile_ready(dve, f"ktok{t}")
                go(per_token(t, tile_heads(f"ktok{t}"), kbe, tiny[:, 13]))
                tile_used_wait(dve, per_token(t, tile_heads(f"ktok{t}"), kdec, egd), f"ktok{t}")
            for t in range(TT):
                tile_ready(dve, f"vtok{t}")
                tile_used_wait(dve, per_token(t, tile_heads(f"vtok{t}"), vbeta, beta), f"vtok{t}")

            for j in range(2):
                p = FIRST_PAIR["h"] + j
                need(dve, "cT", j + 1)
                pair_ready(dve, p)
                pair_used_wait(dve, V.tensor_tensor(hc_pad[:, 2 * j:2 * j + 2, 2:2 + S], blocks(pair_ps(p), 2),
                                                    cT[:, 2 * j:2 * j + 2, :], ALU.mult), p)
            need(dve, "bT", 2)
            for b in range(4):
                go(V.tensor_scalar(yT[:, b], hc_pad[:, b, 0:S], col("conv_w", b), None, ALU.mult))
                for i in range(1, TAPS):
                    go(V.scalar_tensor_tensor(out=yT[:, b], in0=hc_pad[:, b, i:i + S], scalar=col("conv_w", 4 * i + b),
                                              in1=yT[:, b], op0=ALU.mult, op1=ALU.add))
                go(V.tensor_tensor(yT[:, b], yT[:, b], bT[:, b], ALU.mult), "y_conv")

            def mask(name):
                return cst(name).unsqueeze(1).broadcast_to([P, NH, P])

            for t in range(TT):
                need(dve, "E", t + 1)
                tile_ready(dve, f"KK{t}")
                tile_used_wait(dve, V.tensor_tensor(Y[:, t], tile_heads(f"KK{t}"), E[:, t], ALU.mult), f"KK{t}")
                go(V.tensor_tensor(Y[:, t], Y[:, t], beta[:, t].unsqueeze(2).broadcast_to([P, NH, P]), ALU.mult))
                go(V.scalar_tensor_tensor(out=N_[:, t], in0=Y[:, t], scalar=-1.0, in1=mask("strict16"),
                                          op0=ALU.mult, op1=ALU.mult), "N16")
                go(V.tensor_tensor(off32[:, t], Y[:, t], mask("off32"), ALU.mult))
                go(V.tensor_tensor(off64[:, t], Y[:, t], mask("off64"), ALU.mult))
                go(V.tensor_tensor(E[:, t], E[:, t], mask("causal"), ALU.mult))
                tile_ready(dve, f"QK{t}")
                tile_used_wait(dve, V.tensor_tensor(intra[:, t], tile_heads(f"QK{t}"), E[:, t], ALU.mult), f"QK{t}")
                signal(dve, "intra", 1)
            for t in range(TT):
                tile_ready(dve, f"NT{t}")
                tile_used_wait(dve, V.tensor_copy(NT[:, t], tile_heads(f"NT{t}")), f"NT{t}")
                signal(dve, "P_ready", 1)
                go(V.tensor_tensor(T_[:, t], N_[:, t], mask("ident"), ALU.add), "T_ready")
                go(V.tensor_tensor(T_T[:, t], NT[:, t], mask("ident"), ALU.add), "T_ready")

            def take(name, t, dst, ready):
                tile_ready(dve, f"{name}_{t}")
                tile_used_wait(dve, V.tensor_copy(dst[:, t], tile_heads(f"{name}_{t}")), f"{name}_{t}")
                if ready:
                    signal(dve, ready, 1)

            def accumulate(name, t, dst, op):
                tile_ready(dve, f"{name}_{t}")
                tile_used_wait(dve, V.tensor_tensor(dst[:, t], dst[:, t], tile_heads(f"{name}_{t}"), op), f"{name}_{t}")
                signal(dve, "T_ready", 1)

            for r in ("2", "4"):
                for t in range(TT):
                    tile_ready(dve, f"PT{r}_{t}")
                    take(f"P{r}", t, N_, "P_ready")
                    take(f"PT{r}", t, NT, "P_ready")
                for t in range(TT):
                    tile_ready(dve, f"TT{r}_{t}")
                    accumulate(f"T{r}", t, T_, ALU.add)
                    accumulate(f"TT{r}", t, T_T, ALU.add)
            for t in range(TT):
                take("P8", t, N_, "P_ready")
            for t in range(TT):
                tile_ready(dve, f"TT8_{t}")
                accumulate("T8", t, T_, ALU.add)
                accumulate("TT8", t, T_T, ALU.add)
            for t in range(TT):
                take("Y32", t, Y, "Y_ready")
            for t in range(TT):
                tile_ready(dve, f"TT32_{t}")
                accumulate("T32", t, T_, ALU.subtract)
                accumulate("TT32", t, T_T, ALU.subtract)
            for t in range(TT):
                take("Y64", t, Y, "Y_ready")
            for t in range(TT):
                accumulate("TT64", t, T_T, ALU.subtract)
            tile_ready(dve, f"intraT{TT - 1}")
            signal(dve, "inverted", 1)
            need(dve, "delta_operands", 6)
            for c in range(4):
                t, o = c // 2, CHUNK * (c % 2)
                rows = slice(o, o + CHUNK)
                if c:
                    tile_ready(dve, f"wS{c}")
                    tile_used_wait(dve, V.tensor_tensor(v_new[rows, t], u_tok[rows, t],
                                                        tile_heads(f"wS{c}")[rows], ALU.subtract), f"wS{c}")
                    signal(dve, "v_new", 1)
                else:
                    go(V.tensor_copy(v_new[rows, t], u_tok[rows, t]), "v_new")
                tile_ready(dve, f"dS{c}")
                if c == 0:
                    tile_used_wait(dve, V.tensor_copy(S_st, tile_heads("dS0")), "dS0")
                else:
                    go(V.tensor_tensor(S_st, S_st, gl[:, c].unsqueeze(2).broadcast_to([P, NH, P]), ALU.mult))
                    tile_used_wait(dve, V.tensor_tensor(S_st, S_st, tile_heads(f"dS{c}"), ALU.add), f"dS{c}")
                signal(dve, "state", 1)
            signal(dve, "scanned", 1)
            need(dve, "o_root", 2)
            need(dve, "zT", 2)
            go(V.reciprocal(norm2[:, 0:1024], norm2[:, 0:1024]))
            go(V.tensor_tensor(zT, zT, blocks(norm2[:, 0:1024], 4), ALU.mult))
            for h in range(NH):
                go(V.scalar_tensor_tensor(out=yT[:, 4 + h], in0=oT[:, h], scalar=col("dn_norm"), in1=zT[:, h],
                                          op0=ALU.mult, op1=ALU.mult), "y_dn")

            def residual(unit0, src, dst, name):
                for i in range(4):
                    p = FIRST_PAIR[unit0] + i
                    pair_ready(dve, p)
                    pair_used_wait(dve, V.tensor_tensor(dst[:, 2 * i:2 * i + 2, :], blocks(pair_ps(p), 2),
                                                        src[:, 2 * i:2 * i + 2, :], ALU.add), p)
                    signal(dve, name, 1)

            residual("mix_out0", hA, hB, "h1")
            norm(3, hB, xn, "norm_x", "xn")
            for h in range(NH):
                tile_ready(dve, f"att_s{h}")
                go(V.tensor_reduce(tiny[:, 13, :, h], tile_ps(f"att_s{h}").rearrange("p (t m) -> p t m", t=TT), AX_X, ALU.max))
                go(V.tensor_scalar(tiny[:, 14, :, h], tiny[:, 13, :, h], -float(S) ** -0.5, None, ALU.mult), "att_max")
            for h in range(NH):
                need(dve, "att_exp", h + 1)
                go(V.reciprocal(tiny[:, 15, :, h], tiny[:, 15, :, h]))
                for t in range(TT):
                    go(V.tensor_scalar(prob[:, h, t], prob[:, h, t], tiny[:, 15, t, h:h + 1], None, ALU.mult), "prob")
            residual("xo0", hB, hA, "h2")
            norm(4, hA, xn, "norm_ffn", "xn")
            need(dve, "mod_sum", MOD_CHUNKS)
            go(V.tensor_tensor(modc[:], ps[:, 7, 0:48], col("b_mod", 0, 48), ALU.add), "mod_read")
            for layer in range(2):
                go(V.scalar_tensor_tensor(out=gmod[:, layer], in0=modc[:, 24 * layer + 8:24 * layer + 16], scalar=1.0,
                                          in1=col(f"norm_g{layer}", 0, KB), op0=ALU.add, op1=ALU.mult))
            go(V.memset(diag[:, 0], 0.0), "zeros")

            B4 = [P, 2, TOPK, TOPK]
            route_posts = [0]

            def route(step, r):
                def done(ins):
                    route_posts[0] += 1
                    ins.then_inc(sem("route"), 1)

                def so_far():
                    dve.wait_ge(sem("route"), r * ROUTE_POSTS + route_posts[0])
                    dve.sem_inc(sem("route_turn"), 1)

                if step == 0:
                    route_posts[0] = 0
                    done(V.tensor_copy(halves.rearrange("p s n -> p (s n)"), all_scores[:, bass.ds(r * 2 * KEYS, 2 * KEYS)]))
                elif step == 1:
                    so_far()
                    for s in range(2):
                        done(V.max(topv[:, s, 0:8], halves[:, s]))
                elif step == 2:
                    so_far()
                    for s in range(2):
                        done(V.max_index(topi[:, s, 0:8], topv[:, s, 0:8], halves[:, s]))
                        done(V.match_replace(scr[:, s * KEYS:(s + 1) * KEYS], topv[:, s, 0:8], halves[:, s], LOWEST))
                elif step == 3:
                    so_far()
                    for s in range(2):
                        done(V.max(topv[:, s, 8:16], scr[:, s * KEYS:(s + 1) * KEYS]))
                elif step == 4:
                    so_far()
                    for s in range(2):
                        done(V.max_index(topi[:, s, 8:16], topv[:, s, 8:16], scr[:, s * KEYS:(s + 1) * KEYS]))
                elif step == 5:
                    so_far()
                    done(V.tensor_copy(topf, topi))
                    done(V.tensor_tensor(cand.rearrange("p (a b) -> p a b", a=TOPK), topv[:, 0].unsqueeze(2).broadcast_to(B4[:1] + B4[2:]),
                                         topv[:, 1].unsqueeze(1).broadcast_to(B4[:1] + B4[2:]), ALU.add))
                elif step == 6:
                    so_far()
                    done(V.max(best[:, 0:8], cand))
                elif step == 7:
                    so_far()
                    done(V.max_index(posn[:, 0:8], best[:, 0:8], cand))
                    done(V.match_replace(scr, best[:, 0:8], cand, LOWEST))
                elif step == 8:
                    so_far()
                    done(V.max(best[:, 8:16], scr))
                elif step == 9:
                    so_far()
                    done(V.max_index(posn[:, 8:16], best[:, 8:16], scr))
                    V.tensor_tensor(gexp, best, best[:, 0:1].broadcast_to([P, TOPK]), ALU.subtract).then_inc(sem("gate_arg"), 1)
                elif step == 10:
                    so_far()
                    done(V.tensor_scalar(pab[:, 0], posn, 4, None, ALU.logical_shift_right))
                    done(V.tensor_scalar(pab[:, 1], posn, 15, None, ALU.bitwise_and))
                elif step == 11:
                    so_far()
                    done(V.tensor_copy(pabf, pab))
                elif step == 12:
                    so_far()
                    done(V.tensor_tensor(hot, pabf.unsqueeze(3).broadcast_to(B4),
                                         cst("iota16").unsqueeze(1).unsqueeze(1).broadcast_to(B4), ALU.is_equal))
                elif step == 13:
                    so_far()
                    done(V.tensor_tensor(hot, hot, topf.unsqueeze(2).broadcast_to(B4), ALU.mult))
                    dve.wait_ge(sem("gate_exp"), r + 1)
                    done(V.reciprocal(gsum, gsum))
                elif step == 14:
                    so_far()
                    done(V.tensor_reduce(picked, hot, AX_X, ALU.add))
                    done(V.tensor_tensor(gate[:, bass.ds(r * TOPK, TOPK)], gexp, gsum.broadcast_to([P, TOPK]), ALU.mult))
                else:
                    so_far()
                    V.scalar_tensor_tensor(out=idx[:, bass.ds(r * TOPK, TOPK)], in0=picked[:, 0],
                                           scalar=float(KEYS), in1=picked[:, 1], op0=ALU.mult, op1=ALU.add).then_inc(sem("routed"), 1)

            need(dve, "scores", 2)
            for r in range(AHEAD):
                for step in range(TOPK):
                    route(step, r)
            need(dve, "scores", 8)
            need(dve, "x_tok", 4)
            need(dve, "acc_zero", 4)

            for t in range(TT):
                x_tok = ps[:, 4 + 2 * t:6 + 2 * t, :].rearrange("p a b -> p (a b)")
                for first, last in HEAD_LOOPS[t]:
                    with dve.Fori(first, last) as h:
                        n = t * PH + h

                        def diagonal(j):
                            dve.wait_ge(sem("gelu"), n * TOPK + j + 1)
                            V.tensor_scalar(diag[:, j], ident, gel16[:, j:j + 1], gate_now[:, j:j + 1],
                                            ALU.mult, ALU.mult).then_inc(sem("diag"), 1)

                        V.tensor_copy(gate_now, gate[:, bass.ds(n * TOPK, TOPK)]).then_inc(sem("gate_now"), 1)
                        for j in range(TOPK):
                            b = j % RING
                            dve.wait_ge(sem(f"row_in{b}"), 16 * (n * 2 + j // RING + 1))
                            V.tensor_tensor_reduce(out=ring[b][:, 0:D], in0=ring[b][:, 0:D], in1=x_tok, scale=1.0, scalar=0.0,
                                                   op0=ALU.mult, op1=ALU.add, accum_out=act16[:, j:j + 1]).then_inc(sem("dots"), 1)
                            if t * PH + first + AHEAD < HEADS:
                                route(j, n + AHEAD)
                            if j == 1:
                                dve.wait_ge(sem("gate_now"), n + 1)
                            if j:
                                diagonal(j - 1)
                        diagonal(TOPK - 1)
                        dve.wait_ge(sem("diag"), (n + 1) * TOPK)
                        dve.sem_inc(sem("head_turn"), 1)
                for i in range(2):
                    need(dve, "y_back", 2 * t + i + 1)
                    src = ps[:, 4 + 2 * t + i, :].rearrange("p (k t) -> p k t", k=4)
                    h = hA[:, 4 * i:4 * i + 4, t * P:(t + 1) * P]
                    go(V.tensor_tensor(h, src, h, ALU.add), "h2y")
            norm(5, hA, hB, "norm_final", "h3")
            need(dve, "h3", KB)
            norm_mod(6, hB, 0)

            go(V.memset(ypad[:, :, 0:15], 0.0))
            go(V.memset(ypad[:, :, 15 + S:], 0.0))
            for i in range(4):
                p = FIRST_PAIR[f"cv_ab{i}"]
                need(dve, "sig_b", i + 1)
                pair_ready(dve, p)
                pair_used_wait(dve, V.tensor_tensor(ypad[:, 2 * i:2 * i + 2, 15:15 + S], blocks(pair_ps(p), 2), sgb, ALU.mult), p)
                signal(dve, "glu", 1)
                for tap in range(CV_TAPS):
                    for b in (2 * i, 2 * i + 1):
                        w = col("cv_dw", 8 * tap + b)
                        x = ypad[:, b, tap:tap + S]
                        if tap == 0:
                            last = post(V.tensor_scalar(yc[:, b], x, w, col("cv_db", b), ALU.mult, ALU.add), "tap")
                        else:
                            need(dve, "tap", last - 1)
                            last = post(V.scalar_tensor_tensor(out=yc[:, b], in0=x, scalar=w, in1=yc[:, b],
                                                               op0=ALU.mult, op1=ALU.add), "tap")
                need(dve, "tap", last)
                signal(dve, "conv_out", 2)
            need(dve, "mean_sb")
            go(V.tensor_tensor(yc, yc, rms[:].broadcast_to([P, KB, S]), ALU.subtract), "centred")
            need(dve, "root", 7)
            go(V.reciprocal(rinv[:, 0], rms[:, 0]), "rinv")
            for k in range(KB):
                post(V.tensor_tensor(ycn[:, k], yc[:, k], rinv[:, 0], ALU.mult), "standard")
            need(dve, "gT", 4)
            for k in range(KB):
                need(dve, "ln_silu", k + 1)
                post(V.tensor_tensor(ycn[:, k], ycn[:, k], gT[:, k], ALU.mult), "cv_y")

            def gated_residual(unit0, src, dst, layer, name):
                for i in range(4):
                    p = FIRST_PAIR[unit0] + i
                    pair_ready(dve, p)
                    for j in range(2):
                        k = 2 * i + j
                        ins = V.scalar_tensor_tensor(out=dst[:, k], in0=pair_ps(p)[:, j * S:(j + 1) * S],
                                                     scalar=modc[:, 24 * layer + 16 + k:24 * layer + 17 + k], in1=src[:, k],
                                                     op0=ALU.mult, op1=ALU.add)
                        if j == 0:
                            go(ins)
                        else:
                            pair_used_wait(dve, ins, p)
                    signal(dve, name, 2)

            gated_residual("cv_out0", hB, hA, 0, "h4")
            go(V.memset(vpad[:, :, 0:8], 0.0))
            go(V.memset(vpad[:, :, 8 + S:], 0.0), "vpads")
            norm_mod(8, hA, 1)
            for g in range(4):
                w = 2 << g
                need(dve, "vpad", g + 1)
                src, n = vpad[:, 2 * g:2 * g + 2, :], 272
                for i in range(g + 1):
                    step = 1 << i
                    n -= step
                    go(V.tensor_tensor(win[i][:, :, 0:n], src[:, :, 0:n], src[:, :, step:step + n], ALU.add))
                    src = win[i]
                first = 8 - w // 2
                inv = cst("count_inv")[:, g * S:(g + 1) * S].unsqueeze(1).broadcast_to([P, 2, S])
                o = pooled[:, 2 * g:2 * g + 2, :]
                go(V.tensor_tensor(o, src[:, :, first:first + S], inv, ALU.mult))
                go(V.tensor_tensor(o, o, vpad[:, 2 * g:2 * g + 2, 8:8 + S], ALU.subtract), "pooled")
            for g in range(4):
                p = FIRST_PAIR["grp"] + g
                need(dve, "gT", 4 + 4)
                pair_ready(dve, p)
                for j in range(2):
                    k = 2 * g + j
                    ins = V.scalar_tensor_tensor(out=ycn[:, k], in0=pair_ps(p)[:, j * S:(j + 1) * S], scalar=col("pl_scale", k),
                                                 in1=gT[:, k], op0=ALU.mult, op1=ALU.mult)
                    if j == 0:
                        go(ins)
                    else:
                        pair_used_wait(dve, ins, p)
                signal(dve, "pl_y", 2)
            gated_residual("pl_out0", hA, hB, 1, "result")


def kernel(**inputs):
    import numpy as np
    import concourse.bacc as bacc
    from concourse.bass_utils import run_bass_kernel_spmd

    a = {n: np.asarray(v) for n, v in inputs.items()}
    f4 = np.float32

    def colmajor(v):
        return np.ascontiguousarray(v.reshape(-1, P).T)

    def to_blocks(x):
        return np.ascontiguousarray(x.T.reshape(-1, P, x.shape[0]).transpose(1, 0, 2))

    def unit(w, c=None):
        return w.reshape(KB, P, 512).transpose(1, 0, 2).reshape(P, KB * 512)

    w_in = a["w_in"][0]
    g = {n: w_in[:, 512 * i:512 * (i + 1)] for i, n in enumerate(("b", "c", "h", "q", "k", "v", "z"))}
    kv, cv, pv = a["w_xkv"][0], a["cv_w_in_2"][0], a["pl_w_in_2"][0]
    for i in range(2):
        s = slice(512 * i, 512 * (i + 1))
        g[f"mem_k{i}"], g[f"mem_v{i}"] = kv[:, s], kv[:, 1024 + 512 * i:1536 + 512 * i]
        g[f"mix_out{i}"], g[f"xq{i}"], g[f"xo{i}"], g[f"pq{i}"] = (a[n][0][:, s] for n in ("w_out", "w_xq", "w_xo", "w_pq"))
        g[f"cv_g{i}"], g[f"cv_out{i}"], g[f"pl_out{i}"] = cv[:, 2048 + 512 * i:2560 + 512 * i], a["cv_w_out_2"][0][:, s], a["pl_w_out_2"][0][:, s]
        g[f"pl_v{i}"], g[f"pl_g{i}"] = pv[:, s], pv[:, 1024 + 512 * i:1536 + 512 * i]
    for i in range(4):
        g[f"cv_ab{i}"] = np.concatenate([cv[:, 256 * i:256 * (i + 1)], cv[:, 1024 + 256 * i:1280 + 256 * i]], axis=1)
    units = np.stack([unit(g[u]) for u in UNITS if u != "grp"])
    grp = np.ascontiguousarray(a["pl_w_grp_2"][0].reshape(4, 2, P, 256).transpose(2, 0, 1, 3).reshape(P, 2048))
    mod = np.ascontiguousarray(a["w_mod_2"].reshape(2, KB, P, 12, 256).transpose(0, 3, 2, 1, 4).reshape(MOD_CHUNKS, P, KB * 256))

    parts = {"norm_mix": a["norm_mix"], "norm_x": a["norm_x"], "norm_mem": a["norm_mem"], "norm_ffn": a["norm_ffn"],
             "norm_final": a["norm_final"], "norm_g0": a["norm_g_2"][0], "norm_g1": a["norm_g_2"][1],
             "conv_w": a["conv_w"], "dn_conv_w": a["dn_conv_w"], "dn_norm": a["dn_norm"], "cv_dw": a["cv_dw_2"],
             "cv_db": a["cv_db_2"], "ln_g": a["cv_ln_g_2"], "ln_b": a["cv_ln_b_2"], "pl_scale": a["pl_scale_2"],
             "b_mod": a["b_mod_2"], "c": a["c_2"]}
    cols = np.concatenate([colmajor(parts[n]) if n in parts else
                           np.broadcast_to(a["dn_a_log" if n == "a_log" else "dn_dt_bias"][0], (P, NH)) for n in COLS], axis=1)

    i, j = np.indices((P, P))
    same = i // CHUNK == j // CHUNK
    const = np.zeros((P, NCONST), f4)

    def put(name, v):
        const[:, CONST[name][0]:CONST[name][0] + CONST[name][1]] = v

    put("ident", i == j)
    put("ones", 1)
    put("upto", same & (i <= j))
    put("whole", same)
    put("causal", same & (i >= j))
    put("strict16", (i // 16 == j // 16) & (i > j))
    put("off32", (i // 32 == j // 32) & (i // 16 > j // 16))
    put("off64", same & (i // 32 > j // 32))
    t = np.arange(S)
    put("count_inv", np.concatenate([1.0 / (np.clip(t + w - w // 2, 0, S) - np.clip(t - w // 2, 0, S)) for w in (2, 4, 8, 16)]))
    put("iota16", np.arange(16))
    put("eps", EPS)
    put("one", 1)

    arrays = {
        "x_t": to_blocks(a["x"][0]), "mem_t": to_blocks(a["mem"][0]),
        "cols": np.ascontiguousarray(cols), "const": const,
        "small": np.ascontiguousarray(w_in[:, 3584:3592].reshape(KB, P, 8).transpose(1, 0, 2)),
        "keys": np.ascontiguousarray(a["peer_keys"][0].transpose(1, 3, 0, 2).reshape(P, PH, KEYS)),
        "units": units, "grp": grp, "mod": mod,
        "uv": np.concatenate([a["expert_u"][0], a["expert_v"][0]], axis=1),
    }
    nc = bacc.Bacc("TRN2", target_bir_lowering=False, num_devices=1)
    args = [nc.dram_tensor(f"{n}_dram", v.shape, mybir.dt.from_np(v.dtype), kind="ExternalInput").ap() for n, v in arrays.items()]
    out = nc.dram_tensor("out", (P, KB, S), F32, kind="ExternalOutput").ap()
    build(nc, *args, out)
    r = run_bass_kernel_spmd(nc, [{f"{n}_dram": v for n, v in arrays.items()}], core_ids=[0])
    o = r.results[0]["out"]
    return np.ascontiguousarray(o.transpose(2, 1, 0).reshape(1, S, D))
```

```python
from contextlib import ExitStack

import concourse.bass as bass
from concourse import mybir

F32 = mybir.dt.float32
U32 = mybir.dt.uint32
ALU = mybir.AluOpType
ACT = mybir.ActivationFunctionType
AX_X = mybir.AxisListType.X

P = 128
D = 1024
S = 256
KB = D // P
TT = S // P
CHUNK = 64
NH = 4
PH, TOPK, KEYS = 8, 16, 128
TAPS, DN_TAPS, CV_TAPS = 3, 4, 31
EPS = 1e-6
LOWEST = -3.0e38

COLS = {}
_n = 0
for _name, _w in (("norm_mix", 8), ("norm_x", 8), ("norm_mem", 8), ("norm_ffn", 8), ("norm_final", 8),
                  ("norm_g0", 8), ("norm_g1", 8), ("conv_w", TAPS * 4), ("dn_conv_w", DN_TAPS * 12),
                  ("dn_norm", 1), ("cv_dw", CV_TAPS * 8), ("cv_db", 8), ("ln_g", 8), ("ln_b", 8),
                  ("pl_scale", 8), ("b_mod", 48), ("c", 8), ("a_log", 4), ("dt_bias", 4)):
    COLS[_name] = (_n, _w)
    _n += _w
NCOLS = _n

CONST = {}
_n = 0
for _name, _w in (("ones", P), ("eps", 1), ("one", 1), ("iota16", 16), ("ident", P), ("upto", P), ("whole", P),
                  ("causal", P), ("strict16", P), ("off32", P), ("off64", P), ("count_inv", 4 * S)):
    CONST[_name] = (_n, _w)
    _n += _w
NCONST = _n
CONST_FIRST = 2 * P

UNITS = (["q", "k", "v", "b", "c", "h", "z"] + ["mem_k0", "mem_k1", "mem_v0", "mem_v1"]
         + ["mix_out0", "mix_out1", "xq0", "xq1", "xo0", "xo1", "pq0", "pq1"]
         + [f"cv_ab{i}" for i in range(4)] + ["cv_g0", "cv_g1", "cv_out0", "cv_out1"]
         + ["pl_v0", "pl_v1", "pl_g0", "pl_g1", "grp", "pl_out0", "pl_out1"])
PAIRS = {u: (4 if u == "grp" else 2) for u in UNITS}
FIRST_PAIR = {}
_n = 0
for _u in UNITS:
    FIRST_PAIR[_u] = _n
    _n += PAIRS[_u]
W_SLOTS = 3
PAIR_BANKS = 4

PRODUCTS = 4
MOD_CHUNKS = 24
MOD_SUMS = 2
MOD_AFTER = {}
_n = 0
for _i, _u in enumerate(UNITS[1:18]):
    _w = 1 if _i < 10 else 2
    MOD_AFTER[_u] = (_n, min(_n + _w, MOD_CHUNKS))
    _n += _w

TILE_BANKS = 3
TILES = (["ss_x", "ss_mem", "logits", "ss_q0", "ss_q1", "ss_k0", "ss_k1", "gcum", "gB0", "gB1"]
         + [f"{n}{t}" for n in ("ktok", "vtok", "KK", "QK") for t in range(TT)]
         + [f"{n}{t}" for n in ("NT",) for t in range(TT)]
         + [f"{n}{t}" for r in ("2", "4") for g in (("P" + r, "PT" + r), ("T" + r, "TT" + r))
            for t in range(TT) for n in (g[0] + "_", g[1] + "_")]
         + [f"P8_{t}" for t in range(TT)]
         + [f"{n}{t}" for t in range(TT) for n in ("T8_", "TT8_")]
         + [f"Y32_{t}" for t in range(TT)]
         + [f"{n}{t}" for t in range(TT) for n in ("T32_", "TT32_")]
         + [f"Y64_{t}" for t in range(TT)] + [f"TT64_{t}" for t in range(TT)]
         + [f"{n}{t}" for n in ("intraT", "u", "wT") for t in range(TT)]
         + [n + str(c) for c in range(4) for n in ((["wS"] if c else []) + ["o", "dS"])]
         + ["ss_o0", "ss_o1", "ss_h1"] + [f"att_s{h}" for h in range(NH)]
         + [f"att_p{h}" for h in range(NH)] + [f"att_o{h}" for h in range(NH)]
         + ["ss_h2"] + [f"sc{t}_{i}" for t in range(TT) for i in range(4)]
         + ["mean", "var", "ss_m1"])
TILE_NO = {n: i for i, n in enumerate(TILES)}

RING = 8
HEADS = TT * PH
AHEAD = 2
HEAD_LOOPS = [[(0, PH)]] * (TT - 1) + [[(0, PH - AHEAD), (PH - AHEAD, PH)]]
ROUTE_POSTS = 26


def build(nc, x_t, mem_t, cols_d, const_d, small_d, keys_d, units_d, grp_d, mod_d, uv_d, out_d, dbg=None):
    with ExitStack() as ctx:
        def sb(name, shape, dt=F32):
            return ctx.enter_context(nc.sbuf_tensor(name, shape, dt))

        sems = {}

        def sem(name):
            if name not in sems:
                sems[name] = ctx.enter_context(nc.semaphore(name))
            return sems[name]

        hA = sb("hA", [P, KB, S])
        hB = sb("hB", [P, KB, S])
        xn = sb("xn", [P, KB, S])
        sq = sb("sq", [P, KB, S])
        wring = sb("wring", [P, W_SLOTS, KB, 512])
        cols = sb("cols", [P, NCOLS])
        const = sb("const", [P, NCONST])
        small_w = sb("small_w", [P, KB, 8])
        modc = sb("modc", [P, 48])
        gmod = sb("gmod", [P, 2, KB])
        mod_p = sb("mod_p", [P, MOD_SUMS, 256])
        silu_c = sb("silu_c", [P, KB])
        rms = sb("rms", [P, 1, S])
        rinv = sb("rinv", [P, 1, S])
        gl = sb("gl", [P, 4, NH])
        tiny = sb("tiny", [P, 16, TT, NH])
        arena = sb("arena", [P, 28 * 1024])
        ps = ctx.enter_context(nc.psum_tensor("ps", [P, 8, 512], F32))

        def col(name, i=0, n=1):
            return cols[:, COLS[name][0] + i:COLS[name][0] + i + n]

        def cst(name):
            return const[:, CONST[name][0]:CONST[name][0] + CONST[name][1]]

        ident, ones = cst("ident"), cst("ones")

        def slab(i, width=1024):
            return arena[:, i * 1024:i * 1024 + width]

        def blocks(ap, b):
            return ap.rearrange("p (b t) -> p b t", b=b)

        def heads(ap):
            return ap.rearrange("p (t h j) -> p t h j", t=TT, h=NH)

        mod_w = slab(0, 4096).rearrange("p (s k n) -> p s k n", s=2, k=KB)
        mem_kT = blocks(slab(4, 2048), KB)
        mem_v = slab(6, 2048).rearrange("p (m n) -> p m n", m=TT)
        qkv = blocks(slab(8, 3072), 12)
        zT = blocks(slab(11), 4)
        yT = blocks(slab(12, 2048), KB)
        S_st = slab(14, 512).rearrange("p (h e) -> p h e", h=NH)
        kbe, kdec, vbeta, qdec = (heads(slab(15 + i)) for i in range(4))
        E, N_, NT, T_, T_T, off32, off64, intra, Y = (heads(slab(19 + i)) for i in range(9))
        intraT, u_tok, wT, v_new, oT = E, N_, NT, T_, blocks(slab(26), 4)
        qkv_pad = slab(19, 12 * 259).rearrange("p (b t) -> p b t", b=12)
        bT, cT = blocks(slab(4), 4), blocks(slab(5), 4)
        hc_pad = slab(6, 4 * 258).rearrange("p (b t) -> p b t", b=4)
        xg = blocks(slab(12, 2048), KB)
        norm2 = slab(15, 2048)
        egB = heads(slab(27))
        aq = blocks(slab(8, 2048), KB)
        prob = slab(10, 2048).rearrange("p (h t m) -> p h t m", h=NH, t=TT)
        probT = slab(12, 2048).rearrange("p (h m t) -> p h m t", h=NH, m=TT)
        ao = blocks(slab(14, 2048), KB)
        keys = slab(27).rearrange("p (h n) -> p h n", h=PH)
        pq = blocks(slab(16, 2048), KB)
        ring = [slab(2 * i, 2048) for i in range(RING)]
        score = [slab(18 + 2 * t, 2048) for t in range(TT)]
        all_scores = slab(18, 4096)
        ysb = [slab(16), slab(17)]
        diag = slab(26, 2048).rearrange("p (j t) -> p j t", j=TOPK)
        sq_h = blocks(slab(22, 2048), KB)
        sq_g = blocks(slab(24, 2048), KB)
        spare = sq[:].rearrange("p k t -> p (k t)")
        halves = spare[:, 0:256].rearrange("p (s n) -> p s n", s=2)
        cand = spare[:, 256:512]
        scr = spare[:, 512:768]
        hot = spare[:, 0:512].rearrange("p (s j a) -> p s j a", s=2, j=TOPK)

        def small(i, dt=None):
            ap = spare[:, 1280 + 32 * i:1312 + 32 * i]
            return (ap.bitcast(dt) if dt else ap).rearrange("p (s k) -> p s k", s=2)

        topv, topi, topf, pab, pabf, picked = small(0), small(1, U32), small(2), small(3, U32), small(4), small(5)
        best, posn, gate_now = small(6)[:, 0], small(7, U32)[:, 0], small(8)[:, 0]
        gexp, gsum = small(9)[:, 0], small(10)[:, 0, 0:1]
        idx = spare[:, 768:768 + HEADS * TOPK].bitcast(U32)
        gate = spare[:, 1664:1664 + HEADS * TOPK]
        idx_now = sb("idx_now", [P, 2, RING], U32)
        act16 = sb("act16", [P, TOPK])
        gel16 = sb("gel16", [P, TOPK])
        ypad = slab(0, 8 * 286).rearrange("p (b t) -> p b t", b=KB)
        sgb = blocks(slab(3, 512), 2)
        products = [blocks(slab(10, 2048)[:, 512 * i:512 * (i + 1)], 2) for i in range(PRODUCTS)]
        yc = blocks(slab(4, 2048), KB)
        gT = blocks(slab(6, 2048), KB)
        ycn = blocks(slab(8, 2048), KB)
        vpad = slab(10, 8 * 272).rearrange("p (b t) -> p b t", b=KB)
        win = [slab(13 + i, 544).rearrange("p (b t) -> p b t", b=2) for i in range(4)]
        pooled = blocks(slab(17, 2048), KB)

        counts = {}

        def post(ins, name):
            counts[name] = counts.get(name, 0) + 1
            ins.then_inc(sem(name), 1)
            return counts[name]

        def signal(eng, name, n=1):
            counts[name] = counts.get(name, 0) + n
            eng.sem_inc(sem(name), n)

        def did(eng, ins, name):
            n = post(ins, name)
            eng.wait_ge(sem(name), n)
            return n

        def need(eng, name, n=1):
            eng.wait_ge(sem(name), n)

        def tile_bank(name):
            return 4 + TILE_NO[name] % TILE_BANKS

        def tile_ps(name):
            return ps[:, tile_bank(name), :]

        def tile_ready(eng, name):
            eng.wait_ge(sem("tiles"), TILE_NO[name] + 1)

        def tile_used(ins, name):
            ins.then_inc(sem(f"tile_free{tile_bank(name)}"), 1)

        def tile_used_wait(eng, ins, name):
            tile_used(ins, name)
            eng.wait_ge(sem(f"tile_free{tile_bank(name)}"), TILE_NO[name] // TILE_BANKS + 1)

        def pair_ps(p):
            return ps[:, p % PAIR_BANKS, :]

        def pair_ready(eng, p):
            eng.wait_ge(sem("pairs"), p + 1)

        def pair_used(ins, p):
            ins.then_inc(sem(f"pair_free{p % PAIR_BANKS}"), 1)

        def pair_used_wait(eng, ins, p):
            pair_used(ins, p)
            eng.wait_ge(sem(f"pair_free{p % PAIR_BANKS}"), p // PAIR_BANKS + 1)

        block = ctx.enter_context(nc.Block())

        @block.sync
        def _(sp):
            sp.dma_start(hA[:], x_t).then_inc(sem("x_in"), 16)
            for n, u in enumerate(UNITS):
                slot = n % W_SLOTS
                if n >= W_SLOTS:
                    before = UNITS[n - W_SLOTS]
                    sp.wait_ge(sem("pairs"), FIRST_PAIR[before] + PAIRS[before])
                if u == "grp":
                    sp.dma_start(wring[:, slot, 0:4, :].rearrange("p k n -> p (k n)"), grp_d).then_inc(sem(f"w_in{slot}"), 16)
                else:
                    sp.dma_start(wring[:, slot].rearrange("p k n -> p (k n)"),
                                 units_d[n if n < UNITS.index("grp") else n - 1]).then_inc(sem(f"w_in{slot}"), 16)
            for i in range(4):
                need(sp, "result", 2 * (i + 1))
                sp.dma_start(out_d[:, 2 * i:2 * i + 2], hB[:, 2 * i:2 * i + 2]).then_inc(sem("stored"), 16)
            sp.wait_ge(sem("stored"), 4 * 16)

        @block.gpsimd
        def _(pool):
            for i in range(2):
                pool.dma_start(mod_w[:, i].rearrange("p k n -> p (k n)"), mod_d[i]).then_inc(sem(f"mod_in{i}"), 16)
            need(pool, "silu_c")
            for i in range(MOD_CHUNKS):
                w = mod_w[:, i % 2]
                pool.wait_ge(sem(f"mod_in{i % 2}"), 16 * (i // 2 + 1))
                did(pool, pool.tensor_tensor(w, w, silu_c[:].unsqueeze(2).broadcast_to([P, KB, 256]), ALU.mult), "pool_step")
                did(pool, pool.tensor_tensor(w[:, 0:4], w[:, 0:4], w[:, 4:8], ALU.add), "pool_step")
                did(pool, pool.tensor_tensor(w[:, 0:2], w[:, 0:2], w[:, 2:4], ALU.add), "pool_step")
                if i >= MOD_SUMS:
                    need(pool, "mod_sum", i - MOD_SUMS + 1)
                did(pool, pool.tensor_tensor(mod_p[:, i % MOD_SUMS], w[:, 0], w[:, 1], ALU.add), "mod_part")
                if i + 2 < MOD_CHUNKS:
                    pool.dma_start(w.rearrange("p k n -> p (k n)"), mod_d[i + 2]).then_inc(sem(f"mod_in{i % 2}"), 16)
            for b in range(RING):
                pool.sem_inc(sem(f"row_free{b}"), 1)
            with pool.Fori(0, HEADS) as h:
                pool.wait_ge(sem("routed"), h + 1)
                for half in range(TOPK // RING):
                    pool.tensor_copy(idx_now[:, half, :],
                                     idx[:, bass.ds(h * TOPK + half * RING, RING)]).then_inc(sem("idx_now"), 1)
                    for b in range(RING):
                        if b == 0:
                            pool.wait_ge(sem("idx_now"), 2 * h + half + 1)
                        pool.wait_ge(sem(f"row_free{b}"), 2 * h + half + 1)
                        pool.sem_inc(sem("row_turn"), 1)
                        pool.indirect_dma_start(
                            ring[b], None, uv_d,
                            bass.IndirectOffsetOnAxis(ap=idx_now[:, half, b:b + 1], axis=0)
                        ).then_inc(sem(f"row_in{b}"), 16)
            acc = yc[:, 2:4, :]
            for tap in range(1, CV_TAPS):
                if tap > 1:
                    need(pool, "conv_sum", tap - 1)
                need(pool, "product", tap + 1)
                post(pool.tensor_tensor(acc, products[0] if tap == 1 else acc, products[tap % PRODUCTS], ALU.add), "conv_sum")
            need(pool, "conv_sum", CV_TAPS - 1)
            signal(pool, "conv_out1")

        @block.tensor
        def _(pe):
            def tile_begin(name):
                n = TILE_NO[name]
                if n >= TILE_BANKS:
                    pe.wait_ge(sem(f"tile_free{tile_bank(name)}"), n // TILE_BANKS)
                return tile_ps(name)

            def sum_channels(name, src, nblk, ready=None):
                out = tile_begin(name)
                for k in range(nblk):
                    if ready and k % 2 == 0:
                        ready(k // 2)
                    mm = pe.matmul(out[:, 0:S], lhsT=ones, rhs=src[:, k, :], start=(k == 0), stop=(k == nblk - 1))
                post(mm, "tiles")

            def squared(n):
                return lambda i: need(pe, "squares", 4 * n + i + 1)

            def unit(u, rhs, ready=None, tokens_out=False, between=None):
                n = UNITS.index(u)
                w = wring[:, n % W_SLOTS]
                pe.wait_ge(sem(f"w_in{n % W_SLOTS}"), 16 * (n // W_SLOTS + 1))
                for i in range(2):
                    if i and between:
                        between()
                    p = FIRST_PAIR[u] + i
                    if p >= PAIR_BANKS:
                        pe.wait_ge(sem(f"pair_free{p % PAIR_BANKS}"), p // PAIR_BANKS)
                    out = pair_ps(p)
                    if tokens_out:
                        for k in range(KB):
                            mm = pe.matmul(out, lhsT=rhs[:, k, i * P:(i + 1) * P], rhs=w[:, k, :],
                                           start=(k == 0), stop=(k == KB - 1))
                    else:
                        for j in range(2):
                            for k in range(KB):
                                if ready and i == 0 and j == 0:
                                    ready(k)
                                mm = pe.matmul(out[:, j * S:(j + 1) * S], lhsT=w[:, k, (2 * i + j) * P:(2 * i + j + 1) * P],
                                               rhs=rhs[:, k, :], start=(k == 0), stop=(k == KB - 1))
                    post(mm, "pairs")
                for i in range(*MOD_AFTER.get(u, (0, 0))):
                    mod_chunk(i)

            def mod_chunk(i):
                need(pe, "mod_part", i + 1)
                for j in range(2):
                    mm = pe.matmul(ps[:, 7, 2 * i + j:2 * i + j + 1], lhsT=mod_p[:, i % MOD_SUMS, j * P:(j + 1) * P], rhs=cst("one"),
                                   start=True, stop=True)
                post(mm, "mod_sum")

            def four(name, lhs, rhs, transpose=False):
                out = tile_begin(name)
                for h in range(NH):
                    o = out[:, h * P:(h + 1) * P]
                    if transpose:
                        mm = pe.transpose(o, lhs(h), ident)
                    else:
                        mm = pe.matmul(o, lhsT=lhs(h), rhs=rhs(h), start=True, stop=True)
                post(mm, "tiles")

            pe.wait_ge(sem("const_in"), 16)
            sum_channels("ss_x", sq, KB, ready=squared(0))
            unit("q", xg, ready=lambda k: need(pe, "xg", k + 1))
            sum_channels("ss_mem", sq, KB, ready=squared(1))
            need(pe, "xn", KB)
            pe.wait_ge(sem("small_in"), 16)
            out = tile_begin("logits")
            for t in range(TT):
                for k in range(KB):
                    mm = pe.matmul(out[:, t * 8:(t + 1) * 8], lhsT=xn[:, k, t * P:(t + 1) * P], rhs=small_w[:, k, :],
                                   start=(k == 0), stop=(k == KB - 1))
            post(mm, "tiles")
            unit("k", xn)
            unit("v", xn)
            unit("b", xn)
            for i, n in enumerate(("ss_q0", "ss_q1", "ss_k0", "ss_k1")):
                need(pe, "qk_squares", i // 2 + 1)
                out = tile_begin(n)
                post(pe.matmul(out, lhsT=ones, rhs=norm2[:, 512 * (i % 2) + 1024 * (i // 2):][:, 0:512],
                               start=True, stop=True), "tiles")
            unit("c", xn)
            pe.wait_ge(sem("const2_in"), 16)
            need(pe, "g")
            out = tile_begin("gcum")
            g = tiny[:, 8].rearrange("p t h -> p (t h)")
            pe.matmul(out[:, 0:8], lhsT=cst("upto"), rhs=g, start=True, stop=True)
            post(pe.matmul(out[:, 8:16], lhsT=cst("whole"), rhs=g, start=True, stop=True), "tiles")
            for t in range(TT):
                four(f"gB{t}", lambda h: tiny[:, 8, t, h:h + 1].broadcast_to([P, P]), lambda h: cst("upto"))
            def seg(i, h, t):
                return qkv[:, 4 * i + h, t * P:(t + 1) * P]
            need(pe, "k_normed")
            for t in range(TT):
                four(f"ktok{t}", lambda h: seg(1, h, t), None, transpose=True)
            for t in range(TT):
                four(f"vtok{t}", lambda h: seg(2, h, t), None, transpose=True)
            for t in range(TT):
                four(f"KK{t}", lambda h: seg(1, h, t), lambda h: seg(1, h, t))
            need(pe, "q_normed")
            for t in range(TT):
                four(f"QK{t}", lambda h: seg(0, h, t), lambda h: seg(1, h, t))
            unit("h", xn)
            unit("z", xn)
            for t in range(TT):
                need(pe, "N16", t + 1)
                four(f"NT{t}", lambda h: N_[:, t, h], None, transpose=True)
            for r in ("2", "4"):
                for t in range(TT):
                    need(pe, "P_ready", (t + 1) if r == "2" else TT + 2 * t + 2)
                    four(f"P{r}_{t}", lambda h: NT[:, t, h], lambda h: N_[:, t, h])
                    four(f"PT{r}_{t}", lambda h: N_[:, t, h], lambda h: NT[:, t, h])
                for t in range(TT):
                    need(pe, "P_ready", TT + (0 if r == "2" else 2 * TT) + 2 * t + 2)
                    need(pe, "T_ready", (2 * t + 2) + (0 if r == "2" else 2 * TT))
                    four(f"T{r}_{t}", lambda h: T_T[:, t, h], lambda h: N_[:, t, h])
                    four(f"TT{r}_{t}", lambda h: N_[:, t, h], lambda h: T_T[:, t, h])
            unit("mem_k0", hB, ready=lambda k: need(pe, "mem_n", k + 1))
            for t in range(TT):
                four(f"P8_{t}", lambda h: NT[:, t, h], lambda h: N_[:, t, h])
            for t in range(TT):
                need(pe, "P_ready", 5 * TT + t + 1)
                need(pe, "T_ready", 4 * TT + 2 * t + 2)
                four(f"T8_{t}", lambda h: T_T[:, t, h], lambda h: N_[:, t, h])
                four(f"TT8_{t}", lambda h: N_[:, t, h], lambda h: T_T[:, t, h])
            for t in range(TT):
                need(pe, "T_ready", 6 * TT + 2 * t + 2)
                four(f"Y32_{t}", lambda h: off32[:, t, h], lambda h: T_T[:, t, h])
            for t in range(TT):
                need(pe, "Y_ready", t + 1)
                four(f"T32_{t}", lambda h: Y[:, t, h], lambda h: T_[:, t, h])
                four(f"TT32_{t}", lambda h: T_[:, t, h], lambda h: Y[:, t, h])
            unit("mem_k1", hB)
            for t in range(TT):
                need(pe, "T_ready", 8 * TT + 2 * t + 2)
                four(f"Y64_{t}", lambda h: off64[:, t, h], lambda h: T_T[:, t, h])
            for t in range(TT):
                need(pe, "Y_ready", TT + t + 1)
                four(f"TT64_{t}", lambda h: T_[:, t, h], lambda h: Y[:, t, h])
            for t in range(TT):
                need(pe, "intra", t + 1)
                four(f"intraT{t}", lambda h: intra[:, t, h], None, transpose=True)
            for t in range(TT):
                need(pe, "T_ready", 10 * TT + t + 1)
                four(f"u{t}", lambda h: T_T[:, t, h], lambda h: vbeta[:, t, h])
            for t in range(TT):
                four(f"wT{t}", lambda h: kbe[:, t, h], lambda h: T_T[:, t, h])
            unit("mem_v0", hB, tokens_out=True)
            need(pe, "delta_operands", 6)
            for c in range(4):
                t, o = c // 2, CHUNK * (c % 2)
                rows = slice(o, o + CHUNK)
                if c:
                    need(pe, "state", c)
                    out = tile_begin(f"wS{c}")
                    for h in range(NH):
                        mm = pe.matmul(out[rows, h * P:(h + 1) * P], lhsT=wT[:, t, h, rows], rhs=S_st[:, h, :],
                                       start=True, stop=True)
                    post(mm, "tiles")
                out = tile_begin(f"o{c}")
                need(pe, "v_new", c + 1)
                for h in range(NH):
                    oh = out[:, h * CHUNK:(h + 1) * CHUNK]
                    if c:
                        pe.matmul(oh, lhsT=S_st[:, h, :], rhs=qdec[:, t, h, rows], start=True, stop=False)
                    mm = pe.matmul(oh, lhsT=v_new[rows, t, h, :], rhs=intraT[rows, t, h, rows], start=(c == 0), stop=True)
                post(mm, "tiles")
                out = tile_begin(f"dS{c}")
                for h in range(NH):
                    mm = pe.matmul(out[:, h * P:(h + 1) * P], lhsT=kdec[rows, t, h, :], rhs=v_new[rows, t, h, :],
                                   start=True, stop=True)
                post(mm, "tiles")
            def delta_sums():
                need(pe, "o_squares")
                for i in range(2):
                    out = tile_begin(f"ss_o{i}")
                    post(pe.matmul(out, lhsT=ones, rhs=norm2[:, 512 * i:512 * (i + 1)], start=True, stop=True), "tiles")

            unit("mem_v1", hB, tokens_out=True, between=delta_sums)
            unit("mix_out0", yT, ready=lambda k: need(pe, "y_conv", k + 1) if k < 4 else need(pe, "y_dn", k - 3))
            unit("mix_out1", yT)
            unit("xq0", xn, ready=lambda k: need(pe, "xn", KB + k + 1),
                 between=lambda: sum_channels("ss_h1", sq, KB, ready=squared(2)))
            unit("xq1", xn)
            need(pe, "mem_kv", 8)
            for h in range(NH):
                need(pe, "aq", h + 1)
                out = tile_begin(f"att_s{h}")
                for t in range(TT):
                    for j in range(2):
                        mm = pe.matmul(out[:, t * S:(t + 1) * S], lhsT=aq[:, 2 * h + j, t * P:(t + 1) * P],
                                       rhs=mem_kT[:, 2 * h + j, :], start=(j == 0), stop=(j == 1))
                post(mm, "tiles")
            for h in range(NH):
                need(pe, "prob", TT * (h + 1))
                out = tile_begin(f"att_p{h}")
                for m in range(2):
                    for t in range(TT):
                        mm = pe.transpose(out[:, m * S + t * P:m * S + (t + 1) * P], prob[:, h, t, m * P:(m + 1) * P], ident)
                post(mm, "tiles")
            for h in range(NH):
                need(pe, "probT", h + 1)
                out = tile_begin(f"att_o{h}")
                for j in range(2):
                    for m in range(2):
                        mm = pe.matmul(out[:, j * S:(j + 1) * S], lhsT=mem_v[:, m, (2 * h + j) * P:(2 * h + j + 1) * P],
                                       rhs=probT[:, h, m, :], start=(m == 0), stop=(m == 1))
                post(mm, "tiles")
            unit("xo0", ao, ready=lambda k: need(pe, "ao", k // 2 + 1))
            unit("xo1", ao)
            unit("pq0", xn, ready=lambda k: need(pe, "xn", 2 * KB + k + 1),
                 between=lambda: sum_channels("ss_h2", sq, KB, ready=squared(3)))
            unit("pq1", xn)
            pe.wait_ge(sem("keys_in"), 16)
            for t in range(TT):
                for i in range(4):
                    half = slice(64 * (i % 2), 64 * (i % 2) + 64)
                    need(pe, "pq", 2 * (i // 2) + 2)
                    out = tile_begin(f"sc{t}_{i}")
                    for j in range(4):
                        h = 4 * (i // 2) + j
                        mm = pe.matmul(out[:, j * KEYS:(j + 1) * KEYS], lhsT=pq[half, h, t * P:(t + 1) * P],
                                       rhs=keys[half, h, :], start=True, stop=True)
                    post(mm, "tiles")
            need(pe, "scores", 8)
            need(pe, "mod_read")
            need(pe, "xn", 4 * KB)
            for t in range(TT):
                for i in range(2):
                    for j in range(4):
                        mm = pe.transpose(ps[:, 4 + 2 * t + i, j * P:(j + 1) * P], xn[:, 4 * i + j, t * P:(t + 1) * P], ident)
                    post(mm, "x_tok")
            need(pe, "pq", 4)
            need(pe, "zeros")
            for i in range(4):
                pe.matmul(ps[:, i, :], lhsT=diag[:, 0], rhs=const[:, 0:512],
                          start=True, stop=False, skip_group_check=True).then_inc(sem("acc_zero"), 1)
            for t in range(TT):
                with pe.Fori(0, PH) as h:
                    for j in range(TOPK):
                        b = j % RING
                        pe.wait_ge(sem("diag"), t * PH * TOPK + h * TOPK + j + 1)
                        for n in range(2):
                            mm = pe.matmul(ps[:, 2 * t + n, :], lhsT=diag[:, j], rhs=ring[b][:, D + 512 * n:D + 512 * (n + 1)],
                                           start=False, stop=False, skip_group_check=True)
                        mm.then_inc(sem(f"row_free{b}"), 1)
                need(pe, "y_tok", t + 1)
                for i in range(2):
                    for j in range(4):
                        mm = pe.transpose(ps[:, 4 + 2 * t + i, j * P:(j + 1) * P],
                                          ysb[t][:, (4 * i + j) * P:(4 * i + j + 1) * P], ident)
                    post(mm, "y_back")
                need(pe, "h3_squares", t + 1)
                for i, src in enumerate((sq_h, sq_g)):
                    for k in range(KB):
                        mm = pe.matmul(ps[:, 4, (2 * i + t) * P:(2 * i + t + 1) * P], lhsT=ones, rhs=src[:, k, t * P:(t + 1) * P],
                                       start=(k == 0), stop=(k == KB - 1))
                post(mm, "h3_sums")
            for i in range(4):
                unit(f"cv_ab{i}", xn, ready=(lambda k: need(pe, "xn", 4 * KB + k + 1)) if i == 0 else None)
            unit("cv_g0", xn)
            unit("cv_g1", xn, between=lambda: sum_channels("mean", yc, KB, ready=lambda i: need(pe, f"conv_out{i}")))
            sum_channels("var", sq, KB, ready=squared(4))
            unit("cv_out0", ycn, ready=lambda k: need(pe, "cv_y", k + 1))
            unit("cv_out1", ycn)
            sum_channels("ss_m1", sq, KB, ready=squared(5))
            unit("pl_v0", xn, ready=lambda k: need(pe, "xn", 5 * KB + k + 1))
            for n in ("pl_v1", "pl_g0", "pl_g1"):
                unit(n, xn)
            n = UNITS.index("grp")
            wg = wring[:, n % W_SLOTS].rearrange("p k n -> p (k n)")[:, 0:2048].rearrange("p (k n) -> p k n", k=8)
            pe.wait_ge(sem(f"w_in{n % W_SLOTS}"), 16 * (n // W_SLOTS + 1))
            for g in range(4):
                p = FIRST_PAIR["grp"] + g
                pe.wait_ge(sem(f"pair_free{p % PAIR_BANKS}"), p // PAIR_BANKS)
                need(pe, "pooled", g + 1)
                for j in range(2):
                    for k in range(2):
                        mm = pe.matmul(pair_ps(p)[:, j * S:(j + 1) * S], lhsT=wg[:, 2 * g + k, j * P:(j + 1) * P],
                                       rhs=pooled[:, 2 * g + k, :], start=(k == 0), stop=(k == 1))
                post(mm, "pairs")
            unit("pl_out0", ycn, ready=lambda k: need(pe, "pl_y", k + 1))
            unit("pl_out1", ycn)

        @block.scalar
        def _(act):
            def go(ins, name):
                return did(act, ins, name)

            act.dma_start(const[:, 0:CONST_FIRST], const_d[:, 0:CONST_FIRST]).then_inc(sem("const_in"), 16)
            act.dma_start(cols[:], cols_d).then_inc(sem("cols_in"), 16)
            act.dma_start(hB[:], mem_t).then_inc(sem("mem_in"), 16)
            act.dma_start(small_w[:], small_d).then_inc(sem("small_in"), 16)
            act.dma_start(const[:, CONST_FIRST:], const_d[:, CONST_FIRST:]).then_inc(sem("const2_in"), 16)

            def squares(src, ready=None):
                for i in range(4):
                    if ready:
                        ready(i)
                    last = post(act.activation(sq[:, 2 * i:2 * i + 2, :], src[:, 2 * i:2 * i + 2, :], ACT.Square), "squares")
                need(act, "squares", last)

            def root(name, out, n, scale):
                tile_ready(act, name)
                tile_used_wait(act, act.activation(out, tile_ps(name)[:, 0:n], ACT.Sqrt, bias=cst("eps"), scale=scale), name)

            act.wait_ge(sem("x_in"), 16)
            squares(hA[:])
            act.wait_ge(sem("const_in"), 16)
            root("ss_x", rms[:, 0], S, 1.0 / D)
            signal(act, "root")
            act.wait_ge(sem("mem_in"), 16)
            squares(hB[:])
            act.wait_ge(sem("cols_in"), 16)
            go(act.activation(silu_c[:], col("c", 0, KB), ACT.Silu), "silu_c")
            need(act, "rinv", 1)
            root("ss_mem", rms[:, 0], S, 1.0 / D)
            signal(act, "root")
            need(act, "pads")
            for i, u in enumerate(("k", "v")):
                for j in range(2):
                    p = FIRST_PAIR[u] + j
                    pair_ready(act, p)
                    pair_used_wait(act, act.copy(qkv_pad[:, 4 * i + 4 + 2 * j:4 * i + 6 + 2 * j, 3:3 + S],
                                                 pair_ps(p).rearrange("p (b t) -> p b t", b=2)), p)
                    signal(act, "kv_in", 1)
            for i in range(3):
                need(act, "qkv_conv", 4 * (i + 1))
                v = qkv[:, 4 * i:4 * i + 4, :]
                go(act.activation(v, v, ACT.Silu), "qkv_act")
            for i in range(2):
                go(act.activation(blocks(norm2[:, 1024 * i:1024 * (i + 1)], 4), qkv[:, 4 * i:4 * i + 4, :], ACT.Square), "qk_squares")
            for i, n in enumerate(("ss_q0", "ss_q1", "ss_k0", "ss_k1")):
                root(n, norm2[:, 512 * i:512 * (i + 1)], 512, 1.0)
                signal(act, "qk_root", 1)
            need(act, "logits")
            beta_l, z_abs = tiny[:, 1], tiny[:, 4]
            go(act.activation(tiny[:, 2], beta_l, ACT.Exp, scale=-1.0), "exp_b")
            need(act, "z_abs")
            go(act.activation(tiny[:, 5], z_abs, ACT.Exp, scale=-1.0), "exp_z")
            go(act.activation(tiny[:, 6, 0], col("a_log", 0, NH), ACT.Exp), "exp_a")
            need(act, "z_exp1")
            go(act.activation(tiny[:, 5], tiny[:, 5], ACT.Ln), "ln_z")
            for j in range(2):
                p = FIRST_PAIR["b"] + j
                pair_ready(act, p)
                pair_used_wait(act, act.copy(bT[:, 2 * j:2 * j + 2, :], blocks(pair_ps(p), 2)), p)
                signal(act, "bT", 1)
            need(act, "gcum")
            go(act.activation(tiny[:, 10], tiny[:, 9], ACT.Exp), "exp_g")
            go(act.activation(tiny[:, 12], tiny[:, 11], ACT.Exp), "exp_gd")
            for t in range(TT):
                tile_ready(act, f"gB{t}")
                go(act.activation(egB[:, t].rearrange("p h j -> p (h j)"), tile_ps(f"gB{t}"), ACT.Exp), "egB")
            for t in range(TT):
                need(act, "diff", t + 1)
                go(act.activation(E[:, t], E[:, t], ACT.Exp, scale=-1.0), "E")
            for j in range(2):
                p = FIRST_PAIR["c"] + j
                pair_ready(act, p)
                pair_used_wait(act, act.copy(cT[:, 2 * j:2 * j + 2, :], blocks(pair_ps(p), 2)), p)
                signal(act, "cT", 1)
            for j in range(2):
                p = FIRST_PAIR["z"] + j
                pair_ready(act, p)
                pair_used_wait(act, act.activation(zT[:, 2 * j:2 * j + 2, :], blocks(pair_ps(p), 2), ACT.Silu), p)
                signal(act, "zT", 1)
            def kv_copy(u, js=range(2)):
                for j in js:
                    p = FIRST_PAIR[u] + j
                    pair_ready(act, p)
                    if u[4] == "k":
                        dst, src = mem_kT[:, 4 * int(u[5]) + 2 * j:4 * int(u[5]) + 2 * j + 2, :], blocks(pair_ps(p), 2)
                    else:
                        dst, src = mem_v[:, j, 512 * int(u[5]):512 * int(u[5]) + 512], pair_ps(p)
                    pair_used_wait(act, act.copy(dst, src), p)
                    signal(act, "mem_kv", 1)
            need(act, "y_conv", 4)
            kv_copy("mem_k0")
            kv_copy("mem_k1")
            for t in range(TT):
                tile_ready(act, f"intraT{t}")
                tile_used_wait(act, act.copy(intraT[:, t].rearrange("p h j -> p (h j)"), tile_ps(f"intraT{t}")), f"intraT{t}")
                signal(act, "delta_operands", 1)
            for t in range(TT):
                tile_ready(act, f"u{t}")
                tile_used_wait(act, act.copy(u_tok[:, t].rearrange("p h j -> p (h j)"), tile_ps(f"u{t}")), f"u{t}")
                signal(act, "delta_operands", 1)
            for t in range(TT):
                tile_ready(act, f"wT{t}")
                tile_used_wait(act, act.copy(wT[:, t].rearrange("p h j -> p (h j)"), tile_ps(f"wT{t}")), f"wT{t}")
                signal(act, "delta_operands", 1)
            kv_copy("mem_v0")
            need(act, "inverted")
            for c in range(4):
                tile_ready(act, f"o{c}")
                tile_used_wait(act, act.copy(oT[:, :, c * CHUNK:(c + 1) * CHUNK],
                                             tile_ps(f"o{c}")[:, 0:NH * CHUNK].rearrange("p (h j) -> p h j", h=NH)), f"o{c}")
            need(act, "scanned")
            act.dma_start(keys, keys_d).then_inc(sem("keys_in"), 16)
            go(act.activation(blocks(norm2[:, 0:1024], 4), oT, ACT.Square), "o_squares")
            kv_copy("mem_v1", (0,))
            for i in range(2):
                root(f"ss_o{i}", norm2[:, 512 * i:512 * (i + 1)], 512, 1.0 / P)
                signal(act, "o_root", 1)
            kv_copy("mem_v1", (1,))

            def norm_act(src, name, ready, rinvs):
                squares(src, ready)
                need(act, "rinv", rinvs)
                root(name, rms[:, 0], S, 1.0 / D)
                signal(act, "root")

            norm_act(hB[:], "ss_h1", lambda i: need(act, "h1", i + 1), 2)
            for h in range(NH):
                need(act, "att_max", h + 1)
                for t in range(TT):
                    ins = act.activation(prob[:, h, t], tile_ps(f"att_s{h}")[:, t * S:(t + 1) * S], ACT.Exp,
                                         bias=tiny[:, 14, t, h:h + 1], scale=float(S) ** -0.5,
                                         accum_out=tiny[:, 15, t, h:h + 1])
                    if t == TT - 1:
                        tile_used_wait(act, ins, f"att_s{h}")
                    else:
                        go(ins, "att_exp0")
                signal(act, "att_exp", 1)
            for h in range(NH):
                tile_ready(act, f"att_p{h}")
                tile_used_wait(act, act.copy(probT[:, h].rearrange("p m t -> p (m t)"), tile_ps(f"att_p{h}")), f"att_p{h}")
                signal(act, "probT", 1)
            for h in range(NH):
                tile_ready(act, f"att_o{h}")
                tile_used_wait(act, act.copy(ao[:, 2 * h:2 * h + 2, :], blocks(tile_ps(f"att_o{h}"), 2)), f"att_o{h}")
                signal(act, "ao", 1)
            norm_act(hA[:], "ss_h2", lambda i: need(act, "h2", i + 1), 3)
            for t in range(TT):
                s4 = score[t].rearrange("p (h s n) -> p h s n", h=PH, s=2)
                for i in range(4):
                    tile_ready(act, f"sc{t}_{i}")
                    tile_used_wait(act, act.copy(s4[:, 4 * (i // 2):4 * (i // 2) + 4, i % 2, :],
                                                 tile_ps(f"sc{t}_{i}").rearrange("p (h n) -> p h n", h=4)), f"sc{t}_{i}")
                    signal(act, "scores", 1)
            def gate_exp(r):
                act.wait_ge(sem("gate_arg"), r + 1)
                act.activation(gexp, gexp, ACT.Exp, accum_out=gsum).then_inc(sem("gate_exp"), 1)

            for r in range(AHEAD):
                gate_exp(r)
            for t in range(TT):
                for first, last in HEAD_LOOPS[t]:
                    with act.Fori(first, last) as h:
                        for j in range(TOPK):
                            act.wait_ge(sem("dots"), (t * PH + h) * TOPK + j + 1)
                            act.activation(gel16[:, j:j + 1], act16[:, j:j + 1], ACT.Gelu).then_inc(sem("gelu"), 1)
                            if j == 10 and t * PH + first + AHEAD < HEADS:
                                gate_exp(t * PH + h + AHEAD)
                act.wait_ge(sem(f"row_free{RING - 1}"), (t + 1) * 2 * PH + 1)
                for n in range(2):
                    go(act.copy(ysb[t][:, 512 * n:512 * (n + 1)], ps[:, 2 * t + n, :]), "y_half")
                signal(act, "y_tok", 1)
                tok = slice(t * P, (t + 1) * P)
                for i in range(2):
                    need(act, "h2y", 2 * t + i + 1)
                    k4 = slice(4 * i, 4 * i + 4)
                    last = post(act.activation(sq_h[:, k4, tok], hA[:, k4, tok], ACT.Square), "h3_part")
                    for k in range(4 * i, 4 * i + 4):
                        last = post(act.activation(sq_g[:, k, tok], hA[:, k, tok], ACT.Square, scale=col("norm_final", k)), "h3_part")
                need(act, "h3_part", last)
                signal(act, "h3_squares", 1)
            need(act, "h3_sums", TT)
            need(act, "rinv", 4)
            go(act.activation(rms[:, 0], ps[:, 4, 0:S], ACT.Sqrt, bias=cst("eps"), scale=1.0 / D), "root")
            need(act, "h3_mean", 1)
            go(act.activation(rms[:, 0], rms[:, 0], ACT.Sqrt, bias=cst("eps"), scale=1.0 / D), "root")
            def product(tap):
                if tap >= PRODUCTS:
                    need(act, "conv_sum", max(tap - PRODUCTS, 1))
                for j in range(2):
                    w = col("cv_dw", 8 * tap + 2 + j)
                    bias = {"bias": col("cv_db", 2 + j)} if tap == 0 else {}
                    ins = act.activation(products[tap % PRODUCTS][:, j], ypad[:, 2 + j, tap:tap + S],
                                         ACT.Identity if tap == 0 else ACT.Copy, scale=w, **bias)
                    n = post(ins, "product_half")
                need(act, "product_half", n)
                signal(act, "product")

            for i in range(4):
                if i >= 2:
                    if i == 2:
                        need(act, "glu", 2)
                        need(act, "ypads")
                    for tap in range(12 * (i - 2), 12 * (i - 1)):
                        product(tap)
                p = FIRST_PAIR[f"cv_ab{i}"] + 1
                pair_ready(act, p)
                if i:
                    need(act, "glu", i)
                pair_used_wait(act, act.activation(sgb, blocks(pair_ps(p), 2), ACT.Sigmoid), p)
                signal(act, "sig_b", 1)
            for tap in range(24, CV_TAPS):
                product(tap)

            def gate_silu(i):
                p = FIRST_PAIR["cv_g0"] + i
                pair_ready(act, p)
                pair_used_wait(act, act.activation(gT[:, 2 * i:2 * i + 2, :], blocks(pair_ps(p), 2), ACT.Silu), p)
                signal(act, "gT", 1)

            for i in range(3):
                gate_silu(i)
            tile_ready(act, "mean")
            tile_used_wait(act, act.activation(rms[:, 0], tile_ps("mean")[:, 0:S], ACT.Copy, scale=1.0 / D), "mean")
            signal(act, "mean_sb", 1)
            squares(yc, lambda i: need(act, "centred", i + 1))
            gate_silu(3)
            root("var", rms[:, 0], S, 1.0 / D)
            signal(act, "root")
            for k in range(KB):
                need(act, "standard", k + 1)
                go(act.activation(ycn[:, k], ycn[:, k], ACT.Silu, bias=col("ln_b", k), scale=col("ln_g", k)), "ln_silu")
            norm_act(hA[:], "ss_m1", lambda i: need(act, "h4", 2 * (i + 1)), 7)
            for i in range(4):
                p = FIRST_PAIR["pl_v0"] + i
                pair_ready(act, p)
                pair_used_wait(act, act.copy(vpad[:, 2 * i:2 * i + 2, 8:8 + S], blocks(pair_ps(p), 2)), p)
                signal(act, "vpad", 1)
            for i in range(4):
                p = FIRST_PAIR["pl_g0"] + i
                pair_ready(act, p)
                pair_used_wait(act, act.activation(gT[:, 2 * i:2 * i + 2, :], blocks(pair_ps(p), 2), ACT.Silu), p)
                signal(act, "gT", 1)

        @block.vector
        def _(dve):
            V = nc.vector

            def go(ins, name="dve_step"):
                return did(dve, ins, name)

            def norm(n, src, dst, gain, name):
                need(dve, "root", n)
                go(V.reciprocal(rinv[:, 0], rms[:, 0]), "rinv")
                for k in range(KB):
                    last = post(V.scalar_tensor_tensor(out=dst[:, k], in0=src[:, k], scalar=col(gain, k), in1=rinv[:, 0],
                                                       op0=ALU.mult, op1=ALU.mult), name)
                need(dve, name, last)

            def norm_mod(n, src, layer):
                need(dve, "root", n)
                go(V.reciprocal(rinv[:, 0], rms[:, 0]), "rinv")
                for k in range(KB):
                    go(V.tensor_tensor(xn[:, k], src[:, k], rinv[:, 0], ALU.mult))
                    last = post(V.tensor_scalar(xn[:, k], xn[:, k], gmod[:, layer, k:k + 1],
                                                modc[:, 24 * layer + k:24 * layer + k + 1], ALU.mult, ALU.add), "xn")
                need(dve, "xn", last)

            dve.memset(qkv_pad[:, :, 0:3], 0.0)
            go(V.memset(hc_pad[:, :, 0:2], 0.0), "pads")
            dve.wait_ge(sem("cols_in"), 16)
            def gained(src, dst, gain, name, ready=None):
                for k in range(KB):
                    if ready and k % 2 == 0:
                        ready(k // 2)
                    last = post(V.tensor_scalar(dst[:, k], src[:, k], col(gain, k), None, ALU.mult), name)
                need(dve, name, last)

            def inverse_root(n):
                need(dve, "root", n)
                go(V.reciprocal(rinv[:, 0], rms[:, 0]), "rinv")

            def rooted(p, dst):
                pair_ready(dve, p)
                pair_used_wait(dve, V.tensor_tensor(dst, blocks(pair_ps(p), 2), rinv[:].broadcast_to([P, 2, S]), ALU.mult), p)

            dve.wait_ge(sem("x_in"), 16)
            gained(hA, xg, "norm_mix", "xg")
            inverse_root(1)
            for k in range(KB):
                last = post(V.tensor_tensor(xn[:, k], xg[:, k], rinv[:, 0], ALU.mult), "xn")
            need(dve, "xn", last)
            for j in range(2):
                rooted(FIRST_PAIR["q"] + j, qkv_pad[:, 2 * j:2 * j + 2, 3:3 + S])
            norm(2, hB, hB, "norm_mem", "mem_n")

            dve.wait_ge(sem("const_in"), 16)
            tile_ready(dve, "logits")
            lg = tile_ps("logits")[:, 0:16].rearrange("p (t c) -> p t c", t=TT)
            dt = col("dt_bias", 0, NH).unsqueeze(1).broadcast_to([P, TT, NH])
            go(V.tensor_copy(tiny[:, 1], lg[:, :, 0:4]), "logits")
            tile_used_wait(dve, V.tensor_tensor(tiny[:, 3], lg[:, :, 4:8], dt, ALU.add), "logits")
            go(V.scalar_tensor_tensor(out=tiny[:, 4], in0=tiny[:, 3], scalar=-1.0, in1=tiny[:, 3],
                                      op0=ALU.mult, op1=ALU.max), "z_abs")
            go(V.tensor_scalar(tiny[:, 3], tiny[:, 3], 0.0, None, ALU.max))

            for b in range(0, 12, 2):
                if b >= 4:
                    need(dve, "kv_in", b // 2 - 1)
                for i in range(DN_TAPS):
                    for k in (b, b + 1):
                        w = col("dn_conv_w", 12 * i + k)
                        x = qkv_pad[:, k, i:i + S]
                        if i == 0:
                            last = post(V.tensor_scalar(qkv[:, k], x, w, None, ALU.mult), "dn_tap")
                        else:
                            need(dve, "dn_tap", last - 1)
                            last = post(V.scalar_tensor_tensor(out=qkv[:, k], in0=x, scalar=w, in1=qkv[:, k],
                                                               op0=ALU.mult, op1=ALU.add), "dn_tap")
                need(dve, "dn_tap", last)
                signal(dve, "qkv_conv", 2)

            need(dve, "exp_b")
            go(V.tensor_scalar(tiny[:, 2], tiny[:, 2], 1.0, None, ALU.add))
            go(V.reciprocal(tiny[:, 2], tiny[:, 2]), "beta")
            need(dve, "exp_z")
            go(V.tensor_scalar(tiny[:, 5], tiny[:, 5], 1.0, None, ALU.add), "z_exp1")
            need(dve, "ln_z")
            go(V.tensor_tensor(tiny[:, 7], tiny[:, 3], tiny[:, 5], ALU.add))
            need(dve, "exp_a")
            go(V.scalar_tensor_tensor(out=tiny[:, 8], in0=tiny[:, 7], scalar=-1.0,
                                      in1=tiny[:, 6, 0].unsqueeze(1).broadcast_to([P, TT, NH]),
                                      op0=ALU.mult, op1=ALU.mult), "g")
            beta, eg, egd = tiny[:, 2], tiny[:, 10], tiny[:, 12]

            def flat(ap):
                return ap.rearrange("p t h -> p (t h)")

            for i in range(2):
                need(dve, "qk_root", 2 * (i + 1))
                r = norm2[:, 1024 * i:1024 * (i + 1)]
                go(V.reciprocal(r, r))
                x = qkv[:, 4 * i:4 * i + 4, :]
                if i == 0:
                    go(V.scalar_tensor_tensor(out=x, in0=x, scalar=float(P) ** -0.5, in1=blocks(r, 4),
                                              op0=ALU.mult, op1=ALU.mult), "q_normed")
                else:
                    go(V.tensor_tensor(x, x, blocks(r, 4), ALU.mult), "k_normed")

            tile_ready(dve, "gcum")
            go(V.tensor_copy(flat(tiny[:, 9]), tile_ps("gcum")[:, 0:8]))
            tile_used_wait(dve, V.tensor_tensor(flat(tiny[:, 11]), tile_ps("gcum")[:, 8:16], flat(tiny[:, 9]), ALU.subtract), "gcum")
            signal(dve, "gcum", 1)
            for t in range(TT):
                need(dve, "egB", t + 1)
                src = tile_ps(f"gB{t}").rearrange("p (h j) -> p h j", h=NH)
                tile_used_wait(dve, V.tensor_tensor(E[:, t], src, tiny[:, 9, t].unsqueeze(2).broadcast_to([P, NH, P]), ALU.subtract), f"gB{t}")
                go(V.tensor_scalar(E[:, t], E[:, t], 0.0, None, ALU.max), "diff")
            need(dve, "exp_g")
            go(V.tensor_tensor(tiny[:, 13], beta, eg, ALU.mult))
            need(dve, "exp_gd")

            def per_token(t, src, dst, c):
                return V.tensor_tensor(dst[:, t], src, c[:, t].unsqueeze(2).broadcast_to([P, NH, P]), ALU.mult)

            def tile_heads(name):
                return tile_ps(name).rearrange("p (h j) -> p h j", h=NH)

            need(dve, "egB", TT)
            for t in range(TT):
                go(V.tensor_tensor(qdec[:, t], qkv[:, 0:4, t * P:(t + 1) * P], egB[:, t], ALU.mult))
            for c in range(4):
                go(V.tensor_copy(gl[:, c], egB[:, c // 2, :, CHUNK * (c % 2) + CHUNK - 1]))
            for t in range(TT):
                tile_ready(dve, f"ktok{t}")
                go(per_token(t, tile_heads(f"ktok{t}"), kbe, tiny[:, 13]))
                tile_used_wait(dve, per_token(t, tile_heads(f"ktok{t}"), kdec, egd), f"ktok{t}")
            for t in range(TT):
                tile_ready(dve, f"vtok{t}")
                tile_used_wait(dve, per_token(t, tile_heads(f"vtok{t}"), vbeta, beta), f"vtok{t}")

            def mask(name):
                return cst(name).unsqueeze(1).broadcast_to([P, NH, P])

            for t in range(TT):
                need(dve, "E", t + 1)
                tile_ready(dve, f"KK{t}")
                tile_used_wait(dve, V.tensor_tensor(Y[:, t], tile_heads(f"KK{t}"), E[:, t], ALU.mult), f"KK{t}")
                go(V.tensor_tensor(Y[:, t], Y[:, t], beta[:, t].unsqueeze(2).broadcast_to([P, NH, P]), ALU.mult))
                go(V.scalar_tensor_tensor(out=N_[:, t], in0=Y[:, t], scalar=-1.0, in1=mask("strict16"),
                                          op0=ALU.mult, op1=ALU.mult), "N16")
                go(V.tensor_tensor(off32[:, t], Y[:, t], mask("off32"), ALU.mult))
                go(V.tensor_tensor(off64[:, t], Y[:, t], mask("off64"), ALU.mult))
                go(V.tensor_tensor(E[:, t], E[:, t], mask("causal"), ALU.mult))
                tile_ready(dve, f"QK{t}")
                tile_used_wait(dve, V.tensor_tensor(intra[:, t], tile_heads(f"QK{t}"), E[:, t], ALU.mult), f"QK{t}")
                signal(dve, "intra", 1)
            for j in range(2):
                p = FIRST_PAIR["h"] + j
                need(dve, "cT", j + 1)
                pair_ready(dve, p)
                pair_used_wait(dve, V.tensor_tensor(hc_pad[:, 2 * j:2 * j + 2, 2:2 + S], blocks(pair_ps(p), 2),
                                                    cT[:, 2 * j:2 * j + 2, :], ALU.mult), p)
            need(dve, "bT", 2)
            for b in range(4):
                go(V.tensor_scalar(yT[:, b], hc_pad[:, b, 0:S], col("conv_w", b), None, ALU.mult))
                for i in range(1, TAPS):
                    go(V.scalar_tensor_tensor(out=yT[:, b], in0=hc_pad[:, b, i:i + S], scalar=col("conv_w", 4 * i + b),
                                              in1=yT[:, b], op0=ALU.mult, op1=ALU.add))
                go(V.tensor_tensor(yT[:, b], yT[:, b], bT[:, b], ALU.mult), "y_conv")

            for t in range(TT):
                tile_ready(dve, f"NT{t}")
                tile_used_wait(dve, V.tensor_copy(NT[:, t], tile_heads(f"NT{t}")), f"NT{t}")
                signal(dve, "P_ready", 1)
                go(V.tensor_tensor(T_[:, t], N_[:, t], mask("ident"), ALU.add), "T_ready")
                go(V.tensor_tensor(T_T[:, t], NT[:, t], mask("ident"), ALU.add), "T_ready")

            def take(name, t, dst, ready):
                tile_ready(dve, f"{name}_{t}")
                tile_used_wait(dve, V.tensor_copy(dst[:, t], tile_heads(f"{name}_{t}")), f"{name}_{t}")
                if ready:
                    signal(dve, ready, 1)

            def accumulate(name, t, dst, op):
                tile_ready(dve, f"{name}_{t}")
                tile_used_wait(dve, V.tensor_tensor(dst[:, t], dst[:, t], tile_heads(f"{name}_{t}"), op), f"{name}_{t}")
                signal(dve, "T_ready", 1)

            for r in ("2", "4"):
                for t in range(TT):
                    tile_ready(dve, f"PT{r}_{t}")
                    take(f"P{r}", t, N_, "P_ready")
                    take(f"PT{r}", t, NT, "P_ready")
                for t in range(TT):
                    tile_ready(dve, f"TT{r}_{t}")
                    accumulate(f"T{r}", t, T_, ALU.add)
                    accumulate(f"TT{r}", t, T_T, ALU.add)
            for t in range(TT):
                take("P8", t, N_, "P_ready")
            for t in range(TT):
                tile_ready(dve, f"TT8_{t}")
                accumulate("T8", t, T_, ALU.add)
                accumulate("TT8", t, T_T, ALU.add)
            for t in range(TT):
                take("Y32", t, Y, "Y_ready")
            for t in range(TT):
                tile_ready(dve, f"TT32_{t}")
                accumulate("T32", t, T_, ALU.subtract)
                accumulate("TT32", t, T_T, ALU.subtract)
            for t in range(TT):
                take("Y64", t, Y, "Y_ready")
            for t in range(TT):
                accumulate("TT64", t, T_T, ALU.subtract)
            tile_ready(dve, f"intraT{TT - 1}")
            signal(dve, "inverted", 1)
            need(dve, "delta_operands", 6)
            for c in range(4):
                t, o = c // 2, CHUNK * (c % 2)
                rows = slice(o, o + CHUNK)
                if c:
                    tile_ready(dve, f"wS{c}")
                    tile_used_wait(dve, V.tensor_tensor(v_new[rows, t], u_tok[rows, t],
                                                        tile_heads(f"wS{c}")[rows], ALU.subtract), f"wS{c}")
                    signal(dve, "v_new", 1)
                else:
                    go(V.tensor_copy(v_new[rows, t], u_tok[rows, t]), "v_new")
                tile_ready(dve, f"dS{c}")
                if c == 0:
                    tile_used_wait(dve, V.tensor_copy(S_st, tile_heads("dS0")), "dS0")
                else:
                    go(V.tensor_tensor(S_st, S_st, gl[:, c].unsqueeze(2).broadcast_to([P, NH, P]), ALU.mult))
                    tile_used_wait(dve, V.tensor_tensor(S_st, S_st, tile_heads(f"dS{c}"), ALU.add), f"dS{c}")
                signal(dve, "state", 1)
            signal(dve, "scanned", 1)
            need(dve, "o_root", 2)
            need(dve, "zT", 2)
            go(V.reciprocal(norm2[:, 0:1024], norm2[:, 0:1024]))
            go(V.tensor_tensor(zT, zT, blocks(norm2[:, 0:1024], 4), ALU.mult))
            for h in range(NH):
                go(V.scalar_tensor_tensor(out=yT[:, 4 + h], in0=oT[:, h], scalar=col("dn_norm"), in1=zT[:, h],
                                          op0=ALU.mult, op1=ALU.mult), "y_dn")

            def residual(unit0, src, dst, name, gain):
                for i in range(4):
                    p = FIRST_PAIR[unit0] + i
                    pair_ready(dve, p)
                    pair_used_wait(dve, V.tensor_tensor(dst[:, 2 * i:2 * i + 2, :], blocks(pair_ps(p), 2),
                                                        src[:, 2 * i:2 * i + 2, :], ALU.add), p)
                    signal(dve, name, 1)
                    for k in (2 * i, 2 * i + 1):
                        last = post(V.tensor_scalar(xn[:, k], dst[:, k], col(gain, k), None, ALU.mult), "xn")
                need(dve, "xn", last)

            residual("mix_out0", hA, hB, "h1", "norm_x")
            inverse_root(3)
            for i in range(4):
                rooted(FIRST_PAIR["xq0"] + i, aq[:, 2 * i:2 * i + 2, :])
                signal(dve, "aq", 1)
            for h in range(NH):
                tile_ready(dve, f"att_s{h}")
                go(V.tensor_reduce(tiny[:, 13, :, h], tile_ps(f"att_s{h}").rearrange("p (t m) -> p t m", t=TT), AX_X, ALU.max))
                go(V.tensor_scalar(tiny[:, 14, :, h], tiny[:, 13, :, h], -float(S) ** -0.5, None, ALU.mult), "att_max")
            for h in range(NH):
                need(dve, "att_exp", h + 1)
                go(V.reciprocal(tiny[:, 15, :, h], tiny[:, 15, :, h]))
                for t in range(TT):
                    go(V.tensor_scalar(prob[:, h, t], prob[:, h, t], tiny[:, 15, t, h:h + 1], None, ALU.mult), "prob")
            residual("xo0", hB, hA, "h2", "norm_ffn")
            inverse_root(4)
            for i in range(4):
                rooted(FIRST_PAIR["pq0"] + i, pq[:, 2 * i:2 * i + 2, :])
                signal(dve, "pq", 1)
            for k in range(KB):
                last = post(V.tensor_tensor(xn[:, k], xn[:, k], rinv[:, 0], ALU.mult), "xn")
            need(dve, "xn", last)
            need(dve, "mod_sum", MOD_CHUNKS)
            go(V.tensor_tensor(modc[:], ps[:, 7, 0:48], col("b_mod", 0, 48), ALU.add), "mod_read")
            for layer in range(2):
                go(V.scalar_tensor_tensor(out=gmod[:, layer], in0=modc[:, 24 * layer + 8:24 * layer + 16], scalar=1.0,
                                          in1=col(f"norm_g{layer}", 0, KB), op0=ALU.add, op1=ALU.mult))
            go(V.memset(diag[:, 0], 0.0), "zeros")

            B4 = [P, 2, TOPK, TOPK]
            route_posts = [0]

            def route(step, r):
                def done(ins):
                    route_posts[0] += 1
                    ins.then_inc(sem("route"), 1)

                def so_far():
                    dve.wait_ge(sem("route"), r * ROUTE_POSTS + route_posts[0])
                    dve.sem_inc(sem("route_turn"), 1)

                if step == 0:
                    route_posts[0] = 0
                    done(V.tensor_copy(halves.rearrange("p s n -> p (s n)"), all_scores[:, bass.ds(r * 2 * KEYS, 2 * KEYS)]))
                elif step == 1:
                    so_far()
                    for s in range(2):
                        done(V.max(topv[:, s, 0:8], halves[:, s]))
                elif step == 2:
                    so_far()
                    for s in range(2):
                        done(V.max_index(topi[:, s, 0:8], topv[:, s, 0:8], halves[:, s]))
                        done(V.match_replace(scr[:, s * KEYS:(s + 1) * KEYS], topv[:, s, 0:8], halves[:, s], LOWEST))
                elif step == 3:
                    so_far()
                    for s in range(2):
                        done(V.max(topv[:, s, 8:16], scr[:, s * KEYS:(s + 1) * KEYS]))
                elif step == 4:
                    so_far()
                    for s in range(2):
                        done(V.max_index(topi[:, s, 8:16], topv[:, s, 8:16], scr[:, s * KEYS:(s + 1) * KEYS]))
                elif step == 5:
                    so_far()
                    done(V.tensor_copy(topf, topi))
                    done(V.tensor_tensor(cand.rearrange("p (a b) -> p a b", a=TOPK), topv[:, 0].unsqueeze(2).broadcast_to(B4[:1] + B4[2:]),
                                         topv[:, 1].unsqueeze(1).broadcast_to(B4[:1] + B4[2:]), ALU.add))
                elif step == 6:
                    so_far()
                    done(V.max(best[:, 0:8], cand))
                elif step == 7:
                    so_far()
                    done(V.max_index(posn[:, 0:8], best[:, 0:8], cand))
                    done(V.match_replace(scr, best[:, 0:8], cand, LOWEST))
                elif step == 8:
                    so_far()
                    done(V.max(best[:, 8:16], scr))
                elif step == 9:
                    so_far()
                    done(V.max_index(posn[:, 8:16], best[:, 8:16], scr))
                    V.tensor_tensor(gexp, best, best[:, 0:1].broadcast_to([P, TOPK]), ALU.subtract).then_inc(sem("gate_arg"), 1)
                elif step == 10:
                    so_far()
                    done(V.tensor_scalar(pab[:, 0], posn, 4, None, ALU.logical_shift_right))
                    done(V.tensor_scalar(pab[:, 1], posn, 15, None, ALU.bitwise_and))
                elif step == 11:
                    so_far()
                    done(V.tensor_copy(pabf, pab))
                elif step == 12:
                    so_far()
                    done(V.tensor_tensor(hot, pabf.unsqueeze(3).broadcast_to(B4),
                                         cst("iota16").unsqueeze(1).unsqueeze(1).broadcast_to(B4), ALU.is_equal))
                elif step == 13:
                    so_far()
                    done(V.tensor_tensor(hot, hot, topf.unsqueeze(2).broadcast_to(B4), ALU.mult))
                    dve.wait_ge(sem("gate_exp"), r + 1)
                    done(V.reciprocal(gsum, gsum))
                elif step == 14:
                    so_far()
                    done(V.tensor_reduce(picked, hot, AX_X, ALU.add))
                    done(V.tensor_tensor(gate[:, bass.ds(r * TOPK, TOPK)], gexp, gsum.broadcast_to([P, TOPK]), ALU.mult))
                else:
                    so_far()
                    V.scalar_tensor_tensor(out=idx[:, bass.ds(r * TOPK, TOPK)], in0=picked[:, 0],
                                           scalar=float(KEYS), in1=picked[:, 1], op0=ALU.mult, op1=ALU.add).then_inc(sem("routed"), 1)

            need(dve, "scores", 2)
            for r in range(AHEAD):
                for step in range(TOPK):
                    route(step, r)
            need(dve, "scores", 8)
            need(dve, "x_tok", 4)
            need(dve, "acc_zero", 4)

            for t in range(TT):
                x_tok = ps[:, 4 + 2 * t:6 + 2 * t, :].rearrange("p a b -> p (a b)")
                for first, last in HEAD_LOOPS[t]:
                    with dve.Fori(first, last) as h:
                        n = t * PH + h

                        def diagonal(j):
                            dve.wait_ge(sem("gelu"), n * TOPK + j + 1)
                            V.tensor_scalar(diag[:, j], ident, gel16[:, j:j + 1], gate_now[:, j:j + 1],
                                            ALU.mult, ALU.mult).then_inc(sem("diag"), 1)

                        V.tensor_copy(gate_now, gate[:, bass.ds(n * TOPK, TOPK)]).then_inc(sem("gate_now"), 1)
                        for j in range(TOPK):
                            b = j % RING
                            dve.wait_ge(sem(f"row_in{b}"), 16 * (n * 2 + j // RING + 1))
                            V.tensor_tensor_reduce(out=ring[b][:, 0:D], in0=ring[b][:, 0:D], in1=x_tok, scale=1.0, scalar=0.0,
                                                   op0=ALU.mult, op1=ALU.add, accum_out=act16[:, j:j + 1]).then_inc(sem("dots"), 1)
                            if t * PH + first + AHEAD < HEADS:
                                route(j, n + AHEAD)
                            if j == 1:
                                dve.wait_ge(sem("gate_now"), n + 1)
                            if j:
                                diagonal(j - 1)
                        diagonal(TOPK - 1)
                        dve.wait_ge(sem("diag"), (n + 1) * TOPK)
                        dve.sem_inc(sem("head_turn"), 1)
                for i in range(2):
                    need(dve, "y_back", 2 * t + i + 1)
                    src = ps[:, 4 + 2 * t + i, :].rearrange("p (k t) -> p k t", k=4)
                    h = hA[:, 4 * i:4 * i + 4, t * P:(t + 1) * P]
                    go(V.tensor_tensor(h, src, h, ALU.add), "h2y")
            inverse_root(5)
            go(V.tensor_tensor(sq[:, 0], rinv[:, 0], rinv[:, 0], ALU.mult))
            go(V.tensor_tensor(rms[:, 0], sq[:, 0], ps[:, 4, S:2 * S], ALU.mult), "h3_mean")
            for k in range(KB):
                last = post(V.scalar_tensor_tensor(out=hB[:, k], in0=hA[:, k], scalar=col("norm_final", k), in1=rinv[:, 0],
                                                   op0=ALU.mult, op1=ALU.mult), "h3")
            need(dve, "h3", last)
            norm_mod(6, hB, 0)

            def conv_taps(i):
                name = f"tap{i}"
                for tap in range(CV_TAPS):
                    for b in (2 * i, 2 * i + 1):
                        w = col("cv_dw", 8 * tap + b)
                        x = ypad[:, b, tap:tap + S]
                        if tap == 0:
                            last = post(V.tensor_scalar(yc[:, b], x, w, col("cv_db", b), ALU.mult, ALU.add), name)
                        else:
                            need(dve, name, last - 1)
                            last = post(V.scalar_tensor_tensor(out=yc[:, b], in0=x, scalar=w, in1=yc[:, b],
                                                                 op0=ALU.mult, op1=ALU.add), name)
                need(dve, name, last)
                signal(dve, f"conv_out{i}", 1)

            go(V.memset(ypad[:, :, 0:15], 0.0))
            go(V.memset(ypad[:, :, 15 + S:], 0.0), "ypads")
            for i in range(4):
                p = FIRST_PAIR[f"cv_ab{i}"]
                need(dve, "sig_b", i + 1)
                pair_ready(dve, p)
                pair_used_wait(dve, V.tensor_tensor(ypad[:, 2 * i:2 * i + 2, 15:15 + S], blocks(pair_ps(p), 2), sgb, ALU.mult), p)
                signal(dve, "glu", 1)
                if i != 1:
                    conv_taps(i)
            need(dve, "mean_sb")
            for i in range(4):
                yi = yc[:, 2 * i:2 * i + 2]
                last = post(V.tensor_tensor(yi, yi, rms[:].broadcast_to([P, 2, S]), ALU.subtract), "centred")
            need(dve, "centred", last)
            need(dve, "root", 7)
            go(V.reciprocal(rinv[:, 0], rms[:, 0]), "rinv")
            for k in range(KB):
                post(V.tensor_tensor(ycn[:, k], yc[:, k], rinv[:, 0], ALU.mult), "standard")
            need(dve, "gT", 4)
            for k in range(KB):
                need(dve, "ln_silu", k + 1)
                post(V.tensor_tensor(ycn[:, k], ycn[:, k], gT[:, k], ALU.mult), "cv_y")

            def gated_residual(unit0, src, dst, layer, name):
                for i in range(4):
                    p = FIRST_PAIR[unit0] + i
                    pair_ready(dve, p)
                    for j in range(2):
                        k = 2 * i + j
                        ins = V.scalar_tensor_tensor(out=dst[:, k], in0=pair_ps(p)[:, j * S:(j + 1) * S],
                                                     scalar=modc[:, 24 * layer + 16 + k:24 * layer + 17 + k], in1=src[:, k],
                                                     op0=ALU.mult, op1=ALU.add)
                        if j == 0:
                            go(ins)
                        else:
                            pair_used_wait(dve, ins, p)
                    signal(dve, name, 2)

            gated_residual("cv_out0", hB, hA, 0, "h4")
            go(V.memset(vpad[:, :, 0:8], 0.0))
            go(V.memset(vpad[:, :, 8 + S:], 0.0), "vpads")
            norm_mod(8, hA, 1)
            for g in range(4):
                w = 2 << g
                need(dve, "vpad", g + 1)
                src, n = vpad[:, 2 * g:2 * g + 2, :], 272
                for i in range(g + 1):
                    step = 1 << i
                    n -= step
                    go(V.tensor_tensor(win[i][:, :, 0:n], src[:, :, 0:n], src[:, :, step:step + n], ALU.add))
                    src = win[i]
                first = 8 - w // 2
                inv = cst("count_inv")[:, g * S:(g + 1) * S].unsqueeze(1).broadcast_to([P, 2, S])
                o = pooled[:, 2 * g:2 * g + 2, :]
                go(V.tensor_tensor(o, src[:, :, first:first + S], inv, ALU.mult))
                go(V.tensor_tensor(o, o, vpad[:, 2 * g:2 * g + 2, 8:8 + S], ALU.subtract), "pooled")
            for g in range(4):
                p = FIRST_PAIR["grp"] + g
                need(dve, "gT", 4 + 4)
                pair_ready(dve, p)
                for j in range(2):
                    k = 2 * g + j
                    ins = V.scalar_tensor_tensor(out=ycn[:, k], in0=pair_ps(p)[:, j * S:(j + 1) * S], scalar=col("pl_scale", k),
                                                 in1=gT[:, k], op0=ALU.mult, op1=ALU.mult)
                    if j == 0:
                        go(ins)
                    else:
                        pair_used_wait(dve, ins, p)
                signal(dve, "pl_y", 2)
            gated_residual("pl_out0", hA, hB, 1, "result")


def kernel(**inputs):
    import numpy as np
    import concourse.bacc as bacc
    from concourse.bass_utils import run_bass_kernel_spmd

    a = {n: np.asarray(v) for n, v in inputs.items()}
    f4 = np.float32

    def colmajor(v):
        return np.ascontiguousarray(v.reshape(-1, P).T)

    def to_blocks(x):
        return np.ascontiguousarray(x.T.reshape(-1, P, x.shape[0]).transpose(1, 0, 2))

    def unit(w, c=None):
        return w.reshape(KB, P, 512).transpose(1, 0, 2).reshape(P, KB * 512)

    w_in = a["w_in"][0]
    g = {n: w_in[:, 512 * i:512 * (i + 1)] for i, n in enumerate(("b", "c", "h", "q", "k", "v", "z"))}
    kv, cv, pv = a["w_xkv"][0], a["cv_w_in_2"][0], a["pl_w_in_2"][0]
    for i in range(2):
        s = slice(512 * i, 512 * (i + 1))
        g[f"mem_k{i}"], g[f"mem_v{i}"] = kv[:, s], kv[:, 1024 + 512 * i:1536 + 512 * i]
        g[f"mix_out{i}"], g[f"xq{i}"], g[f"xo{i}"], g[f"pq{i}"] = (a[n][0][:, s] for n in ("w_out", "w_xq", "w_xo", "w_pq"))
        g[f"cv_g{i}"], g[f"cv_out{i}"], g[f"pl_out{i}"] = cv[:, 2048 + 512 * i:2560 + 512 * i], a["cv_w_out_2"][0][:, s], a["pl_w_out_2"][0][:, s]
        g[f"pl_v{i}"], g[f"pl_g{i}"] = pv[:, s], pv[:, 1024 + 512 * i:1536 + 512 * i]
    for i in range(4):
        g[f"cv_ab{i}"] = np.concatenate([cv[:, 256 * i:256 * (i + 1)], cv[:, 1024 + 256 * i:1280 + 256 * i]], axis=1)
    units = np.stack([unit(g[u]) for u in UNITS if u != "grp"])
    grp = np.ascontiguousarray(a["pl_w_grp_2"][0].reshape(4, 2, P, 256).transpose(2, 0, 1, 3).reshape(P, 2048))
    mod = np.ascontiguousarray(a["w_mod_2"].reshape(2, KB, P, 12, 256).transpose(0, 3, 2, 1, 4).reshape(MOD_CHUNKS, P, KB * 256))

    parts = {"norm_mix": a["norm_mix"], "norm_x": a["norm_x"], "norm_mem": a["norm_mem"], "norm_ffn": a["norm_ffn"],
             "norm_final": a["norm_final"], "norm_g0": a["norm_g_2"][0], "norm_g1": a["norm_g_2"][1],
             "conv_w": a["conv_w"], "dn_conv_w": a["dn_conv_w"], "dn_norm": a["dn_norm"], "cv_dw": a["cv_dw_2"],
             "cv_db": a["cv_db_2"], "ln_g": a["cv_ln_g_2"], "ln_b": a["cv_ln_b_2"], "pl_scale": a["pl_scale_2"],
             "b_mod": a["b_mod_2"], "c": a["c_2"]}
    cols = np.concatenate([colmajor(parts[n]) if n in parts else
                           np.broadcast_to(a["dn_a_log" if n == "a_log" else "dn_dt_bias"][0], (P, NH)) for n in COLS], axis=1)

    i, j = np.indices((P, P))
    same = i // CHUNK == j // CHUNK
    const = np.zeros((P, NCONST), f4)

    def put(name, v):
        const[:, CONST[name][0]:CONST[name][0] + CONST[name][1]] = v

    put("ident", i == j)
    put("ones", 1)
    put("upto", same & (i <= j))
    put("whole", same)
    put("causal", same & (i >= j))
    put("strict16", (i // 16 == j // 16) & (i > j))
    put("off32", (i // 32 == j // 32) & (i // 16 > j // 16))
    put("off64", same & (i // 32 > j // 32))
    t = np.arange(S)
    put("count_inv", np.concatenate([1.0 / (np.clip(t + w - w // 2, 0, S) - np.clip(t - w // 2, 0, S)) for w in (2, 4, 8, 16)]))
    put("iota16", np.arange(16))
    put("eps", EPS)
    put("one", 1)

    arrays = {
        "x_t": to_blocks(a["x"][0]), "mem_t": to_blocks(a["mem"][0]),
        "cols": np.ascontiguousarray(cols), "const": const,
        "small": np.ascontiguousarray(w_in[:, 3584:3592].reshape(KB, P, 8).transpose(1, 0, 2)),
        "keys": np.ascontiguousarray(a["peer_keys"][0].transpose(1, 3, 0, 2).reshape(P, PH, KEYS)),
        "units": units, "grp": grp, "mod": mod,
        "uv": np.concatenate([a["expert_u"][0], a["expert_v"][0]], axis=1),
    }
    nc = bacc.Bacc("TRN2", target_bir_lowering=False, num_devices=1)
    args = [nc.dram_tensor(f"{n}_dram", v.shape, mybir.dt.from_np(v.dtype), kind="ExternalInput").ap() for n, v in arrays.items()]
    out = nc.dram_tensor("out", (P, KB, S), F32, kind="ExternalOutput").ap()
    build(nc, *args, out)
    r = run_bass_kernel_spmd(nc, [{f"{n}_dram": v for n, v in arrays.items()}], core_ids=[0])
    o = r.results[0]["out"]
    return np.ascontiguousarray(o.transpose(2, 1, 0).reshape(1, S, D))
```

```python
from contextlib import ExitStack

import concourse.bass as bass
from concourse import mybir

F32 = mybir.dt.float32
U32 = mybir.dt.uint32
ALU = mybir.AluOpType
ACT = mybir.ActivationFunctionType
AX_X = mybir.AxisListType.X

P = 128
D = 1024
S = 256
KB = D // P
TT = S // P
CHUNK = 64
NH = 4
PH, TOPK, KEYS = 8, 16, 128
TAPS, DN_TAPS, CV_TAPS = 3, 4, 31
EPS = 1e-6
LOWEST = -3.0e38

COLS = {}
_n = 0
for _name, _w in (("norm_mix", 8), ("norm_x", 8), ("norm_mem", 8), ("norm_ffn", 8), ("norm_final", 8),
                  ("norm_g0", 8), ("norm_g1", 8), ("conv_w", TAPS * 4), ("dn_conv_w", DN_TAPS * 12),
                  ("dn_norm", 1), ("cv_dw", CV_TAPS * 8), ("cv_db", 8), ("ln_g", 8), ("ln_b", 8),
                  ("pl_scale", 8), ("b_mod", 48), ("c", 8), ("a_log", 4), ("dt_bias", 4)):
    COLS[_name] = (_n, _w)
    _n += _w
NCOLS = _n

CONST = {}
_n = 0
for _name, _w in (("ones", P), ("eps", 1), ("one", 1), ("iota16", 16), ("ident", P), ("upto", P), ("whole", P),
                  ("causal", P), ("strict16", P), ("off32", P), ("off64", P), ("count_inv", 4 * S)):
    CONST[_name] = (_n, _w)
    _n += _w
NCONST = _n
CONST_FIRST = 2 * P

UNITS = (["q", "k", "v", "b", "c", "h", "z"] + ["mem_k0", "mem_k1", "mem_v0", "mem_v1"]
         + ["mix_out0", "mix_out1", "xq0", "xq1", "xo0", "xo1", "pq0", "pq1"]
         + [f"cv_ab{i}" for i in range(4)] + ["cv_g0", "cv_g1", "cv_out0", "cv_out1"]
         + ["pl_v0", "pl_v1", "pl_g0", "pl_g1", "grp", "pl_out0", "pl_out1"])
PAIRS = {u: (4 if u == "grp" else 2) for u in UNITS}
FIRST_PAIR = {}
_n = 0
for _u in UNITS:
    FIRST_PAIR[_u] = _n
    _n += PAIRS[_u]
W_SLOTS = 3
PAIR_BANKS = 4

PRODUCTS = 8
CONV_POOL = (1, 5)
CONV_DVE = (0, 2, 3, 4, 6, 7)
MOD_CHUNKS = 24
MOD_SUMS = 2
MOD_AFTER = {}
_n = 0
for _i, _u in enumerate(UNITS[1:18]):
    _w = 1 if _i < 10 else 2
    MOD_AFTER[_u] = (_n, min(_n + _w, MOD_CHUNKS))
    _n += _w

SCORE_TILES = [(0, (0, 1), 0), (0, (0, 1), 1), (0, (2, 3), 0), (0, (2, 3), 1), (0, (4, 5, 6, 7), 0), (0, (4, 5, 6, 7), 1)] + [
    (1, heads, half) for heads in ((0, 1, 2, 3), (4, 5, 6, 7)) for half in range(2)]

TILE_BANKS = 3
TILES = (["ss_x", "ss_mem", "logits", "ss_q0", "ss_q1", "ss_k0", "ss_k1", "gcum", "gB0", "gB1"]
         + [f"{n}{t}" for n in ("ktok", "vtok", "KK", "QK") for t in range(TT)]
         + [f"{n}{t}" for n in ("NT",) for t in range(TT)]
         + [f"{n}{t}" for r in ("2", "4") for g in (("P" + r, "PT" + r), ("T" + r, "TT" + r))
            for t in range(TT) for n in (g[0] + "_", g[1] + "_")]
         + [f"P8_{t}" for t in range(TT)]
         + [f"{n}{t}" for t in range(TT) for n in ("T8_", "TT8_")]
         + [f"Y32_{t}" for t in range(TT)]
         + [f"{n}{t}" for t in range(TT) for n in ("T32_", "TT32_")]
         + [f"Y64_{t}" for t in range(TT)] + [f"TT64_{t}" for t in range(TT)]
         + [f"{n}{t}" for n in ("intraT", "u", "wT") for t in range(TT)]
         + [n + str(c) for c in range(4) for n in ((["wS"] if c else []) + ["o"] + (["dS"] if c < 3 else []))]
         + ["ss_o0", "ss_o1", "ss_h1"] + [f"att_s{h}" for h in range(NH)]
         + [f"att_p{h}" for h in range(NH)] + [f"att_o{h}" for h in range(NH)]
         + ["ss_h2"] + [f"scores{i}" for i in range(len(SCORE_TILES))]
         + ["mean", "var", "ss_m1"])
TILE_NO = {n: i for i, n in enumerate(TILES)}

RING = 8
HEADS = TT * PH
AHEAD = 2
HEAD_LOOPS = [[(0, PH)]] * (TT - 1) + [[(0, PH - AHEAD), (PH - AHEAD, PH)]]
ROUTE_POSTS = 26


def build(nc, x_t, mem_t, cols_d, const_d, small_d, keys_d, units_d, grp_d, mod_d, uv_d, out_d, dbg=None):
    with ExitStack() as ctx:
        def sb(name, shape, dt=F32):
            return ctx.enter_context(nc.sbuf_tensor(name, shape, dt))

        sems = {}

        def sem(name):
            if name not in sems:
                sems[name] = ctx.enter_context(nc.semaphore(name))
            return sems[name]

        hA = sb("hA", [P, KB, S])
        hB = sb("hB", [P, KB, S])
        xn = sb("xn", [P, KB, S])
        sq = sb("sq", [P, KB, S])
        wring = sb("wring", [P, W_SLOTS, KB, 512])
        cols = sb("cols", [P, NCOLS])
        const = sb("const", [P, NCONST])
        small_w = sb("small_w", [P, KB, 8])
        modc = sb("modc", [P, 48])
        gmod = sb("gmod", [P, 2, KB])
        gain2 = sb("gain2", [P, KB])
        warm = sb("warm", [P, 1])
        gain_both = sb("gain_both", [P, KB])
        mod_p = sb("mod_p", [P, MOD_SUMS, 256])
        silu_c = sb("silu_c", [P, KB])
        rms = sb("rms", [P, 1, S])
        rinv = sb("rinv", [P, 1, S])
        gl = sb("gl", [P, 4, NH])
        tiny = sb("tiny", [P, 16, TT, NH])
        arena = sb("arena", [P, 28 * 1024])
        ps = ctx.enter_context(nc.psum_tensor("ps", [P, 8, 512], F32))

        def col(name, i=0, n=1):
            return cols[:, COLS[name][0] + i:COLS[name][0] + i + n]

        def cst(name):
            return const[:, CONST[name][0]:CONST[name][0] + CONST[name][1]]

        ident, ones = cst("ident"), cst("ones")

        def slab(i, width=1024):
            return arena[:, i * 1024:i * 1024 + width]

        def blocks(ap, b):
            return ap.rearrange("p (b t) -> p b t", b=b)

        def heads(ap):
            return ap.rearrange("p (t h j) -> p t h j", t=TT, h=NH)

        mod_w = slab(0, 4096).rearrange("p (s k n) -> p s k n", s=2, k=KB)
        mem_kT = blocks(slab(4, 2048), KB)
        mem_v = slab(6, 2048).rearrange("p (m n) -> p m n", m=TT)
        qkv = blocks(slab(8, 3072), 12)
        zT = blocks(slab(11), 4)
        yT = blocks(slab(12, 2048), KB)
        S_st = slab(14, 512).rearrange("p (h e) -> p h e", h=NH)
        kbe, kdec, vbeta, qdec = (heads(slab(15 + i)) for i in range(4))
        E, N_, NT, T_, T_T, off32, off64, intra, Y = (heads(slab(19 + i)) for i in range(9))
        intraT, u_tok, wT, v_new, oT = E, N_, NT, T_, blocks(slab(26), 4)
        qkv_pad = slab(19, 12 * 259).rearrange("p (b t) -> p b t", b=12)
        bT, cT = blocks(slab(4), 4), blocks(slab(5), 4)
        hc_pad = slab(6, 4 * 258).rearrange("p (b t) -> p b t", b=4)
        xg = blocks(slab(12, 2048), KB)
        norm2 = slab(15, 2048)
        egB = heads(slab(27))
        aq = blocks(slab(8, 2048), KB)
        prob = slab(10, 2048).rearrange("p (h t m) -> p h t m", h=NH, t=TT)
        probT = slab(12, 2048).rearrange("p (h m t) -> p h m t", h=NH, m=TT)
        ao = blocks(slab(14, 2048), KB)
        keys = slab(27).rearrange("p (h n) -> p h n", h=PH)
        pq = blocks(slab(16, 2048), KB)
        ring = [slab(2 * i, 2048) for i in range(RING)]
        score = [slab(18 + 2 * t, 2048) for t in range(TT)]
        all_scores = slab(18, 4096)
        ysb = [slab(16), slab(17)]
        diag = slab(26, 2048).rearrange("p (j t) -> p j t", j=TOPK)
        zeros = slab(24, P)
        sq_h = blocks(slab(22, 2048), KB)
        spare = sq[:].rearrange("p k t -> p (k t)")
        halves = spare[:, 0:256].rearrange("p (s n) -> p s n", s=2)
        cand = spare[:, 256:512]
        scr = spare[:, 512:768]
        hot = spare[:, 0:512].rearrange("p (s j a) -> p s j a", s=2, j=TOPK)

        def small(i, dt=None):
            ap = spare[:, 1280 + 32 * i:1312 + 32 * i]
            return (ap.bitcast(dt) if dt else ap).rearrange("p (s k) -> p s k", s=2)

        topv, topi, topf, pab, pabf, picked = small(0), small(1, U32), small(2), small(3, U32), small(4), small(5)
        best, posn, gate_now = small(6)[:, 0], small(7, U32)[:, 0], small(8)[:, 0]
        gexp, gsum = small(9)[:, 0], small(10)[:, 0, 0:1]
        idx = spare[:, 768:768 + HEADS * TOPK].bitcast(U32)
        gate = spare[:, 1664:1664 + HEADS * TOPK]
        idx_now = sb("idx_now", [P, 2, RING], U32)
        act16 = sb("act16", [P, TOPK])
        gel16 = sb("gel16", [P, TOPK])
        ypad = slab(0, 8 * 286).rearrange("p (b t) -> p b t", b=KB)
        sgb = blocks(slab(3, 512), 2)
        odd_taps = slab(19, S)
        products = [slab(10, 2048)[:, S * i:S * (i + 1)] for i in range(PRODUCTS)]
        yc = blocks(slab(4, 2048), KB)
        gT = blocks(slab(6, 2048), KB)
        ycn = blocks(slab(8, 2048), KB)
        vpad = slab(10, 8 * 272).rearrange("p (b t) -> p b t", b=KB)
        win = [slab(13 + i, 544).rearrange("p (b t) -> p b t", b=2) for i in range(4)]
        pooled = blocks(slab(17, 2048), KB)

        counts = {}

        def post(ins, name):
            counts[name] = counts.get(name, 0) + 1
            ins.then_inc(sem(name), 1)
            return counts[name]

        def signal(eng, name, n=1):
            counts[name] = counts.get(name, 0) + n
            eng.sem_inc(sem(name), n)

        def did(eng, ins, name):
            n = post(ins, name)
            eng.wait_ge(sem(name), n)
            return n

        def need(eng, name, n=1):
            eng.wait_ge(sem(name), n)

        def tile_bank(name):
            return 4 + TILE_NO[name] % TILE_BANKS

        def tile_ps(name):
            return ps[:, tile_bank(name), :]

        def tile_ready(eng, name):
            eng.wait_ge(sem("tiles"), TILE_NO[name] + 1)

        def tile_used(ins, name):
            ins.then_inc(sem(f"tile_free{tile_bank(name)}"), 1)

        def tile_used_wait(eng, ins, name):
            tile_used(ins, name)
            eng.wait_ge(sem(f"tile_free{tile_bank(name)}"), TILE_NO[name] // TILE_BANKS + 1)

        def pair_ps(p):
            return ps[:, p % PAIR_BANKS, :]

        def sum_bank(t, n):
            return (FIRST_PAIR["pq0"] + 2 * t + n) % PAIR_BANKS

        def pair_ready(eng, p):
            eng.wait_ge(sem("pairs"), p + 1)

        def pair_used(ins, p):
            ins.then_inc(sem(f"pair_free{p % PAIR_BANKS}"), 1)

        def pair_used_wait(eng, ins, p):
            pair_used(ins, p)
            eng.wait_ge(sem(f"pair_free{p % PAIR_BANKS}"), p // PAIR_BANKS + 1)

        block = ctx.enter_context(nc.Block())

        @block.sync
        def _(sp):
            sp.dma_start(hA[:], x_t).then_inc(sem("x_in"), 16)
            sp.dma_start(cols[:], cols_d).then_inc(sem("cols_in"), 16)
            for n, u in enumerate(UNITS):
                slot = n % W_SLOTS
                if u == "cv_ab1":
                    sp.wait_ge(sem(f"row_in{RING - 1}"), 16 * HEADS * TOPK // RING)
                if n >= W_SLOTS:
                    before = UNITS[n - W_SLOTS]
                    sp.wait_ge(sem("pairs"), FIRST_PAIR[before] + PAIRS[before])
                if u == "grp":
                    sp.dma_start(wring[:, slot, 0:4, :].rearrange("p k n -> p (k n)"), grp_d).then_inc(sem(f"w_in{slot}"), 16)
                else:
                    sp.dma_start(wring[:, slot].rearrange("p k n -> p (k n)"),
                                 units_d[n if n < UNITS.index("grp") else n - 1]).then_inc(sem(f"w_in{slot}"), 16)
            for i in range(4):
                need(sp, "result", 2 * (i + 1))
                sp.dma_start(out_d[:, 2 * i:2 * i + 2], hB[:, 2 * i:2 * i + 2]).then_inc(sem("stored"), 16)
            sp.wait_ge(sem("stored"), 4 * 16)

        @block.gpsimd
        def _(pool):
            pool.wait_ge(sem("w_in0"), 16)
            for i in range(2):
                pool.dma_start(mod_w[:, i].rearrange("p k n -> p (k n)"), mod_d[i]).then_inc(sem(f"mod_in{i}"), 16)
            need(pool, "silu_c")
            for i in range(MOD_CHUNKS):
                w = mod_w[:, i % 2]
                pool.wait_ge(sem(f"mod_in{i % 2}"), 16 * (i // 2 + 1))
                did(pool, pool.tensor_tensor(w, w, silu_c[:].unsqueeze(2).broadcast_to([P, KB, 256]), ALU.mult), "pool_step")
                did(pool, pool.tensor_tensor(w[:, 0:4], w[:, 0:4], w[:, 4:8], ALU.add), "pool_step")
                did(pool, pool.tensor_tensor(w[:, 0:2], w[:, 0:2], w[:, 2:4], ALU.add), "pool_step")
                if i >= MOD_SUMS:
                    need(pool, "mod_sum", i - MOD_SUMS + 1)
                did(pool, pool.tensor_tensor(mod_p[:, i % MOD_SUMS], w[:, 0], w[:, 1], ALU.add), "mod_part")
                if i + 2 < MOD_CHUNKS:
                    pool.dma_start(w.rearrange("p k n -> p (k n)"), mod_d[i + 2]).then_inc(sem(f"mod_in{i % 2}"), 16)
            for b in range(RING):
                pool.sem_inc(sem(f"row_free{b}"), 1)
            with pool.Fori(0, HEADS) as h:
                pool.wait_ge(sem("routed"), h + 1)
                for half in range(TOPK // RING):
                    pool.tensor_copy(idx_now[:, half, :],
                                     idx[:, bass.ds(h * TOPK + half * RING, RING)]).then_inc(sem("idx_now"), 1)
                    for b in range(RING):
                        if b == 0:
                            pool.wait_ge(sem("idx_now"), 2 * h + half + 1)
                        pool.wait_ge(sem(f"row_free{b}"), 2 * h + half + 1)
                        pool.sem_inc(sem("row_turn"), 1)
                        pool.indirect_dma_start(
                            ring[b], None, uv_d,
                            bass.IndirectOffsetOnAxis(ap=idx_now[:, half, b:b + 1], axis=0)
                        ).then_inc(sem(f"row_in{b}"), 16)
            for i, b in enumerate(CONV_POOL):
                for tap in range(1, CV_TAPS):
                    n = i * CV_TAPS + tap
                    if tap > 1:
                        need(pool, "conv_sum", n - i - 1)
                    need(pool, "product", n + 1)
                    post(pool.tensor_tensor(yc[:, b], products[(n - 1) % PRODUCTS] if tap == 1 else yc[:, b], products[n % PRODUCTS], ALU.add), "conv_sum")
                need(pool, "conv_sum", (i + 1) * (CV_TAPS - 1))
                signal(pool, "conv_pool")

        @block.tensor
        def _(pe):
            def tile_begin(name):
                n = TILE_NO[name]
                if n >= TILE_BANKS:
                    pe.wait_ge(sem(f"tile_free{tile_bank(name)}"), n // TILE_BANKS)
                return tile_ps(name)

            def sum_channels(name, src, nblk, ready=None):
                out = tile_begin(name)
                for k in range(nblk):
                    if ready and k % 2 == 0:
                        ready(k // 2)
                    mm = pe.matmul(out[:, 0:S], lhsT=ones, rhs=src[:, k, :], start=(k == 0), stop=(k == nblk - 1))
                post(mm, "tiles")

            def squared(n):
                return lambda i: need(pe, "squares", 4 * n + i + 1)

            def unit(u, rhs, ready=None, tokens_out=False, between=None, first_tile=None):
                n = UNITS.index(u)
                w = wring[:, n % W_SLOTS]
                pe.wait_ge(sem(f"w_in{n % W_SLOTS}"), 16 * (n // W_SLOTS + 1))
                for i in range(2):
                    if i and between:
                        between()
                    p = FIRST_PAIR[u] + i
                    if p >= PAIR_BANKS:
                        pe.wait_ge(sem(f"pair_free{p % PAIR_BANKS}"), p // PAIR_BANKS)
                    out = pair_ps(p)
                    if tokens_out:
                        for k in range(KB):
                            mm = pe.matmul(out, lhsT=rhs[:, k, i * P:(i + 1) * P], rhs=w[:, k, :],
                                           start=(k == 0), stop=(k == KB - 1))
                    elif first_tile and i == 0:
                        for t in range(TT):
                            for j in range(2):
                                for k in range(KB):
                                    if t == 0 and j == 0:
                                        ready(k)
                                    mm = pe.matmul(out[:, j * S + t * P:j * S + (t + 1) * P], lhsT=w[:, k, j * P:(j + 1) * P],
                                                   rhs=rhs[:, k, t * P:(t + 1) * P], start=(k == 0), stop=(k == KB - 1))
                            if t == 0:
                                post(mm, "pair_tile")
                                first_tile()
                    else:
                        for j in range(2):
                            for k in range(KB):
                                if ready and i == 0 and j == 0:
                                    ready(k)
                                mm = pe.matmul(out[:, j * S:(j + 1) * S], lhsT=w[:, k, (2 * i + j) * P:(2 * i + j + 1) * P],
                                               rhs=rhs[:, k, :], start=(k == 0), stop=(k == KB - 1))
                    post(mm, "pairs")
                for i in range(*MOD_AFTER.get(u, (0, 0))):
                    mod_chunk(i)

            def mod_chunk(i):
                need(pe, "mod_part", i + 1)
                for j in range(2):
                    mm = pe.matmul(ps[:, 7, 2 * i + j:2 * i + j + 1], lhsT=mod_p[:, i % MOD_SUMS, j * P:(j + 1) * P], rhs=cst("one"),
                                   start=True, stop=True)
                post(mm, "mod_sum")

            def four(name, lhs, rhs, transpose=False):
                out = tile_begin(name)
                for h in range(NH):
                    o = out[:, h * P:(h + 1) * P]
                    if transpose:
                        mm = pe.transpose(o, lhs(h), ident)
                    else:
                        mm = pe.matmul(o, lhsT=lhs(h), rhs=rhs(h), start=True, stop=True)
                post(mm, "tiles")

            pe.wait_ge(sem("const_in"), 16)
            sum_channels("ss_x", sq, KB, ready=squared(0))
            unit("q", xg, ready=lambda k: need(pe, "xg", k + 1))
            sum_channels("ss_mem", sq, KB, ready=squared(1))
            need(pe, "xn", KB)
            pe.wait_ge(sem("small_in"), 16)
            out = tile_begin("logits")
            for t in range(TT):
                for k in range(KB):
                    mm = pe.matmul(out[:, t * 8:(t + 1) * 8], lhsT=xn[:, k, t * P:(t + 1) * P], rhs=small_w[:, k, :],
                                   start=(k == 0), stop=(k == KB - 1))
            post(mm, "tiles")
            unit("k", xn)
            unit("v", xn)
            unit("b", xn)
            for i, n in enumerate(("ss_q0", "ss_q1", "ss_k0", "ss_k1")):
                need(pe, "qk_squares", i // 2 + 1)
                out = tile_begin(n)
                post(pe.matmul(out, lhsT=ones, rhs=norm2[:, 512 * (i % 2) + 1024 * (i // 2):][:, 0:512],
                               start=True, stop=True), "tiles")
            unit("c", xn)
            pe.wait_ge(sem("const2_in"), 16)
            need(pe, "g")
            out = tile_begin("gcum")
            g = tiny[:, 8].rearrange("p t h -> p (t h)")
            pe.matmul(out[:, 0:8], lhsT=cst("upto"), rhs=g, start=True, stop=True)
            post(pe.matmul(out[:, 8:16], lhsT=cst("whole"), rhs=g, start=True, stop=True), "tiles")
            for t in range(TT):
                four(f"gB{t}", lambda h: tiny[:, 8, t, h:h + 1].broadcast_to([P, P]), lambda h: cst("upto"))
            unit("h", xn)
            def seg(i, h, t):
                return qkv[:, 4 * i + h, t * P:(t + 1) * P]
            need(pe, "k_normed")
            for t in range(TT):
                four(f"ktok{t}", lambda h: seg(1, h, t), None, transpose=True)
            for t in range(TT):
                four(f"vtok{t}", lambda h: seg(2, h, t), None, transpose=True)
            for t in range(TT):
                four(f"KK{t}", lambda h: seg(1, h, t), lambda h: seg(1, h, t))
            need(pe, "q_normed")
            for t in range(TT):
                four(f"QK{t}", lambda h: seg(0, h, t), lambda h: seg(1, h, t))
            unit("z", xn)
            for t in range(TT):
                need(pe, "N16", t + 1)
                four(f"NT{t}", lambda h: N_[:, t, h], None, transpose=True)
            for r in ("2", "4"):
                for t in range(TT):
                    need(pe, "P_ready", (t + 1) if r == "2" else TT + 2 * t + 2)
                    four(f"P{r}_{t}", lambda h: NT[:, t, h], lambda h: N_[:, t, h])
                    four(f"PT{r}_{t}", lambda h: N_[:, t, h], lambda h: NT[:, t, h])
                    if r == "2" and t == 0:
                        unit("mem_k0", hB, ready=lambda k: need(pe, "mem_n", k + 1))
                for t in range(TT):
                    need(pe, "P_ready", TT + (0 if r == "2" else 2 * TT) + 2 * t + 2)
                    need(pe, "T_ready", (2 * t + 2) + (0 if r == "2" else 2 * TT))
                    four(f"T{r}_{t}", lambda h: T_T[:, t, h], lambda h: N_[:, t, h])
                    four(f"TT{r}_{t}", lambda h: N_[:, t, h], lambda h: T_T[:, t, h])
            for t in range(TT):
                four(f"P8_{t}", lambda h: NT[:, t, h], lambda h: N_[:, t, h])
            for t in range(TT):
                need(pe, "P_ready", 5 * TT + t + 1)
                need(pe, "T_ready", 4 * TT + 2 * t + 2)
                four(f"T8_{t}", lambda h: T_T[:, t, h], lambda h: N_[:, t, h])
                four(f"TT8_{t}", lambda h: N_[:, t, h], lambda h: T_T[:, t, h])
            for t in range(TT):
                need(pe, "T_ready", 6 * TT + 2 * t + 2)
                four(f"Y32_{t}", lambda h: off32[:, t, h], lambda h: T_T[:, t, h])
            for t in range(TT):
                need(pe, "Y_ready", t + 1)
                four(f"T32_{t}", lambda h: Y[:, t, h], lambda h: T_[:, t, h])
                four(f"TT32_{t}", lambda h: T_[:, t, h], lambda h: Y[:, t, h])
            unit("mem_k1", hB)
            for t in range(TT):
                need(pe, "T_ready", 8 * TT + 2 * t + 2)
                four(f"Y64_{t}", lambda h: off64[:, t, h], lambda h: T_T[:, t, h])
            for t in range(TT):
                need(pe, "Y_ready", TT + t + 1)
                four(f"TT64_{t}", lambda h: T_[:, t, h], lambda h: Y[:, t, h])
            for t in range(TT):
                need(pe, "intra", t + 1)
                four(f"intraT{t}", lambda h: intra[:, t, h], None, transpose=True)
            for t in range(TT):
                need(pe, "T_ready", 10 * TT + t + 1)
                four(f"u{t}", lambda h: T_T[:, t, h], lambda h: vbeta[:, t, h])
            for t in range(TT):
                four(f"wT{t}", lambda h: kbe[:, t, h], lambda h: T_T[:, t, h])
            unit("mem_v0", hB, tokens_out=True)
            need(pe, "delta_operands", 6)
            for c in range(4):
                t, o = c // 2, CHUNK * (c % 2)
                rows = slice(o, o + CHUNK)
                if c:
                    need(pe, "state", c)
                    out = tile_begin(f"wS{c}")
                    for h in range(NH):
                        mm = pe.matmul(out[rows, h * P:(h + 1) * P], lhsT=wT[:, t, h, rows], rhs=S_st[:, h, :],
                                       start=True, stop=True)
                    post(mm, "tiles")
                out = tile_begin(f"o{c}")
                need(pe, "v_new", c + 1)
                for h in range(NH):
                    oh = out[:, h * CHUNK:(h + 1) * CHUNK]
                    if c:
                        pe.matmul(oh, lhsT=S_st[:, h, :], rhs=qdec[:, t, h, rows], start=True, stop=False)
                    mm = pe.matmul(oh, lhsT=v_new[rows, t, h, :], rhs=intraT[rows, t, h, rows], start=(c == 0), stop=True)
                post(mm, "tiles")
                if c == 3:
                    continue
                out = tile_begin(f"dS{c}")
                for h in range(NH):
                    mm = pe.matmul(out[:, h * P:(h + 1) * P], lhsT=kdec[rows, t, h, :], rhs=v_new[rows, t, h, :],
                                   start=True, stop=True)
                post(mm, "tiles")
            def delta_sums():
                need(pe, "o_squares")
                for i in range(2):
                    out = tile_begin(f"ss_o{i}")
                    post(pe.matmul(out, lhsT=ones, rhs=norm2[:, 512 * i:512 * (i + 1)], start=True, stop=True), "tiles")

            unit("mem_v1", hB, tokens_out=True, between=delta_sums)
            unit("mix_out0", yT, ready=lambda k: need(pe, "y_conv", k + 1) if k < 4 else need(pe, "y_dn", k - 3))
            unit("mix_out1", yT)
            unit("xq0", xn, ready=lambda k: need(pe, "xn", KB + k + 1),
                 between=lambda: sum_channels("ss_h1", sq, KB, ready=squared(2)))
            unit("xq1", xn)
            need(pe, "mem_kv", 8)
            for h in range(NH):
                need(pe, "aq", h + 1)
                out = tile_begin(f"att_s{h}")
                for t in range(TT):
                    for j in range(2):
                        mm = pe.matmul(out[:, t * S:(t + 1) * S], lhsT=aq[:, 2 * h + j, t * P:(t + 1) * P],
                                       rhs=mem_kT[:, 2 * h + j, :], start=(j == 0), stop=(j == 1))
                post(mm, "tiles")
            for h in range(NH):
                need(pe, "prob", TT * (h + 1))
                out = tile_begin(f"att_p{h}")
                for m in range(2):
                    for t in range(TT):
                        mm = pe.transpose(out[:, m * S + t * P:m * S + (t + 1) * P], prob[:, h, t, m * P:(m + 1) * P], ident)
                post(mm, "tiles")
            for h in range(NH):
                need(pe, "probT", h + 1)
                out = tile_begin(f"att_o{h}")
                for j in range(2):
                    for m in range(2):
                        mm = pe.matmul(out[:, j * S:(j + 1) * S], lhsT=mem_v[:, m, (2 * h + j) * P:(2 * h + j + 1) * P],
                                       rhs=probT[:, h, m, :], start=(m == 0), stop=(m == 1))
                post(mm, "tiles")
            unit("xo0", ao, ready=lambda k: need(pe, "ao", k // 2 + 1))
            unit("xo1", ao)
            sum_channels("ss_h2", sq, KB, ready=squared(3))
            pe.wait_ge(sem("keys_in"), 16)

            def key_scores(tiles):
                for i in tiles:
                    t, heads, s = SCORE_TILES[i]
                    half = slice(64 * s, 64 * s + 64)
                    if i < 2:
                        need(pe, "pq_first")
                    else:
                        need(pe, "pq", heads[-1] // 2 + 1)
                    out = tile_begin(f"scores{i}")
                    for j, h in enumerate(heads):
                        mm = pe.matmul(out[:, j * KEYS:(j + 1) * KEYS], lhsT=pq[half, h, t * P:(t + 1) * P],
                                       rhs=keys[half, h, :], start=True, stop=True)
                    post(mm, "tiles")

            unit("pq0", xn, ready=lambda k: need(pe, "xn", 2 * KB + k + 1), first_tile=lambda: key_scores(range(2)))
            def zero_sums(t):
                for i in range(2):
                    mm = pe.matmul(ps[:, sum_bank(t, i), :], lhsT=zeros, rhs=const[:, 0:512], start=True, stop=False, skip_group_check=True)
                post(mm, "acc_zero")

            need(pe, "zeros")
            need(pe, "pq", 2)
            unit("pq1", xn, between=lambda: zero_sums(0))
            key_scores(range(2, len(SCORE_TILES)))
            need(pe, "scores", len(SCORE_TILES))
            need(pe, "mod_read")
            need(pe, "xn", 4 * KB)
            for t in range(TT):
                for i in range(2):
                    for j in range(4):
                        mm = pe.transpose(ps[:, 4 + 2 * t + i, j * P:(j + 1) * P], xn[:, 4 * i + j, t * P:(t + 1) * P], ident)
                    post(mm, "x_tok")
            for t in range(TT):
                if t:
                    zero_sums(t)
                with pe.Fori(0, PH) as h:
                    for j in range(TOPK):
                        b = j % RING
                        pe.wait_ge(sem("diag"), t * PH * TOPK + h * TOPK + j + 1)
                        for n in range(2):
                            mm = pe.matmul(ps[:, sum_bank(t, n), :], lhsT=diag[:, j], rhs=ring[b][:, D + 512 * n:D + 512 * (n + 1)],
                                           start=False, stop=False, skip_group_check=True)
                        mm.then_inc(sem(f"row_free{b}"), 1)
                need(pe, "y_tok", t + 1)
                for i in range(2):
                    for j in range(4):
                        mm = pe.transpose(ps[:, 4 + 2 * t + i, j * P:(j + 1) * P],
                                          ysb[t][:, (4 * i + j) * P:(4 * i + j + 1) * P], ident)
                    post(mm, "y_back")
                need(pe, "h3_squares", t + 1)
                for i in range(2):
                    for k in range(KB):
                        weight = gain2[:, k:k + 1].broadcast_to([P, P]) if i else ones
                        mm = pe.matmul(ps[:, 4, (2 * i + t) * P:(2 * i + t + 1) * P], lhsT=weight, rhs=sq_h[:, k, t * P:(t + 1) * P],
                                       start=(k == 0), stop=(k == KB - 1))
                post(mm, "h3_sums")
            for i in range(4):
                unit(f"cv_ab{i}", xn, ready=(lambda k: need(pe, "shifted", k + 1)) if i == 0 else None)
            unit("cv_g0", xn)

            def mean_of(order):
                for k in order:
                    if k in CONV_POOL:
                        need(pe, "conv_pool", CONV_POOL.index(k) + 1)
                    else:
                        need(pe, "conv_dve", CONV_DVE.index(k) + 1)
                    mm = pe.matmul(tile_ps("mean")[:, 0:S], lhsT=ones, rhs=yc[:, k, :], start=(k == 0), stop=(k == KB - 1))
                return mm

            tile_begin("mean")
            unit("cv_g1", xn, between=lambda: mean_of(range(KB - 1)))
            post(mean_of((KB - 1,)), "tiles")
            sum_channels("var", sq, KB, ready=squared(4))
            unit("cv_out0", ycn, ready=lambda k: need(pe, "cv_y", k + 1))
            unit("cv_out1", ycn)
            sum_channels("ss_m1", sq, KB, ready=squared(5))
            unit("pl_v0", xn, ready=lambda k: need(pe, "shifted", KB + k + 1))
            for n in ("pl_v1", "pl_g0", "pl_g1"):
                unit(n, xn)
            n = UNITS.index("grp")
            wg = wring[:, n % W_SLOTS].rearrange("p k n -> p (k n)")[:, 0:2048].rearrange("p (k n) -> p k n", k=8)
            pe.wait_ge(sem(f"w_in{n % W_SLOTS}"), 16 * (n // W_SLOTS + 1))
            for g in range(4):
                p = FIRST_PAIR["grp"] + g
                pe.wait_ge(sem(f"pair_free{p % PAIR_BANKS}"), p // PAIR_BANKS)
                need(pe, "pooled", g + 1)
                for j in range(2):
                    for k in range(2):
                        mm = pe.matmul(pair_ps(p)[:, j * S:(j + 1) * S], lhsT=wg[:, 2 * g + k, j * P:(j + 1) * P],
                                       rhs=pooled[:, 2 * g + k, :], start=(k == 0), stop=(k == 1))
                post(mm, "pairs")
            unit("pl_out0", ycn, ready=lambda k: need(pe, "pl_y", k + 1))
            unit("pl_out1", ycn)

        @block.scalar
        def _(act):
            def go(ins, name):
                return did(act, ins, name)

            act.dma_start(const[:, 0:CONST_FIRST], const_d[:, 0:CONST_FIRST]).then_inc(sem("const_in"), 16)

            def squares(src, ready=None):
                for i in range(4):
                    if ready:
                        ready(i)
                    last = post(act.activation(sq[:, 2 * i:2 * i + 2, :], src[:, 2 * i:2 * i + 2, :], ACT.Square), "squares")
                need(act, "squares", last)

            def root(name, out, n, scale):
                go(act.activation(warm[:], cst("one"), ACT.Sqrt), "warm")
                tile_ready(act, name)
                tile_used_wait(act, act.activation(out, tile_ps(name)[:, 0:n], ACT.Sqrt, bias=cst("eps"), scale=scale), name)

            act.wait_ge(sem("x_in"), 16)
            squares(hA[:])
            act.dma_start(hB[:], mem_t).then_inc(sem("mem_in"), 16)
            act.dma_start(small_w[:], small_d).then_inc(sem("small_in"), 16)
            act.dma_start(const[:, CONST_FIRST:], const_d[:, CONST_FIRST:]).then_inc(sem("const2_in"), 16)
            act.wait_ge(sem("const_in"), 16)
            root("ss_x", rms[:, 0], S, 1.0 / D)
            signal(act, "root")
            act.wait_ge(sem("mem_in"), 16)
            squares(hB[:])
            act.wait_ge(sem("cols_in"), 16)
            go(act.activation(silu_c[:], col("c", 0, KB), ACT.Silu), "silu_c")
            need(act, "rinv", 1)
            root("ss_mem", rms[:, 0], S, 1.0 / D)
            signal(act, "root")
            need(act, "pads")
            for i, u in enumerate(("k", "v")):
                for j in range(2):
                    p = FIRST_PAIR[u] + j
                    pair_ready(act, p)
                    pair_used_wait(act, act.copy(qkv_pad[:, 4 * i + 4 + 2 * j:4 * i + 6 + 2 * j, 3:3 + S],
                                                 pair_ps(p).rearrange("p (b t) -> p b t", b=2)), p)
                    signal(act, "kv_in", 1)
            for i in range(3):
                need(act, "qkv_conv", 4 * (i + 1))
                v = qkv[:, 4 * i:4 * i + 4, :]
                go(act.activation(v, v, ACT.Silu), "qkv_act")
            for i in range(2):
                go(act.activation(blocks(norm2[:, 1024 * i:1024 * (i + 1)], 4), qkv[:, 4 * i:4 * i + 4, :], ACT.Square), "qk_squares")
            for i, n in enumerate(("ss_q0", "ss_q1", "ss_k0", "ss_k1")):
                root(n, norm2[:, 512 * i:512 * (i + 1)], 512, 1.0)
                signal(act, "qk_root", 1)
            need(act, "logits")
            beta_l, z_abs = tiny[:, 1], tiny[:, 4]
            go(act.activation(tiny[:, 2], beta_l, ACT.Exp, scale=-1.0), "exp_b")
            need(act, "z_abs")
            go(act.activation(tiny[:, 5], z_abs, ACT.Exp, scale=-1.0), "exp_z")
            go(act.activation(tiny[:, 6, 0], col("a_log", 0, NH), ACT.Exp), "exp_a")
            need(act, "z_exp1")
            go(act.activation(tiny[:, 5], tiny[:, 5], ACT.Ln), "ln_z")
            for j in range(2):
                p = FIRST_PAIR["b"] + j
                pair_ready(act, p)
                pair_used_wait(act, act.copy(bT[:, 2 * j:2 * j + 2, :], blocks(pair_ps(p), 2)), p)
                signal(act, "bT", 1)
            need(act, "gcum")
            go(act.activation(tiny[:, 10], tiny[:, 9], ACT.Exp), "exp_g")
            go(act.activation(tiny[:, 12], tiny[:, 11], ACT.Exp), "exp_gd")
            for t in range(TT):
                tile_ready(act, f"gB{t}")
                go(act.activation(egB[:, t].rearrange("p h j -> p (h j)"), tile_ps(f"gB{t}"), ACT.Exp), "egB")
            for t in range(TT):
                need(act, "diff", t + 1)
                go(act.activation(E[:, t], E[:, t], ACT.Exp, scale=-1.0), "E")
            for j in range(2):
                p = FIRST_PAIR["c"] + j
                pair_ready(act, p)
                pair_used_wait(act, act.copy(cT[:, 2 * j:2 * j + 2, :], blocks(pair_ps(p), 2)), p)
                signal(act, "cT", 1)
            for j in range(2):
                p = FIRST_PAIR["z"] + j
                pair_ready(act, p)
                pair_used_wait(act, act.activation(zT[:, 2 * j:2 * j + 2, :], blocks(pair_ps(p), 2), ACT.Silu), p)
                signal(act, "zT", 1)
            def kv_copy(u, js=range(2)):
                for j in js:
                    p = FIRST_PAIR[u] + j
                    pair_ready(act, p)
                    if u[4] == "k":
                        dst, src = mem_kT[:, 4 * int(u[5]) + 2 * j:4 * int(u[5]) + 2 * j + 2, :], blocks(pair_ps(p), 2)
                    else:
                        dst, src = mem_v[:, j, 512 * int(u[5]):512 * int(u[5]) + 512], pair_ps(p)
                    pair_used_wait(act, act.copy(dst, src), p)
                    signal(act, "mem_kv", 1)
            need(act, "y_conv", 4)
            kv_copy("mem_k0")
            kv_copy("mem_k1")
            for t in range(TT):
                tile_ready(act, f"intraT{t}")
                tile_used_wait(act, act.copy(intraT[:, t].rearrange("p h j -> p (h j)"), tile_ps(f"intraT{t}")), f"intraT{t}")
                signal(act, "delta_operands", 1)
            for t in range(TT):
                tile_ready(act, f"u{t}")
                tile_used_wait(act, act.copy(u_tok[:, t].rearrange("p h j -> p (h j)"), tile_ps(f"u{t}")), f"u{t}")
                signal(act, "delta_operands", 1)
            for t in range(TT):
                tile_ready(act, f"wT{t}")
                tile_used_wait(act, act.copy(wT[:, t].rearrange("p h j -> p (h j)"), tile_ps(f"wT{t}")), f"wT{t}")
                signal(act, "delta_operands", 1)
            kv_copy("mem_v0")
            need(act, "inverted")
            for c in range(4):
                tile_ready(act, f"o{c}")
                tile_used_wait(act, act.copy(oT[:, :, c * CHUNK:(c + 1) * CHUNK],
                                             tile_ps(f"o{c}")[:, 0:NH * CHUNK].rearrange("p (h j) -> p h j", h=NH)), f"o{c}")
            need(act, "scanned")
            act.dma_start(keys, keys_d).then_inc(sem("keys_in"), 16)
            go(act.activation(blocks(norm2[:, 0:1024], 4), oT, ACT.Square), "o_squares")
            kv_copy("mem_v1", (0,))
            for i in range(2):
                root(f"ss_o{i}", norm2[:, 512 * i:512 * (i + 1)], 512, 1.0 / P)
                signal(act, "o_root", 1)
            kv_copy("mem_v1", (1,))

            def norm_act(src, name, ready, rinvs):
                squares(src, ready)
                need(act, "rinv", rinvs)
                root(name, rms[:, 0], S, 1.0 / D)
                signal(act, "root")

            norm_act(hB[:], "ss_h1", lambda i: need(act, "h1", i + 1), 2)
            for h in range(NH):
                need(act, "att_max", h + 1)
                for t in range(TT):
                    ins = act.activation(prob[:, h, t], tile_ps(f"att_s{h}")[:, t * S:(t + 1) * S], ACT.Exp,
                                         bias=tiny[:, 14, t, h:h + 1], scale=float(S) ** -0.5,
                                         accum_out=tiny[:, 15, t, h:h + 1])
                    if t == TT - 1:
                        tile_used_wait(act, ins, f"att_s{h}")
                    else:
                        go(ins, "att_exp0")
                signal(act, "att_exp", 1)
            for h in range(NH):
                tile_ready(act, f"att_p{h}")
                tile_used_wait(act, act.copy(probT[:, h].rearrange("p m t -> p (m t)"), tile_ps(f"att_p{h}")), f"att_p{h}")
                signal(act, "probT", 1)
            for h in range(NH):
                tile_ready(act, f"att_o{h}")
                tile_used_wait(act, act.copy(ao[:, 2 * h:2 * h + 2, :], blocks(tile_ps(f"att_o{h}"), 2)), f"att_o{h}")
                signal(act, "ao", 1)
            norm_act(hA[:], "ss_h2", lambda i: need(act, "h2", i + 1), 3)
            def score_copies(tiles):
                for i in tiles:
                    t, heads, s = SCORE_TILES[i]
                    n = len(heads)
                    dst = score[t].rearrange("p (h s n) -> p h s n", h=PH, s=2)[:, heads[0]:heads[0] + n, s, :]
                    tile_ready(act, f"scores{i}")
                    tile_used_wait(act, act.copy(dst, tile_ps(f"scores{i}")[:, 0:n * KEYS].rearrange("p (h n) -> p h n", h=n)), f"scores{i}")
                    signal(act, "scores", 1)

            score_copies(range(2))
            def gate_exp(r):
                act.wait_ge(sem("gate_arg"), r + 1)
                act.activation(gexp, gexp, ACT.Exp, accum_out=gsum).then_inc(sem("gate_exp"), 1)

            for r in range(AHEAD):
                gate_exp(r)
            score_copies(range(2, len(SCORE_TILES)))
            for t in range(TT):
                for first, last in HEAD_LOOPS[t]:
                    with act.Fori(first, last) as h:
                        for j in range(TOPK):
                            act.wait_ge(sem("dots"), (t * PH + h) * TOPK + j + 1)
                            act.activation(gel16[:, j:j + 1], act16[:, j:j + 1], ACT.Gelu).then_inc(sem("gelu"), 1)
                            if j == 10 and t * PH + first + AHEAD < HEADS:
                                gate_exp(t * PH + h + AHEAD)
                act.wait_ge(sem(f"row_free{RING - 1}"), (t + 1) * 2 * PH + 1)
                for n in range(2):
                    go(act.copy(ysb[t][:, 512 * n:512 * (n + 1)], ps[:, sum_bank(t, n), :]), "y_half")
                signal(act, "y_tok", 1)
                tok = slice(t * P, (t + 1) * P)
                for i in range(2):
                    need(act, "h2y", 2 * t + i + 1)
                    k4 = slice(4 * i, 4 * i + 4)
                    last = post(act.activation(sq_h[:, k4, tok], hA[:, k4, tok], ACT.Square), "h3_part")
                need(act, "h3_part", last)
                signal(act, "h3_squares", 1)
            go(act.activation(warm[:], cst("one"), ACT.Sqrt), "warm")
            need(act, "h3_sums", TT)
            need(act, "rinv", 4)
            go(act.activation(rms[:, 0], ps[:, 4, 0:S], ACT.Sqrt, bias=cst("eps"), scale=1.0 / D), "root")
            need(act, "h3_mean", 1)
            go(act.activation(rms[:, 0], rms[:, 0], ACT.Sqrt, bias=cst("eps"), scale=1.0 / D), "root")
            def shifted(layer):
                for k in range(KB):
                    need(act, "unshifted", KB * layer + k + 1)
                    last = post(act.activation(xn[:, k], xn[:, k], ACT.Identity, bias=modc[:, 24 * layer + k:24 * layer + k + 1]), "shifted")
                need(act, "shifted", last)

            need(act, "mod_read")
            shifted(0)

            def tap_products(i, first, last):
                b = CONV_POOL[i]
                for tap in range(first, last):
                    n = i * CV_TAPS + tap
                    if n >= PRODUCTS:
                        block_before, tap_before = divmod(n - PRODUCTS, CV_TAPS)
                        need(act, "conv_sum", block_before * (CV_TAPS - 1) + max(tap_before, 1))
                    w = col("cv_dw", 8 * tap + b)
                    x = ypad[:, b, tap:tap + S]
                    if tap == 0:
                        post(act.activation(products[n % PRODUCTS], x, ACT.Identity, scale=w, bias=col("cv_db", b)), "product")
                    else:
                        post(act.activation(products[n % PRODUCTS], x, ACT.Copy, scale=w), "product")

            def gate_sigmoid(k):
                pair_ready(act, FIRST_PAIR["cv_ab0"] + k)
                if k >= 2:
                    need(act, "glu", k - 1)
                go(act.activation(sgb[:, k % 2], pair_ps(FIRST_PAIR["cv_ab0"] + k)[:, S:], ACT.Sigmoid), "sig_b")

            def gate_silu(i):
                p = FIRST_PAIR["cv_g0"] + i
                pair_ready(act, p)
                pair_used_wait(act, act.activation(gT[:, 2 * i:2 * i + 2, :], blocks(pair_ps(p), 2), ACT.Silu), p)
                signal(act, "gT", 1)

            go(act.activation(warm[:], cst("one"), ACT.Sigmoid), "warm")
            gate_sigmoid(0)
            gate_sigmoid(1)
            need(act, "ypads")
            need(act, "glu", CONV_POOL[0] + 1)
            for i in range(4):
                tap_products(0, 8 * i, min(8 * i + 8, CV_TAPS))
                gate_sigmoid(2 + i)
            need(act, "glu", CONV_POOL[1] + 1)
            for i in range(4):
                tap_products(1, 8 * i, min(8 * i + 8, CV_TAPS))
                if i < 2:
                    gate_sigmoid(6 + i)
                elif i == 2:
                    gate_silu(0)
            for i in range(1, 4):
                gate_silu(i)
            tile_ready(act, "mean")
            tile_used_wait(act, act.activation(rms[:, 0], tile_ps("mean")[:, 0:S], ACT.Copy, scale=1.0 / D), "mean")
            signal(act, "mean_sb", 1)
            squares(yc, lambda i: need(act, "centred", i + 1))
            root("var", rms[:, 0], S, 1.0 / D)
            signal(act, "root")
            for k in range(KB):
                need(act, "standard", k + 1)
                go(act.activation(ycn[:, k], ycn[:, k], ACT.Silu, bias=col("ln_b", k), scale=col("ln_g", k)), "ln_silu")
            norm_act(hA[:], "ss_m1", lambda i: need(act, "h4", 2 * (i + 1)), 7)
            shifted(1)
            for i in range(4):
                p = FIRST_PAIR["pl_v0"] + i
                pair_ready(act, p)
                pair_used_wait(act, act.copy(vpad[:, 2 * i:2 * i + 2, 8:8 + S], blocks(pair_ps(p), 2)), p)
                signal(act, "vpad", 1)
            for i in range(4):
                p = FIRST_PAIR["pl_g0"] + i
                pair_ready(act, p)
                pair_used_wait(act, act.activation(gT[:, 2 * i:2 * i + 2, :], blocks(pair_ps(p), 2), ACT.Silu), p)
                signal(act, "gT", 1)

        @block.vector
        def _(dve):
            V = nc.vector

            def go(ins, name="dve_step"):
                return did(dve, ins, name)

            def norm(n, src, dst, gain, name):
                need(dve, "root", n)
                go(V.reciprocal(rinv[:, 0], rms[:, 0]), "rinv")
                for k in range(KB):
                    last = post(V.scalar_tensor_tensor(out=dst[:, k], in0=src[:, k], scalar=col(gain, k), in1=rinv[:, 0],
                                                       op0=ALU.mult, op1=ALU.mult), name)
                need(dve, name, last)

            def norm_mod(src, gain, r):
                for k in range(KB):
                    last = post(V.scalar_tensor_tensor(out=xn[:, k], in0=src[:, k], scalar=gain[:, k:k + 1], in1=r,
                                                       op0=ALU.mult, op1=ALU.mult), "unshifted")
                need(dve, "unshifted", last)

            dve.memset(qkv_pad[:, :, 0:3], 0.0)
            go(V.memset(hc_pad[:, :, 0:2], 0.0), "pads")
            dve.wait_ge(sem("cols_in"), 16)
            def gained(src, dst, gain, name, ready=None):
                for k in range(KB):
                    if ready and k % 2 == 0:
                        ready(k // 2)
                    last = post(V.tensor_scalar(dst[:, k], src[:, k], col(gain, k), None, ALU.mult), name)
                need(dve, name, last)

            def inverse_root(n):
                need(dve, "root", n)
                go(V.reciprocal(rinv[:, 0], rms[:, 0]), "rinv")

            def rooted(p, dst):
                pair_ready(dve, p)
                pair_used_wait(dve, V.tensor_tensor(dst, blocks(pair_ps(p), 2), rinv[:].broadcast_to([P, 2, S]), ALU.mult), p)

            dve.wait_ge(sem("x_in"), 16)
            gained(hA, xg, "norm_mix", "xg")
            inverse_root(1)
            for k in range(KB):
                last = post(V.tensor_tensor(xn[:, k], xg[:, k], rinv[:, 0], ALU.mult), "xn")
            need(dve, "xn", last)
            for j in range(2):
                rooted(FIRST_PAIR["q"] + j, qkv_pad[:, 2 * j:2 * j + 2, 3:3 + S])
            norm(2, hB, hB, "norm_mem", "mem_n")

            dve.wait_ge(sem("const_in"), 16)
            tile_ready(dve, "logits")
            lg = tile_ps("logits")[:, 0:16].rearrange("p (t c) -> p t c", t=TT)
            dt = col("dt_bias", 0, NH).unsqueeze(1).broadcast_to([P, TT, NH])
            go(V.tensor_copy(tiny[:, 1], lg[:, :, 0:4]), "logits")
            tile_used_wait(dve, V.tensor_tensor(tiny[:, 3], lg[:, :, 4:8], dt, ALU.add), "logits")
            go(V.scalar_tensor_tensor(out=tiny[:, 4], in0=tiny[:, 3], scalar=-1.0, in1=tiny[:, 3],
                                      op0=ALU.mult, op1=ALU.max), "z_abs")
            go(V.tensor_scalar(tiny[:, 3], tiny[:, 3], 0.0, None, ALU.max))

            for b in range(0, 12, 2):
                if b >= 4:
                    need(dve, "kv_in", b // 2 - 1)
                for i in range(DN_TAPS):
                    for k in (b, b + 1):
                        w = col("dn_conv_w", 12 * i + k)
                        x = qkv_pad[:, k, i:i + S]
                        if i == 0:
                            last = post(V.tensor_scalar(qkv[:, k], x, w, None, ALU.mult), "dn_tap")
                        else:
                            need(dve, "dn_tap", last - 1)
                            last = post(V.scalar_tensor_tensor(out=qkv[:, k], in0=x, scalar=w, in1=qkv[:, k],
                                                               op0=ALU.mult, op1=ALU.add), "dn_tap")
                need(dve, "dn_tap", last)
                signal(dve, "qkv_conv", 2)

            need(dve, "exp_b")
            go(V.tensor_scalar(tiny[:, 2], tiny[:, 2], 1.0, None, ALU.add))
            go(V.reciprocal(tiny[:, 2], tiny[:, 2]), "beta")
            need(dve, "exp_z")
            go(V.tensor_scalar(tiny[:, 5], tiny[:, 5], 1.0, None, ALU.add), "z_exp1")
            need(dve, "ln_z")
            go(V.tensor_tensor(tiny[:, 7], tiny[:, 3], tiny[:, 5], ALU.add))
            need(dve, "exp_a")
            go(V.scalar_tensor_tensor(out=tiny[:, 8], in0=tiny[:, 7], scalar=-1.0,
                                      in1=tiny[:, 6, 0].unsqueeze(1).broadcast_to([P, TT, NH]),
                                      op0=ALU.mult, op1=ALU.mult), "g")
            beta, eg, egd = tiny[:, 2], tiny[:, 10], tiny[:, 12]

            def flat(ap):
                return ap.rearrange("p t h -> p (t h)")

            for i in range(2):
                need(dve, "qk_root", 2 * (i + 1))
                r = norm2[:, 1024 * i:1024 * (i + 1)]
                go(V.reciprocal(r, r))
                x = qkv[:, 4 * i:4 * i + 4, :]
                if i == 0:
                    go(V.scalar_tensor_tensor(out=x, in0=x, scalar=float(P) ** -0.5, in1=blocks(r, 4),
                                              op0=ALU.mult, op1=ALU.mult), "q_normed")
                else:
                    go(V.tensor_tensor(x, x, blocks(r, 4), ALU.mult), "k_normed")

            tile_ready(dve, "gcum")
            go(V.tensor_copy(flat(tiny[:, 9]), tile_ps("gcum")[:, 0:8]))
            tile_used_wait(dve, V.tensor_tensor(flat(tiny[:, 11]), tile_ps("gcum")[:, 8:16], flat(tiny[:, 9]), ALU.subtract), "gcum")
            signal(dve, "gcum", 1)
            for t in range(TT):
                need(dve, "egB", t + 1)
                src = tile_ps(f"gB{t}").rearrange("p (h j) -> p h j", h=NH)
                tile_used_wait(dve, V.tensor_tensor(E[:, t], src, tiny[:, 9, t].unsqueeze(2).broadcast_to([P, NH, P]), ALU.subtract), f"gB{t}")
                go(V.tensor_scalar(E[:, t], E[:, t], 0.0, None, ALU.max), "diff")
            need(dve, "exp_g")
            go(V.tensor_tensor(tiny[:, 13], beta, eg, ALU.mult))
            need(dve, "exp_gd")

            def per_token(t, src, dst, c):
                return V.tensor_tensor(dst[:, t], src, c[:, t].unsqueeze(2).broadcast_to([P, NH, P]), ALU.mult)

            def tile_heads(name):
                return tile_ps(name).rearrange("p (h j) -> p h j", h=NH)

            need(dve, "egB", TT)
            for t in range(TT):
                go(V.tensor_tensor(qdec[:, t], qkv[:, 0:4, t * P:(t + 1) * P], egB[:, t], ALU.mult))
            for c in range(4):
                go(V.tensor_copy(gl[:, c], egB[:, c // 2, :, CHUNK * (c % 2) + CHUNK - 1]))
            for t in range(TT):
                tile_ready(dve, f"ktok{t}")
                go(per_token(t, tile_heads(f"ktok{t}"), kbe, tiny[:, 13]))
                tile_used_wait(dve, per_token(t, tile_heads(f"ktok{t}"), kdec, egd), f"ktok{t}")
            for t in range(TT):
                tile_ready(dve, f"vtok{t}")
                tile_used_wait(dve, per_token(t, tile_heads(f"vtok{t}"), vbeta, beta), f"vtok{t}")

            def mask(name):
                return cst(name).unsqueeze(1).broadcast_to([P, NH, P])

            for t in range(TT):
                need(dve, "E", t + 1)
                tile_ready(dve, f"KK{t}")
                tile_used_wait(dve, V.tensor_tensor(Y[:, t], tile_heads(f"KK{t}"), E[:, t], ALU.mult), f"KK{t}")
                go(V.tensor_tensor(Y[:, t], Y[:, t], beta[:, t].unsqueeze(2).broadcast_to([P, NH, P]), ALU.mult))
                go(V.scalar_tensor_tensor(out=N_[:, t], in0=Y[:, t], scalar=-1.0, in1=mask("strict16"),
                                          op0=ALU.mult, op1=ALU.mult), "N16")
                go(V.tensor_tensor(off32[:, t], Y[:, t], mask("off32"), ALU.mult))
                go(V.tensor_tensor(off64[:, t], Y[:, t], mask("off64"), ALU.mult))
                go(V.tensor_tensor(E[:, t], E[:, t], mask("causal"), ALU.mult))
                tile_ready(dve, f"QK{t}")
                tile_used_wait(dve, V.tensor_tensor(intra[:, t], tile_heads(f"QK{t}"), E[:, t], ALU.mult), f"QK{t}")
                signal(dve, "intra", 1)
            for t in range(TT):
                tile_ready(dve, f"NT{t}")
                tile_used_wait(dve, V.tensor_copy(NT[:, t], tile_heads(f"NT{t}")), f"NT{t}")
                signal(dve, "P_ready", 1)
                go(V.tensor_tensor(T_[:, t], N_[:, t], mask("ident"), ALU.add), "T_ready")
                go(V.tensor_tensor(T_T[:, t], NT[:, t], mask("ident"), ALU.add), "T_ready")

            for j in range(2):
                p = FIRST_PAIR["h"] + j
                need(dve, "cT", j + 1)
                pair_ready(dve, p)
                pair_used_wait(dve, V.tensor_tensor(hc_pad[:, 2 * j:2 * j + 2, 2:2 + S], blocks(pair_ps(p), 2),
                                                    cT[:, 2 * j:2 * j + 2, :], ALU.mult), p)
            need(dve, "bT", 2)
            for b in range(4):
                go(V.tensor_scalar(yT[:, b], hc_pad[:, b, 0:S], col("conv_w", b), None, ALU.mult))
                for i in range(1, TAPS):
                    go(V.scalar_tensor_tensor(out=yT[:, b], in0=hc_pad[:, b, i:i + S], scalar=col("conv_w", 4 * i + b),
                                              in1=yT[:, b], op0=ALU.mult, op1=ALU.add))
                go(V.tensor_tensor(yT[:, b], yT[:, b], bT[:, b], ALU.mult), "y_conv")

            def take(name, t, dst, ready):
                tile_ready(dve, f"{name}_{t}")
                tile_used_wait(dve, V.tensor_copy(dst[:, t], tile_heads(f"{name}_{t}")), f"{name}_{t}")
                if ready:
                    signal(dve, ready, 1)

            def accumulate(name, t, dst, op):
                tile_ready(dve, f"{name}_{t}")
                tile_used_wait(dve, V.tensor_tensor(dst[:, t], dst[:, t], tile_heads(f"{name}_{t}"), op), f"{name}_{t}")
                signal(dve, "T_ready", 1)

            for r in ("2", "4"):
                for t in range(TT):
                    tile_ready(dve, f"PT{r}_{t}")
                    take(f"P{r}", t, N_, "P_ready")
                    take(f"PT{r}", t, NT, "P_ready")
                for t in range(TT):
                    tile_ready(dve, f"TT{r}_{t}")
                    accumulate(f"T{r}", t, T_, ALU.add)
                    accumulate(f"TT{r}", t, T_T, ALU.add)
            for t in range(TT):
                take("P8", t, N_, "P_ready")
            for t in range(TT):
                tile_ready(dve, f"TT8_{t}")
                accumulate("T8", t, T_, ALU.add)
                accumulate("TT8", t, T_T, ALU.add)
            for t in range(TT):
                take("Y32", t, Y, "Y_ready")
            for t in range(TT):
                tile_ready(dve, f"TT32_{t}")
                accumulate("T32", t, T_, ALU.subtract)
                accumulate("TT32", t, T_T, ALU.subtract)
            for t in range(TT):
                take("Y64", t, Y, "Y_ready")
            for t in range(TT):
                accumulate("TT64", t, T_T, ALU.subtract)
            tile_ready(dve, f"intraT{TT - 1}")
            signal(dve, "inverted", 1)
            need(dve, "delta_operands", 6)
            for c in range(4):
                t, o = c // 2, CHUNK * (c % 2)
                rows = slice(o, o + CHUNK)
                if c:
                    tile_ready(dve, f"wS{c}")
                    tile_used_wait(dve, V.tensor_tensor(v_new[rows, t], u_tok[rows, t],
                                                        tile_heads(f"wS{c}")[rows], ALU.subtract), f"wS{c}")
                    signal(dve, "v_new", 1)
                else:
                    go(V.tensor_copy(v_new[rows, t], u_tok[rows, t]), "v_new")
                if c == 3:
                    continue
                tile_ready(dve, f"dS{c}")
                if c == 0:
                    tile_used_wait(dve, V.tensor_copy(S_st, tile_heads("dS0")), "dS0")
                else:
                    go(V.tensor_tensor(S_st, S_st, gl[:, c].unsqueeze(2).broadcast_to([P, NH, P]), ALU.mult))
                    tile_used_wait(dve, V.tensor_tensor(S_st, S_st, tile_heads(f"dS{c}"), ALU.add), f"dS{c}")
                signal(dve, "state", 1)
            signal(dve, "scanned", 1)
            need(dve, "o_root", 2)
            need(dve, "zT", 2)
            go(V.reciprocal(norm2[:, 0:1024], norm2[:, 0:1024]))
            go(V.tensor_tensor(zT, zT, blocks(norm2[:, 0:1024], 4), ALU.mult))
            for h in range(NH):
                go(V.scalar_tensor_tensor(out=yT[:, 4 + h], in0=oT[:, h], scalar=col("dn_norm"), in1=zT[:, h],
                                          op0=ALU.mult, op1=ALU.mult), "y_dn")

            def residual(unit0, src, dst, name, gain):
                for i in range(4):
                    p = FIRST_PAIR[unit0] + i
                    pair_ready(dve, p)
                    pair_used_wait(dve, V.tensor_tensor(dst[:, 2 * i:2 * i + 2, :], blocks(pair_ps(p), 2),
                                                        src[:, 2 * i:2 * i + 2, :], ALU.add), p)
                    signal(dve, name, 1)
                    for k in (2 * i, 2 * i + 1):
                        last = post(V.tensor_scalar(xn[:, k], dst[:, k], col(gain, k), None, ALU.mult), "xn")
                need(dve, "xn", last)

            residual("mix_out0", hA, hB, "h1", "norm_x")
            inverse_root(3)
            for i in range(4):
                rooted(FIRST_PAIR["xq0"] + i, aq[:, 2 * i:2 * i + 2, :])
                signal(dve, "aq", 1)
            for h in range(NH):
                tile_ready(dve, f"att_s{h}")
                go(V.tensor_reduce(tiny[:, 13, :, h], tile_ps(f"att_s{h}").rearrange("p (t m) -> p t m", t=TT), AX_X, ALU.max))
                go(V.tensor_scalar(tiny[:, 14, :, h], tiny[:, 13, :, h], -float(S) ** -0.5, None, ALU.mult), "att_max")
            for h in range(NH):
                need(dve, "att_exp", h + 1)
                go(V.reciprocal(tiny[:, 15, :, h], tiny[:, 15, :, h]))
                for t in range(TT):
                    go(V.tensor_scalar(prob[:, h, t], prob[:, h, t], tiny[:, 15, t, h:h + 1], None, ALU.mult), "prob")
            go(V.memset(zeros, 0.0), "zeros")
            residual("xo0", hB, hA, "h2", "norm_ffn")
            inverse_root(4)
            first = blocks(pair_ps(FIRST_PAIR["pq0"]), 2)
            need(dve, "pair_tile")
            go(V.tensor_tensor(pq[:, 0:2, 0:P], first[:, :, 0:P], rinv[:, :, 0:P].broadcast_to([P, 2, P]), ALU.mult), "pq_first")
            B4 = [P, 2, TOPK, TOPK]
            route_posts = [0]

            def route(step, r):
                def done(ins):
                    route_posts[0] += 1
                    ins.then_inc(sem("route"), 1)

                def so_far():
                    dve.wait_ge(sem("route"), r * ROUTE_POSTS + route_posts[0])
                    dve.sem_inc(sem("route_turn"), 1)

                if step == 0:
                    route_posts[0] = 0
                    done(V.tensor_copy(halves.rearrange("p s n -> p (s n)"), all_scores[:, bass.ds(r * 2 * KEYS, 2 * KEYS)]))
                elif step == 1:
                    so_far()
                    for s in range(2):
                        done(V.max(topv[:, s, 0:8], halves[:, s]))
                elif step == 2:
                    so_far()
                    for s in range(2):
                        done(V.max_index(topi[:, s, 0:8], topv[:, s, 0:8], halves[:, s]))
                        done(V.match_replace(scr[:, s * KEYS:(s + 1) * KEYS], topv[:, s, 0:8], halves[:, s], LOWEST))
                elif step == 3:
                    so_far()
                    for s in range(2):
                        done(V.max(topv[:, s, 8:16], scr[:, s * KEYS:(s + 1) * KEYS]))
                elif step == 4:
                    so_far()
                    for s in range(2):
                        done(V.max_index(topi[:, s, 8:16], topv[:, s, 8:16], scr[:, s * KEYS:(s + 1) * KEYS]))
                elif step == 5:
                    so_far()
                    done(V.tensor_copy(topf, topi))
                    done(V.tensor_tensor(cand.rearrange("p (a b) -> p a b", a=TOPK), topv[:, 0].unsqueeze(2).broadcast_to(B4[:1] + B4[2:]),
                                         topv[:, 1].unsqueeze(1).broadcast_to(B4[:1] + B4[2:]), ALU.add))
                elif step == 6:
                    so_far()
                    done(V.max(best[:, 0:8], cand))
                elif step == 7:
                    so_far()
                    done(V.max_index(posn[:, 0:8], best[:, 0:8], cand))
                    done(V.match_replace(scr, best[:, 0:8], cand, LOWEST))
                elif step == 8:
                    so_far()
                    done(V.max(best[:, 8:16], scr))
                elif step == 9:
                    so_far()
                    done(V.max_index(posn[:, 8:16], best[:, 8:16], scr))
                    V.tensor_tensor(gexp, best, best[:, 0:1].broadcast_to([P, TOPK]), ALU.subtract).then_inc(sem("gate_arg"), 1)
                elif step == 10:
                    so_far()
                    done(V.tensor_scalar(pab[:, 0], posn, 4, None, ALU.logical_shift_right))
                    done(V.tensor_scalar(pab[:, 1], posn, 15, None, ALU.bitwise_and))
                elif step == 11:
                    so_far()
                    done(V.tensor_copy(pabf, pab))
                elif step == 12:
                    so_far()
                    done(V.tensor_tensor(hot, pabf.unsqueeze(3).broadcast_to(B4),
                                         cst("iota16").unsqueeze(1).unsqueeze(1).broadcast_to(B4), ALU.is_equal))
                elif step == 13:
                    so_far()
                    done(V.tensor_tensor(hot, hot, topf.unsqueeze(2).broadcast_to(B4), ALU.mult))
                    dve.wait_ge(sem("gate_exp"), r + 1)
                    done(V.reciprocal(gsum, gsum))
                elif step == 14:
                    so_far()
                    done(V.tensor_reduce(picked, hot, AX_X, ALU.add))
                    done(V.tensor_tensor(gate[:, bass.ds(r * TOPK, TOPK)], gexp, gsum.broadcast_to([P, TOPK]), ALU.mult))
                else:
                    so_far()
                    V.scalar_tensor_tensor(out=idx[:, bass.ds(r * TOPK, TOPK)], in0=picked[:, 0],
                                           scalar=float(KEYS), in1=picked[:, 1], op0=ALU.mult, op1=ALU.add).then_inc(sem("routed"), 1)

            need(dve, "scores", 2)
            for r in range(AHEAD):
                for step in range(TOPK):
                    route(step, r)
                if r == 0:
                    p = FIRST_PAIR["pq0"]
                    pair_ready(dve, p)
                    pair_used_wait(dve, V.tensor_tensor(pq[:, 0:2, P:], first[:, :, P:], rinv[:, :, P:].broadcast_to([P, 2, P]), ALU.mult), p)
                    signal(dve, "pq", 1)
                for i in (range(2, 4) if r else range(1, 2)):
                    rooted(FIRST_PAIR["pq0"] + i, pq[:, 2 * i:2 * i + 2, :])
                    signal(dve, "pq", 1)
            for k in range(KB):
                last = post(V.tensor_tensor(xn[:, k], xn[:, k], rinv[:, 0], ALU.mult), "xn")
            need(dve, "xn", last)
            need(dve, "mod_sum", MOD_CHUNKS)
            go(V.tensor_tensor(modc[:], ps[:, 7, 0:48], col("b_mod", 0, 48), ALU.add), "mod_read")
            for layer in range(2):
                go(V.scalar_tensor_tensor(out=gmod[:, layer], in0=modc[:, 24 * layer + 8:24 * layer + 16], scalar=1.0,
                                          in1=col(f"norm_g{layer}", 0, KB), op0=ALU.add, op1=ALU.mult))
            go(V.tensor_tensor(gain2[:], col("norm_final", 0, KB), col("norm_final", 0, KB), ALU.mult), "gain2")
            go(V.tensor_tensor(gain_both[:], col("norm_final", 0, KB), gmod[:, 0], ALU.mult))
            need(dve, "scores", len(SCORE_TILES))
            need(dve, "x_tok", 4)

            for t in range(TT):
                x_tok = ps[:, 4 + 2 * t:6 + 2 * t, :].rearrange("p a b -> p (a b)")
                for first, last in HEAD_LOOPS[t]:
                    with dve.Fori(first, last) as h:
                        n = t * PH + h

                        def diagonal(j):
                            dve.wait_ge(sem("gelu"), n * TOPK + j + 1)
                            V.tensor_scalar(diag[:, j], ident, gel16[:, j:j + 1], gate_now[:, j:j + 1],
                                            ALU.mult, ALU.mult).then_inc(sem("diag"), 1)

                        V.tensor_copy(gate_now, gate[:, bass.ds(n * TOPK, TOPK)]).then_inc(sem("gate_now"), 1)
                        for j in range(TOPK):
                            b = j % RING
                            dve.wait_ge(sem(f"row_in{b}"), 16 * (n * 2 + j // RING + 1))
                            V.tensor_tensor_reduce(out=ring[b][:, 0:D], in0=ring[b][:, 0:D], in1=x_tok, scale=1.0, scalar=0.0,
                                                   op0=ALU.mult, op1=ALU.add, accum_out=act16[:, j:j + 1]).then_inc(sem("dots"), 1)
                            if t * PH + first + AHEAD < HEADS:
                                route(j, n + AHEAD)
                            if j == 1:
                                dve.wait_ge(sem("gate_now"), n + 1)
                            if j:
                                diagonal(j - 1)
                        diagonal(TOPK - 1)
                        dve.wait_ge(sem("diag"), (n + 1) * TOPK)
                        dve.sem_inc(sem("head_turn"), 1)
                for i in range(2):
                    need(dve, "y_back", 2 * t + i + 1)
                    src = ps[:, 4 + 2 * t + i, :].rearrange("p (k t) -> p k t", k=4)
                    h = hA[:, 4 * i:4 * i + 4, t * P:(t + 1) * P]
                    go(V.tensor_tensor(h, src, h, ALU.add), "h2y")
            inverse_root(5)
            go(V.tensor_tensor(sq[:, 0], rinv[:, 0], rinv[:, 0], ALU.mult))
            go(V.tensor_tensor(rms[:, 0], sq[:, 0], ps[:, 4, S:2 * S], ALU.mult), "h3_mean")
            go(V.tensor_copy(sq[:, 1], rinv[:, 0]))
            inverse_root(6)
            go(V.tensor_tensor(sq[:, 0], sq[:, 1], rinv[:, 0], ALU.mult))
            norm_mod(hA, gain_both, sq[:, 0])
            for k in range(KB):
                last = post(V.scalar_tensor_tensor(out=hB[:, k], in0=hA[:, k], scalar=col("norm_final", k), in1=sq[:, 1],
                                                   op0=ALU.mult, op1=ALU.mult), "h3")
            need(dve, "h3", last)

            def glu(k):
                p = FIRST_PAIR["cv_ab0"] + k
                need(dve, "sig_b", k + 1)
                pair_used_wait(dve, V.tensor_tensor(ypad[:, k, 15:15 + S], pair_ps(p)[:, 0:S], sgb[:, k % 2], ALU.mult), p)
                signal(dve, "glu", 1)

            def conv_taps(b, first=0, end=CV_TAPS):
                last = counts.get("tap", 0)
                for tap in range(first, end):
                    w = col("cv_dw", 8 * tap + b)
                    x = ypad[:, b, tap:tap + S]
                    acc = odd_taps if tap % 2 else yc[:, b]
                    if tap == 0:
                        last = post(V.tensor_scalar(acc, x, w, col("cv_db", b), ALU.mult, ALU.add), "tap")
                    elif tap == 1:
                        last = post(V.tensor_scalar(acc, x, w, None, ALU.mult), "tap")
                    else:
                        need(dve, "tap", last - 1)
                        last = post(V.scalar_tensor_tensor(out=acc, in0=x, scalar=w, in1=acc, op0=ALU.mult, op1=ALU.add), "tap")
                if end == CV_TAPS:
                    need(dve, "tap", last)
                    go(V.tensor_tensor(yc[:, b], yc[:, b], odd_taps, ALU.add), "conv_dve")

            go(V.memset(ypad[:, :, 0:15], 0.0))
            go(V.memset(ypad[:, :, 15 + S:], 0.0), "ypads")
            glu(0)
            conv_taps(0, 0, 16)
            glu(1)
            conv_taps(0, 16)
            glu(2)
            conv_taps(2)
            glu(3)
            conv_taps(3, 0, 20)
            glu(4)
            glu(5)
            conv_taps(3, 20)
            conv_taps(4, 0, 14)
            glu(6)
            conv_taps(4, 14)
            glu(7)
            conv_taps(6)
            conv_taps(7)
            need(dve, "mean_sb")
            for i in range(4):
                yi = yc[:, 2 * i:2 * i + 2]
                last = post(V.tensor_tensor(yi, yi, rms[:].broadcast_to([P, 2, S]), ALU.subtract), "centred")
            need(dve, "centred", last)
            need(dve, "root", 7)
            go(V.reciprocal(rinv[:, 0], rms[:, 0]), "rinv")
            for k in range(KB):
                post(V.tensor_tensor(ycn[:, k], yc[:, k], rinv[:, 0], ALU.mult), "standard")
            need(dve, "gT", 4)
            for k in range(KB):
                need(dve, "ln_silu", k + 1)
                post(V.tensor_tensor(ycn[:, k], ycn[:, k], gT[:, k], ALU.mult), "cv_y")

            def gated_residual(unit0, src, dst, layer, name):
                for i in range(4):
                    p = FIRST_PAIR[unit0] + i
                    pair_ready(dve, p)
                    for j in range(2):
                        k = 2 * i + j
                        ins = V.scalar_tensor_tensor(out=dst[:, k], in0=pair_ps(p)[:, j * S:(j + 1) * S],
                                                     scalar=modc[:, 24 * layer + 16 + k:24 * layer + 17 + k], in1=src[:, k],
                                                     op0=ALU.mult, op1=ALU.add)
                        if j == 0:
                            go(ins)
                        else:
                            pair_used_wait(dve, ins, p)
                    signal(dve, name, 2)

            gated_residual("cv_out0", hB, hA, 0, "h4")
            go(V.memset(vpad[:, :, 0:8], 0.0))
            go(V.memset(vpad[:, :, 8 + S:], 0.0), "vpads")
            inverse_root(8)
            norm_mod(hA, gmod[:, 1], rinv[:, 0])
            for g in range(4):
                w = 2 << g
                need(dve, "vpad", g + 1)
                src, n = vpad[:, 2 * g:2 * g + 2, :], 272
                for i in range(g + 1):
                    step = 1 << i
                    n -= step
                    go(V.tensor_tensor(win[i][:, :, 0:n], src[:, :, 0:n], src[:, :, step:step + n], ALU.add))
                    src = win[i]
                first = 8 - w // 2
                inv = cst("count_inv")[:, g * S:(g + 1) * S].unsqueeze(1).broadcast_to([P, 2, S])
                o = pooled[:, 2 * g:2 * g + 2, :]
                go(V.tensor_tensor(o, src[:, :, first:first + S], inv, ALU.mult))
                go(V.tensor_tensor(o, o, vpad[:, 2 * g:2 * g + 2, 8:8 + S], ALU.subtract), "pooled")
            for g in range(4):
                p = FIRST_PAIR["grp"] + g
                need(dve, "gT", 4 + 4)
                pair_ready(dve, p)
                for j in range(2):
                    k = 2 * g + j
                    ins = V.scalar_tensor_tensor(out=ycn[:, k], in0=pair_ps(p)[:, j * S:(j + 1) * S], scalar=col("pl_scale", k),
                                                 in1=gT[:, k], op0=ALU.mult, op1=ALU.mult)
                    if j == 0:
                        go(ins)
                    else:
                        pair_used_wait(dve, ins, p)
                signal(dve, "pl_y", 2)
            gated_residual("pl_out0", hA, hB, 1, "result")


def kernel(**inputs):
    import numpy as np
    import concourse.bacc as bacc
    from concourse.bass_utils import run_bass_kernel_spmd

    a = {n: np.asarray(v) for n, v in inputs.items()}
    f4 = np.float32

    def colmajor(v):
        return np.ascontiguousarray(v.reshape(-1, P).T)

    def to_blocks(x):
        return np.ascontiguousarray(x.T.reshape(-1, P, x.shape[0]).transpose(1, 0, 2))

    def unit(w, c=None):
        return w.reshape(KB, P, 512).transpose(1, 0, 2).reshape(P, KB * 512)

    w_in = a["w_in"][0]
    g = {n: w_in[:, 512 * i:512 * (i + 1)] for i, n in enumerate(("b", "c", "h", "q", "k", "v", "z"))}
    kv, cv, pv = a["w_xkv"][0], a["cv_w_in_2"][0], a["pl_w_in_2"][0]
    for i in range(2):
        s = slice(512 * i, 512 * (i + 1))
        g[f"mem_k{i}"], g[f"mem_v{i}"] = kv[:, s], kv[:, 1024 + 512 * i:1536 + 512 * i]
        g[f"mix_out{i}"], g[f"xq{i}"], g[f"xo{i}"], g[f"pq{i}"] = (a[n][0][:, s] for n in ("w_out", "w_xq", "w_xo", "w_pq"))
        g[f"cv_g{i}"], g[f"cv_out{i}"], g[f"pl_out{i}"] = cv[:, 2048 + 512 * i:2560 + 512 * i], a["cv_w_out_2"][0][:, s], a["pl_w_out_2"][0][:, s]
        g[f"pl_v{i}"], g[f"pl_g{i}"] = pv[:, s], pv[:, 1024 + 512 * i:1536 + 512 * i]
    for i in range(4):
        g[f"cv_ab{i}"] = np.concatenate([cv[:, c:c + P] for k in (2 * i, 2 * i + 1) for c in (P * k, 1024 + P * k)], axis=1)
    units = np.stack([unit(g[u]) for u in UNITS if u != "grp"])
    grp = np.ascontiguousarray(a["pl_w_grp_2"][0].reshape(4, 2, P, 256).transpose(2, 0, 1, 3).reshape(P, 2048))
    mod = np.ascontiguousarray(a["w_mod_2"].reshape(2, KB, P, 12, 256).transpose(0, 3, 2, 1, 4).reshape(MOD_CHUNKS, P, KB * 256))

    parts = {"norm_mix": a["norm_mix"], "norm_x": a["norm_x"], "norm_mem": a["norm_mem"], "norm_ffn": a["norm_ffn"],
             "norm_final": a["norm_final"], "norm_g0": a["norm_g_2"][0], "norm_g1": a["norm_g_2"][1],
             "conv_w": a["conv_w"], "dn_conv_w": a["dn_conv_w"], "dn_norm": a["dn_norm"], "cv_dw": a["cv_dw_2"],
             "cv_db": a["cv_db_2"], "ln_g": a["cv_ln_g_2"], "ln_b": a["cv_ln_b_2"], "pl_scale": a["pl_scale_2"],
             "b_mod": a["b_mod_2"], "c": a["c_2"]}
    cols = np.concatenate([colmajor(parts[n]) if n in parts else
                           np.broadcast_to(a["dn_a_log" if n == "a_log" else "dn_dt_bias"][0], (P, NH)) for n in COLS], axis=1)

    i, j = np.indices((P, P))
    same = i // CHUNK == j // CHUNK
    const = np.zeros((P, NCONST), f4)

    def put(name, v):
        const[:, CONST[name][0]:CONST[name][0] + CONST[name][1]] = v

    put("ident", i == j)
    put("ones", 1)
    put("upto", same & (i <= j))
    put("whole", same)
    put("causal", same & (i >= j))
    put("strict16", (i // 16 == j // 16) & (i > j))
    put("off32", (i // 32 == j // 32) & (i // 16 > j // 16))
    put("off64", same & (i // 32 > j // 32))
    t = np.arange(S)
    put("count_inv", np.concatenate([1.0 / (np.clip(t + w - w // 2, 0, S) - np.clip(t - w // 2, 0, S)) for w in (2, 4, 8, 16)]))
    put("iota16", np.arange(16))
    put("eps", EPS)
    put("one", 1)

    arrays = {
        "x_t": to_blocks(a["x"][0]), "mem_t": to_blocks(a["mem"][0]),
        "cols": np.ascontiguousarray(cols), "const": const,
        "small": np.ascontiguousarray(w_in[:, 3584:3592].reshape(KB, P, 8).transpose(1, 0, 2)),
        "keys": np.ascontiguousarray(a["peer_keys"][0].transpose(1, 3, 0, 2).reshape(P, PH, KEYS)),
        "units": units, "grp": grp, "mod": mod,
        "uv": np.concatenate([a["expert_u"][0], a["expert_v"][0]], axis=1),
    }
    nc = bacc.Bacc("TRN2", target_bir_lowering=False, num_devices=1)
    args = [nc.dram_tensor(f"{n}_dram", v.shape, mybir.dt.from_np(v.dtype), kind="ExternalInput").ap() for n, v in arrays.items()]
    out = nc.dram_tensor("out", (P, KB, S), F32, kind="ExternalOutput").ap()
    build(nc, *args, out)
    r = run_bass_kernel_spmd(nc, [{f"{n}_dram": v for n, v in arrays.items()}], core_ids=[0])
    o = r.results[0]["out"]
    return np.ascontiguousarray(o.transpose(2, 1, 0).reshape(1, S, D))
```
